# Optimizing a Trainium2 kernel written in Bass

```python
import math
import jax
import jax.numpy as jnp
from jax import lax
import numpy as np
import jax, jax.numpy as jnp

D_MODEL = 1024
BATCH = 1
SEQ = 512
DEPTH = 2

EPS = 1e-6
NEG_INF = -1e30
FORCED_SCORE = 1e9
NSA_HEADS = 8
NSA_KV_GROUPS = 2
NSA_HEAD_DIM = 64
CMP_BLOCK = 32
CMP_STRIDE = 16
CMP_HIDDEN = 256
SEL_BLOCK = 64
SEL_TOP_N = 16
WINDOW = 512
NSA_Q_BLOCK = 64
MLA_HEADS = 8
MLA_Q_RANK = 256
MLA_KV_RANK = 128
MLA_NOPE_DIM = 64
MLA_ROPE_DIM = 32
MLA_V_DIM = 64
ROPE_THETA = 10000.0
ATTN_Q_BLOCK = 128
REL_BUCKETS = 32
REL_MAX_DIST = 128
CONV_WIDTH = 3
D_FF = 2816
N_EXPERTS = 8
TOP_K = 2
D_FF_EXPERT = 1408
MOE_ROW_BLOCK = 256
NSA_Q_W = NSA_HEADS * NSA_HEAD_DIM
NSA_KV_W = NSA_KV_GROUPS * NSA_HEAD_DIM
NSA_GATE_W = NSA_HEADS * 3
EVEN_IN_SIZES = (NSA_Q_W,) + (NSA_KV_W,) * 6 + (NSA_GATE_W, MLA_Q_RANK, MLA_KV_RANK, MLA_ROPE_DIM)
EVEN_IN_W = sum(EVEN_IN_SIZES)
MIX_OUT_W = NSA_HEADS * NSA_HEAD_DIM + MLA_HEADS * MLA_V_DIM


def rms_norm(x, g):
    xf = x.astype(jnp.float32)
    y = xf * lax.rsqrt(jnp.mean(jnp.square(xf), axis=-1, keepdims=True) + EPS)
    return (y * g.astype(jnp.float32)).astype(x.dtype)

def masked_softmax(s, mask):
    p = jax.nn.softmax(jnp.where(mask, s, NEG_INF), axis=-1)
    return jnp.where(mask, p, 0.0)

def t5_bucket(dist):
    n = jnp.maximum(dist, 0)
    max_exact = REL_BUCKETS // 2
    nf = jnp.maximum(n, max_exact).astype(jnp.float32)
    large = max_exact + (jnp.log(nf / max_exact) / math.log(REL_MAX_DIST / max_exact)
                         * (REL_BUCKETS - max_exact)).astype(jnp.int32)
    return jnp.where(n < max_exact, n, jnp.minimum(large, REL_BUCKETS - 1))

def rope(x, pos):
    half = x.shape[-1] // 2
    inv_freq = ROPE_THETA ** (-jnp.arange(half, dtype=jnp.float32) / half)
    ang = pos.astype(jnp.float32)[:, None] * inv_freq[None, :]
    cos = jnp.cos(ang)[:, None, :]
    sin = jnp.sin(ang)[:, None, :]
    xf = x.astype(jnp.float32)
    x1, x2 = xf[..., :half], xf[..., half:]
    return jnp.concatenate([x1 * cos - x2 * sin, x1 * sin + x2 * cos], axis=-1).astype(x.dtype)

def compress(kv, pos_emb, w1, w2):
    B, S, G, dk = kv.shape
    nc = (S - CMP_BLOCK) // CMP_STRIDE + 1
    idx = jnp.arange(nc)[:, None] * CMP_STRIDE + jnp.arange(CMP_BLOCK)[None, :]
    blk = kv[:, idx] + pos_emb[None, None, :, None, :]
    blk = blk.transpose(0, 1, 3, 2, 4).reshape(B, nc, G, CMP_BLOCK * dk)
    return jax.nn.gelu(blk @ w1) @ w2

def nsa_mixer(q, k_cmp, v_cmp, k_sel, v_sel, k_win, v_win, gates, rel_bias,
              q_norm, k_norm, cmp_pos, cmp_w1, cmp_w2):
    B, S = q.shape[0], q.shape[1]
    G, R, dk = NSA_KV_GROUPS, NSA_HEADS // NSA_KV_GROUPS, NSA_HEAD_DIM
    QB, L = NSA_Q_BLOCK, WINDOW + NSA_Q_BLOCK
    scale = dk ** -0.5
    qn = rms_norm(q, q_norm).reshape(B, S, G, R, dk)
    kc = rms_norm(compress(k_cmp, cmp_pos[0], cmp_w1[0], cmp_w2[0]), k_norm[0])
    vc = compress(v_cmp, cmp_pos[1], cmp_w1[1], cmp_w2[1])
    nc = kc.shape[1]
    ns = S // SEL_BLOCK
    n_top = min(SEL_TOP_N, ns)

    def to_blocks(a):
        return a.reshape(B, ns, SEL_BLOCK, G, dk).transpose(0, 3, 1, 2, 4).reshape(B, G, ns, SEL_BLOCK * dk)

    ks_blk = to_blocks(rms_norm(k_sel, k_norm[1]))
    vs_blk = to_blocks(v_sel)
    pad = ((0, 0), (WINDOW, 0), (0, 0), (0, 0))
    kw_pad = jnp.pad(rms_norm(k_win, k_norm[2]), pad)
    vw_pad = jnp.pad(v_win, pad)
    gate_all = gates.reshape(B, S, G, R, 3)

    cmp_start = jnp.arange(nc) * CMP_STRIDE
    cmp_end = cmp_start + CMP_BLOCK - 1
    sel_start = jnp.arange(ns) * SEL_BLOCK
    overlap = ((cmp_start[:, None] < sel_start[None, :] + SEL_BLOCK)
               & (cmp_end[:, None] >= sel_start[None, :])).astype(jnp.float32)
    bias_gr = rel_bias.reshape(REL_BUCKETS, G, R)
    g_idx = jnp.arange(G)[None, :, None, None, None]
    blk_ids = jnp.arange(ns)
    offs_sel = jnp.arange(SEL_BLOCK)
    flat = n_top * SEL_BLOCK

    def one_block(i):
        q0 = i * QB
        t = q0 + jnp.arange(QB)
        qb = lax.dynamic_slice_in_dim(qn, q0, QB, axis=1)
        d_c = t[:, None] - cmp_end[None, :]
        s_c = jnp.einsum('bqgrd,bcgd->bgrqc', qb, kc).astype(jnp.float32) * scale
        s_c = s_c + bias_gr[t5_bucket(d_c)].transpose(2, 3, 0, 1).astype(jnp.float32)
        p_c = masked_softmax(s_c, d_c >= 0)
        o_c = jnp.einsum('bgrqc,bcgd->bqgrd', p_c.astype(vc.dtype), vc)
        imp = jnp.einsum('bgrqc,cj->bgqj', p_c, overlap)
        forced = (blk_ids[None, :] == (t // SEL_BLOCK)[:, None]) | (blk_ids[None, :] == 0)
        imp = jnp.where(forced, FORCED_SCORE, imp)
        imp = jnp.where(sel_start[None, :] <= t[:, None], imp, -1.0)
        _, sel = lax.top_k(imp, n_top)
        sel_flat = sel.reshape(B, G, QB * n_top, 1)
        k_g = jnp.take_along_axis(ks_blk, sel_flat, axis=2).reshape(B, G, QB, n_top, SEL_BLOCK, dk)
        v_g = jnp.take_along_axis(vs_blk, sel_flat, axis=2).reshape(B, G, QB, flat, dk)
        s_pos = sel[..., None] * SEL_BLOCK + offs_sel
        d_s = t[None, None, :, None, None] - s_pos
        s_s = jnp.einsum('bqgrd,bgqnkd->bgrqnk', qb, k_g).astype(jnp.float32) * scale
        s_s = s_s + jnp.moveaxis(bias_gr[t5_bucket(d_s), g_idx], -1, 2).astype(jnp.float32)
        p_s = masked_softmax(s_s.reshape(B, G, R, QB, flat), (d_s >= 0).reshape(B, G, 1, QB, flat))
        o_s = jnp.einsum('bgrqk,bgqkd->bqgrd', p_s.astype(v_g.dtype), v_g)
        k_w = lax.dynamic_slice_in_dim(kw_pad, q0, L, axis=1)
        v_w = lax.dynamic_slice_in_dim(vw_pad, q0, L, axis=1)
        w_pos = q0 - WINDOW + jnp.arange(L)
        d_w = t[:, None] - w_pos[None, :]
        s_w = jnp.einsum('bqgrd,bkgd->bgrqk', qb, k_w).astype(jnp.float32) * scale
        s_w = s_w + bias_gr[t5_bucket(d_w)].transpose(2, 3, 0, 1).astype(jnp.float32)
        p_w = masked_softmax(s_w, (d_w >= 0) & (d_w < WINDOW) & (w_pos[None, :] >= 0))
        o_w = jnp.einsum('bgrqk,bkgd->bqgrd', p_w.astype(v_w.dtype), v_w)
        g = jax.nn.sigmoid(lax.dynamic_slice_in_dim(gate_all, q0, QB, axis=1).astype(jnp.float32))
        o = g[..., 0:1] * o_c + g[..., 1:2] * o_s + g[..., 2:3] * o_w
        return o.astype(q.dtype)

    out = lax.map(one_block, jnp.arange(S // QB))
    return out.transpose(1, 0, 2, 3, 4, 5).reshape(B, S, NSA_HEADS * dk)

def causal_block_attention(q, k, v):
    B, S, H, dh = q.shape
    scale = dh ** -0.5
    key_pos = jnp.arange(S)

    def one_block(i):
        q0 = i * ATTN_Q_BLOCK
        qb = lax.dynamic_slice_in_dim(q, q0, ATTN_Q_BLOCK, axis=1)
        s = jnp.einsum('bqhd,bkhd->bhqk', qb, k).astype(jnp.float32) * scale
        mask = (q0 + jnp.arange(ATTN_Q_BLOCK))[:, None] >= key_pos[None, :]
        p = masked_softmax(s, mask)
        return jnp.einsum('bhqk,bkhd->bqhd', p.astype(v.dtype), v)

    out = lax.map(one_block, jnp.arange(S // ATTN_Q_BLOCK))
    return out.transpose(1, 0, 2, 3, 4).reshape(B, S, H, v.shape[-1])

def mla_mixer(c_q, c_kv, k_rope, cq_norm, ckv_norm, w_uq, w_ukv, q_norm, k_norm):
    B, S = c_q.shape[0], c_q.shape[1]
    H, dn, dr, dv = MLA_HEADS, MLA_NOPE_DIM, MLA_ROPE_DIM, MLA_V_DIM
    pos = jnp.arange(S)
    q = (rms_norm(c_q, cq_norm) @ w_uq).reshape(B, S, H, dn + dr)
    kv = (rms_norm(c_kv, ckv_norm) @ w_ukv).reshape(B, S, H, dn + dv)
    k = jnp.concatenate([kv[..., :dn], jnp.broadcast_to(k_rope[:, :, None, :], (B, S, H, dr))], axis=-1)
    v = kv[..., dn:]
    q = rms_norm(q, q_norm)
    k = rms_norm(k, k_norm)
    q = jnp.concatenate([q[..., :dn], rope(q[..., dn:], pos)], axis=-1)
    k = jnp.concatenate([k[..., :dn], rope(k[..., dn:], pos)], axis=-1)
    return causal_block_attention(q, k, v).reshape(B, S, H * dv)

def short_conv_mixer(u, b_gate, c_gate, conv_w):
    y = lax.conv_general_dilated(c_gate * u, conv_w[:, None, :], window_strides=(1,),
                                 padding=[(CONV_WIDTH - 1, 0)],
                                 dimension_numbers=('NWC', 'WIO', 'NWC'),
                                 feature_group_count=u.shape[-1])
    return b_gate * y

def swiglu(x, w_gate, w_up, w_down):
    return (jax.nn.silu(x @ w_gate) * (x @ w_up)) @ w_down

def moe_swiglu(x, w_router, b_router, w_gate, w_up, w_down):
    B, S, D = x.shape
    T = B * S
    RB = MOE_ROW_BLOCK
    xt = x.reshape(T, D)
    logits = (xt @ w_router).astype(jnp.float32) + b_router.astype(jnp.float32)
    top_logit, top_e = lax.top_k(logits, TOP_K)
    top_w = jax.nn.softmax(top_logit, axis=-1)
    P = T * TOP_K
    e_flat = top_e.reshape(P)
    tok_flat = jnp.arange(P) // TOP_K
    w_flat = top_w.reshape(P)
    order = jnp.argsort(e_flat)
    e_s, tok_s, w_s = e_flat[order], tok_flat[order], w_flat[order]
    counts = jnp.bincount(e_flat, length=N_EXPERTS)
    padded = (counts + RB - 1) // RB * RB
    start = jnp.cumsum(counts) - counts
    pad_end = jnp.cumsum(padded)
    pad_start = pad_end - padded
    dest = pad_start[e_s] + jnp.arange(P) - start[e_s]
    n_blk = (P + RB - 1) // RB + N_EXPERTS
    n_rows = n_blk * RB
    tok_buf = jnp.zeros((n_rows,), jnp.int32).at[dest].set(tok_s)
    w_buf = jnp.zeros((n_rows,), jnp.float32).at[dest].set(w_s)
    blk_expert = jnp.minimum(jnp.sum(pad_end[None, :] <= (jnp.arange(n_blk) * RB)[:, None], axis=1),
                             N_EXPERTS - 1)

    def one_block(args):
        e, toks, w = args
        xb = xt[toks]
        h = jax.nn.silu(xb @ w_gate[e]) * (xb @ w_up[e])
        return (h @ w_down[e]) * w[:, None].astype(h.dtype)

    out = lax.map(one_block, (blk_expert, tok_buf.reshape(n_blk, RB), w_buf.reshape(n_blk, RB)))
    y = jnp.zeros((T, D), x.dtype).at[tok_buf].add(out.reshape(n_rows, D).astype(x.dtype))
    return y.reshape(B, S, D)

def first_inputs(seed: int = 0) -> dict:
    key = jax.random.key(seed)
    keys = iter(jax.random.split(key, 32))
    ne, no = (DEPTH + 1) // 2, DEPTH // 2

    def dense(shape, fan_in):
        return jax.random.normal(next(keys), shape, jnp.float32) * (fan_in ** -0.5)

    def gain(shape):
        return 1.0 + 0.02 * jax.random.normal(next(keys), shape, jnp.float32)

    def small(shape, scale):
        return scale * jax.random.normal(next(keys), shape, jnp.float32)

    cmp_in = CMP_BLOCK * NSA_HEAD_DIM
    mla_qk = MLA_NOPE_DIM + MLA_ROPE_DIM
    return {
        'x': jax.random.normal(next(keys), (BATCH, SEQ, D_MODEL), jnp.float32),
        'rel_bias': small((REL_BUCKETS, NSA_HEADS), 0.1),
        'ev_mix_norm': gain((ne, D_MODEL)),
        'ev_w_in': dense((ne, D_MODEL, EVEN_IN_W), D_MODEL),
        'nsa_q_norm': gain((ne, NSA_HEAD_DIM)),
        'nsa_k_norm': gain((ne, 3, NSA_HEAD_DIM)),
        'nsa_cmp_pos': small((ne, 2, CMP_BLOCK, NSA_HEAD_DIM), 0.02),
        'nsa_cmp_w1': dense((ne, 2, cmp_in, CMP_HIDDEN), cmp_in),
        'nsa_cmp_w2': dense((ne, 2, CMP_HIDDEN, NSA_HEAD_DIM), CMP_HIDDEN),
        'mla_cq_norm': gain((ne, MLA_Q_RANK)),
        'mla_ckv_norm': gain((ne, MLA_KV_RANK)),
        'mla_w_uq': dense((ne, MLA_Q_RANK, MLA_HEADS * mla_qk), MLA_Q_RANK),
        'mla_w_ukv': dense((ne, MLA_KV_RANK, MLA_HEADS * (MLA_NOPE_DIM + MLA_V_DIM)), MLA_KV_RANK),
        'mla_q_norm': gain((ne, mla_qk)),
        'mla_k_norm': gain((ne, mla_qk)),
        'ev_w_out': dense((ne, MIX_OUT_W, D_MODEL), MIX_OUT_W),
        'ev_ffn_norm': gain((ne, D_MODEL)),
        'ffn_w_gate': dense((ne, D_MODEL, D_FF), D_MODEL),
        'ffn_w_up': dense((ne, D_MODEL, D_FF), D_MODEL),
        'ffn_w_down': dense((ne, D_FF, D_MODEL), D_FF),
        'od_mix_norm': gain((no, D_MODEL)),
        'od_w_in': dense((no, D_MODEL, 3 * D_MODEL), D_MODEL),
        'conv_w': dense((no, CONV_WIDTH, D_MODEL), CONV_WIDTH),
        'od_w_out': dense((no, D_MODEL, D_MODEL), D_MODEL),
        'od_ffn_norm': gain((no, D_MODEL)),
        'moe_w_router': dense((no, D_MODEL, N_EXPERTS), D_MODEL),
        'moe_b_router': small((no, N_EXPERTS), 0.01),
        'moe_w_gate': dense((no, N_EXPERTS, D_MODEL, D_FF_EXPERT), D_MODEL),
        'moe_w_up': dense((no, N_EXPERTS, D_MODEL, D_FF_EXPERT), D_MODEL),
        'moe_w_down': dense((no, N_EXPERTS, D_FF_EXPERT, D_MODEL), D_FF_EXPERT),
    }

def first_block(x, rel_bias, ev_mix_norm, ev_w_in, nsa_q_norm, nsa_k_norm, nsa_cmp_pos, nsa_cmp_w1,
              nsa_cmp_w2, mla_cq_norm, mla_ckv_norm, mla_w_uq, mla_w_ukv, mla_q_norm, mla_k_norm,
              ev_w_out, ev_ffn_norm, ffn_w_gate, ffn_w_up, ffn_w_down, od_mix_norm, od_w_in, conv_w,
              od_w_out, od_ffn_norm, moe_w_router, moe_b_router, moe_w_gate, moe_w_up, moe_w_down):
    B, S, _ = x.shape
    split_at = np.cumsum(EVEN_IN_SIZES)[:-1].tolist()
    kv_shape = (B, S, NSA_KV_GROUPS, NSA_HEAD_DIM)
    for layer in range(DEPTH):
        i = layer // 2
        if layer % 2 == 0:
            h = rms_norm(x, ev_mix_norm[i]) @ ev_w_in[i]
            (q, k_c, v_c, k_s, v_s, k_w, v_w, gates, c_q, c_kv, k_rope) = jnp.split(h, split_at, axis=-1)
            o_nsa = nsa_mixer(q.reshape(B, S, NSA_HEADS, NSA_HEAD_DIM),
                              k_c.reshape(kv_shape), v_c.reshape(kv_shape),
                              k_s.reshape(kv_shape), v_s.reshape(kv_shape),
                              k_w.reshape(kv_shape), v_w.reshape(kv_shape),
                              gates, rel_bias, nsa_q_norm[i], nsa_k_norm[i],
                              nsa_cmp_pos[i], nsa_cmp_w1[i], nsa_cmp_w2[i])
            o_mla = mla_mixer(c_q, c_kv, k_rope, mla_cq_norm[i], mla_ckv_norm[i],
                              mla_w_uq[i], mla_w_ukv[i], mla_q_norm[i], mla_k_norm[i])
            x = x + jnp.concatenate([o_nsa, o_mla], axis=-1) @ ev_w_out[i]
            x = x + swiglu(rms_norm(x, ev_ffn_norm[i]), ffn_w_gate[i], ffn_w_up[i], ffn_w_down[i])
        else:
            b_g, c_g, u = jnp.split(rms_norm(x, od_mix_norm[i]) @ od_w_in[i], 3, axis=-1)
            x = x + short_conv_mixer(u, b_g, c_g, conv_w[i]) @ od_w_out[i]
            x = x + moe_swiglu(rms_norm(x, od_ffn_norm[i]), moe_w_router[i], moe_b_router[i],
                               moe_w_gate[i], moe_w_up[i], moe_w_down[i])
    return x


DEPTH_2 = 1

CHUNK = 64
D_MIX = D_MODEL
LRU_WIDTH = D_MIX // 4
LRU_HEADS = 4
LRU_HEAD_DIM = LRU_WIDTH // LRU_HEADS
CONV_WIDTH_2 = 4
LRU_C = 8.0
FOX_WIDTH = D_MIX // 2
FOX_HEAD_DIM = 64
FOX_HEADS = FOX_WIDTH // FOX_HEAD_DIM
Q_BLOCK = 128
RWKV_WIDTH = D_MIX - LRU_WIDTH - FOX_WIDTH
RWKV_HEAD_DIM = 64
RWKV_HEADS = RWKV_WIDTH // RWKV_HEAD_DIM
DECAY_RANK = 32
AAA_RANK = 32
GATE_RANK = 64
N_GROUPS = 4
EXPERTS_PER_GROUP = 4
N_EXPERTS_2 = N_GROUPS * EXPERTS_PER_GROUP
D_EXPERT = 256
NORM_EPS = 1e-6
GN_EPS = 64e-5
LRU_COLS = 2 * LRU_WIDTH
FOX_COLS = 3 * FOX_WIDTH + FOX_HEADS
RWKV_COLS = 3 * RWKV_WIDTH + DECAY_RANK + AAA_RANK + GATE_RANK
D_IN = LRU_COLS + FOX_COLS + RWKV_COLS


def rms_norm_2(x, g, eps=NORM_EPS):
    xf = x.astype(jnp.float32)
    y = xf * lax.rsqrt(jnp.mean(xf * xf, axis=-1, keepdims=True) + eps)
    return (y * g.astype(jnp.float32)).astype(x.dtype)

def rglru_group(x_in, gate_in, conv_w, conv_b, wa, ba, wx, bx, lam, norm_g):
    f32 = jnp.float32
    B, S, W = x_in.shape
    xp = jnp.pad(x_in, ((0, 0), (CONV_WIDTH_2 - 1, 0), (0, 0)))
    xc = conv_b + sum(xp[:, j:j + S] * conv_w[j] for j in range(CONV_WIDTH_2))
    xh = xc.reshape(B, S, LRU_HEADS, LRU_HEAD_DIM)
    r = jax.nn.sigmoid((jnp.einsum('bshi,hij->bshj', xh, wa).reshape(B, S, W) + ba).astype(f32))
    i = jax.nn.sigmoid((jnp.einsum('bshi,hij->bshj', xh, wx).reshape(B, S, W) + bx).astype(f32))
    log_a = -LRU_C * r * jax.nn.softplus(-lam.astype(f32))
    a = jnp.exp(log_a)
    b = jnp.sqrt(-jnp.expm1(2.0 * log_a)) * (i * xc.astype(f32))

    def combine(left, right):
        a1, b1 = left
        a2, b2 = right
        return a1 * a2, a2 * b1 + b2

    _, h = lax.associative_scan(combine, (a, b), axis=1)
    y = jax.nn.gelu(gate_in.astype(f32)) * h
    return rms_norm_2(y.astype(x_in.dtype), norm_g)

def fox_group(q, k, v, f_logit, fb, qn_g, kn_g, norm_g):
    f32 = jnp.float32
    B, S, _ = q.shape
    H, Dh = FOX_HEADS, FOX_HEAD_DIM
    qh = rms_norm_2(q.reshape(B, S, H, Dh), qn_g).transpose(0, 2, 1, 3)
    kh = rms_norm_2(k.reshape(B, S, H, Dh), kn_g).transpose(0, 2, 1, 3)
    vh = v.reshape(B, S, H, Dh).transpose(0, 2, 1, 3)
    log_f = jax.nn.log_sigmoid((f_logit + fb).astype(f32))
    c = jnp.cumsum(log_f, axis=1).transpose(0, 2, 1)
    nb = S // Q_BLOCK
    q_blocks = qh.reshape(B, H, nb, Q_BLOCK, Dh).transpose(2, 0, 1, 3, 4)
    c_blocks = c.reshape(B, H, nb, Q_BLOCK).transpose(2, 0, 1, 3)
    starts = jnp.arange(nb, dtype=jnp.int32) * Q_BLOCK
    k_pos = jnp.arange(S, dtype=jnp.int32)
    scale = FOX_HEAD_DIM ** -0.5

    def block(args):
        qb, cb, s0 = args
        s = jnp.einsum('bhqd,bhkd->bhqk', qb, kh).astype(f32) * scale
        s = s + cb[..., None] - c[:, :, None, :]
        q_pos = s0 + jnp.arange(Q_BLOCK, dtype=jnp.int32)
        mask = k_pos[None, :] <= q_pos[:, None]
        p = jax.nn.softmax(jnp.where(mask, s, -jnp.inf), axis=-1)
        return jnp.einsum('bhqk,bhkd->bhqd', p.astype(vh.dtype), vh)

    o = lax.map(block, (q_blocks, c_blocks, starts))
    o = o.transpose(1, 0, 3, 2, 4).reshape(B, S, FOX_WIDTH)
    return rms_norm_2(o.astype(q.dtype), norm_g)

def rwkv7_group(p, mu, w0, w2, a0, a2, g2, k_k, k_a, r_k, ln_g, ln_b):
    f32 = jnp.float32
    B, S, _ = p.shape
    H, N = RWKV_HEADS, RWKV_HEAD_DIM
    prev = jnp.pad(p, ((0, 0), (1, 0), (0, 0)))[:, :-1]
    p = p + (prev - p) * mu
    o1 = RWKV_WIDTH
    o2 = 2 * RWKV_WIDTH
    o3 = 3 * RWKV_WIDTH
    o4 = o3 + DECAY_RANK
    o5 = o4 + AAA_RANK
    r, k, v, wd, ad, gd = jnp.split(p, [o1, o2, o3, o4, o5], axis=-1)
    r = r.astype(f32)
    k = k.astype(f32)
    v = v.astype(f32)
    w = -jax.nn.softplus(-(w0 + jnp.tanh(wd) @ w2).astype(f32)) - 0.5
    decay = jnp.exp(-jnp.exp(w))
    a = jax.nn.sigmoid((a0 + ad @ a2).astype(f32))
    g = (jax.nn.sigmoid(gd) @ g2).astype(f32)

    def heads(t):
        return t.reshape(B, S, H, N)

    kk = heads(k * k_k)
    kk = kk / jnp.maximum(jnp.sqrt(jnp.sum(kk * kk, axis=-1, keepdims=True)), 1e-12)
    k = k * (1.0 + (a - 1.0) * k_a)
    rh, wh, kh, vh, ah = heads(r), heads(decay), heads(k), heads(v), heads(a)
    n_chunks = S // CHUNK

    def to_chunks(t):
        return t.transpose(1, 0, 2, 3).reshape(n_chunks, CHUNK, B, H, N)

    xs = (to_chunks(rh), to_chunks(wh), to_chunks(kh), to_chunks(vh), to_chunks(kk), to_chunks(kk * ah))

    def frame_step(state, inp):
        r_t, w_t, k_t, v_t, kk_t, b_t = inp
        sa = jnp.einsum('bhvk,bhk->bhv', state, -kk_t)
        state = (state * w_t[:, :, None, :] + sa[..., None] * b_t[:, :, None, :]
                 + v_t[..., None] * k_t[:, :, None, :])
        return state, jnp.einsum('bhvk,bhk->bhv', state, r_t)

    def chunk_step(state, chunk):
        return lax.scan(frame_step, state, chunk)

    state0 = jnp.zeros((B, H, N, N), f32)
    _, o = lax.scan(chunk_step, state0, xs)
    o = o.reshape(S, B, H, N).transpose(1, 0, 2, 3)
    mean = jnp.mean(o, axis=-1, keepdims=True)
    var = jnp.mean(jnp.square(o - mean), axis=-1, keepdims=True)
    o = ((o - mean) * lax.rsqrt(var + GN_EPS)).reshape(B, S, RWKV_WIDTH) * ln_g + ln_b
    bonus = jnp.sum(rh * kh * r_k, axis=-1, keepdims=True) * vh
    return (o + bonus.reshape(B, S, RWKV_WIDTH)) * g

def hier_moe(x, wg, bg, we, be, w_gate, w_up, w_down):
    f32 = jnp.float32
    B, S, D = x.shape
    t = x.reshape(B * S, D)
    g_probs = jax.nn.softmax((t @ wg).astype(f32) + bg, axis=-1)
    g_p, g_idx = lax.top_k(g_probs, 1)
    e_logits = ((t @ we).astype(f32) + be).reshape(-1, N_GROUPS, EXPERTS_PER_GROUP)
    sel = jax.nn.one_hot(g_idx[:, 0], N_GROUPS, dtype=f32)
    e_logits = jnp.einsum('tg,tge->te', sel, e_logits)
    e_p, e_idx = lax.top_k(jax.nn.softmax(e_logits, axis=-1), TOP_K)
    e_p = e_p / jnp.sum(e_p, axis=-1, keepdims=True)
    weights = g_p * e_p
    ids = g_idx * EXPERTS_PER_GROUP + e_idx
    combine = jnp.sum(jax.nn.one_hot(ids, N_EXPERTS_2, dtype=f32) * weights[..., None], axis=1)
    hid = jax.nn.silu(jnp.einsum('td,edf->tef', t, w_gate)) * jnp.einsum('td,edf->tef', t, w_up)
    hid = hid * combine[..., None].astype(hid.dtype)
    y = jnp.einsum('tef,efd->td', hid, w_down)
    return y.reshape(B, S, D).astype(x.dtype)

def second_inputs(seed: int = 0) -> dict:
    key = jax.random.key(seed)
    ks = iter(jax.random.split(key, 40))
    L = DEPTH_2

    def nrm(shape, scale):
        return jax.random.normal(next(ks), shape, jnp.float32) * scale

    def uni(shape, lo, hi):
        return jax.random.uniform(next(ks), shape, jnp.float32, lo, hi)

    x = nrm((BATCH, SEQ, D_MODEL), 1.0)
    norm1_g = 1.0 + nrm((L, D_MODEL), 0.02)
    w_in = nrm((L, D_MODEL, D_IN), D_MODEL ** -0.5)
    conv_w = nrm((L, CONV_WIDTH_2, LRU_WIDTH), CONV_WIDTH_2 ** -0.5)
    conv_b = nrm((L, LRU_WIDTH), 0.01)
    lru_wa = nrm((L, LRU_HEADS, LRU_HEAD_DIM, LRU_HEAD_DIM), LRU_HEAD_DIM ** -0.5)
    lru_ba = nrm((L, LRU_WIDTH), 0.01)
    lru_wx = nrm((L, LRU_HEADS, LRU_HEAD_DIM, LRU_HEAD_DIM), LRU_HEAD_DIM ** -0.5)
    lru_bx = nrm((L, LRU_WIDTH), 0.01)
    a_pow = uni((L, LRU_WIDTH), 0.9, 0.999)
    s = a_pow ** (1.0 / LRU_C)
    lru_lambda = jnp.log(s) - jnp.log1p(-s)
    lru_norm_g = 1.0 + nrm((L, LRU_WIDTH), 0.02)
    fox_fb = uni((L, FOX_HEADS), 1.0, 5.0)
    fox_qnorm_g = 1.0 + nrm((L, FOX_HEAD_DIM), 0.02)
    fox_knorm_g = 1.0 + nrm((L, FOX_HEAD_DIM), 0.02)
    fox_norm_g = 1.0 + nrm((L, FOX_WIDTH), 0.02)
    rwkv_mu = uni((L, RWKV_COLS), 0.0, 1.0)
    rwkv_w0 = uni((L, RWKV_WIDTH), -4.0, 0.0)
    rwkv_w2 = nrm((L, DECAY_RANK, RWKV_WIDTH), 0.1 * DECAY_RANK ** -0.5)
    rwkv_a0 = nrm((L, RWKV_WIDTH), 0.1)
    rwkv_a2 = nrm((L, AAA_RANK, RWKV_WIDTH), 0.5 * AAA_RANK ** -0.5)
    rwkv_g2 = nrm((L, GATE_RANK, RWKV_WIDTH), GATE_RANK ** -0.5)
    rwkv_kk = 0.85 + nrm((L, RWKV_WIDTH), 0.05)
    rwkv_ka = 1.0 + nrm((L, RWKV_WIDTH), 0.05)
    rwkv_rk = nrm((L, RWKV_HEADS, RWKV_HEAD_DIM), 0.1)
    rwkv_ln_g = 1.0 + nrm((L, RWKV_WIDTH), 0.02)
    rwkv_ln_b = nrm((L, RWKV_WIDTH), 0.01)
    w_out = nrm((L, D_MIX, D_MODEL), D_MIX ** -0.5)
    norm2_g = 1.0 + nrm((L, D_MODEL), 0.02)
    router_gw = nrm((L, D_MODEL, N_GROUPS), D_MODEL ** -0.5)
    router_gb = nrm((L, N_GROUPS), 0.01)
    router_ew = nrm((L, D_MODEL, N_EXPERTS_2), D_MODEL ** -0.5)
    router_eb = nrm((L, N_EXPERTS_2), 0.01)
    exp_w_gate = nrm((L, N_EXPERTS_2, D_MODEL, D_EXPERT), D_MODEL ** -0.5)
    exp_w_up = nrm((L, N_EXPERTS_2, D_MODEL, D_EXPERT), D_MODEL ** -0.5)
    exp_w_down = nrm((L, N_EXPERTS_2, D_EXPERT, D_MODEL), D_EXPERT ** -0.5)
    return {'x': x, 'norm1_g': norm1_g, 'w_in': w_in, 'conv_w': conv_w, 'conv_b': conv_b,
            'lru_wa': lru_wa, 'lru_ba': lru_ba, 'lru_wx': lru_wx, 'lru_bx': lru_bx,
            'lru_lambda': lru_lambda, 'lru_norm_g': lru_norm_g, 'fox_fb': fox_fb,
            'fox_qnorm_g': fox_qnorm_g, 'fox_knorm_g': fox_knorm_g, 'fox_norm_g': fox_norm_g,
            'rwkv_mu': rwkv_mu, 'rwkv_w0': rwkv_w0, 'rwkv_w2': rwkv_w2, 'rwkv_a0': rwkv_a0,
            'rwkv_a2': rwkv_a2, 'rwkv_g2': rwkv_g2, 'rwkv_kk': rwkv_kk, 'rwkv_ka': rwkv_ka,
            'rwkv_rk': rwkv_rk, 'rwkv_ln_g': rwkv_ln_g, 'rwkv_ln_b': rwkv_ln_b, 'w_out': w_out,
            'norm2_g': norm2_g, 'router_gw': router_gw, 'router_gb': router_gb,
            'router_ew': router_ew, 'router_eb': router_eb, 'exp_w_gate': exp_w_gate,
            'exp_w_up': exp_w_up, 'exp_w_down': exp_w_down}

def second_block(x, norm1_g, w_in, conv_w, conv_b, lru_wa, lru_ba, lru_wx, lru_bx, lru_lambda,
              lru_norm_g, fox_fb, fox_qnorm_g, fox_knorm_g, fox_norm_g, rwkv_mu, rwkv_w0,
              rwkv_w2, rwkv_a0, rwkv_a2, rwkv_g2, rwkv_kk, rwkv_ka, rwkv_rk, rwkv_ln_g,
              rwkv_ln_b, w_out, norm2_g, router_gw, router_gb, router_ew, router_eb,
              exp_w_gate, exp_w_up, exp_w_down):
    splits = [LRU_WIDTH, LRU_COLS, LRU_COLS + FOX_WIDTH, LRU_COLS + 2 * FOX_WIDTH,
              LRU_COLS + 3 * FOX_WIDTH, LRU_COLS + FOX_COLS]
    for l in range(DEPTH_2):
        h = rms_norm_2(x, norm1_g[l])
        proj = h @ w_in[l]
        xa, ga, q, k, v, fl, pc = jnp.split(proj, splits, axis=-1)
        ya = rglru_group(xa, ga, conv_w[l], conv_b[l], lru_wa[l], lru_ba[l], lru_wx[l],
                         lru_bx[l], lru_lambda[l], lru_norm_g[l])
        yb = fox_group(q, k, v, fl, fox_fb[l], fox_qnorm_g[l], fox_knorm_g[l], fox_norm_g[l])
        yc = rwkv7_group(pc, rwkv_mu[l], rwkv_w0[l], rwkv_w2[l], rwkv_a0[l], rwkv_a2[l],
                         rwkv_g2[l], rwkv_kk[l], rwkv_ka[l], rwkv_rk[l], rwkv_ln_g[l], rwkv_ln_b[l])
        y = jnp.concatenate([ya, yb.astype(x.dtype), yc.astype(x.dtype)], axis=-1)
        x = x + (y @ w_out[l]).astype(x.dtype)
        x = x + hier_moe(rms_norm_2(x, norm2_g[l]), router_gw[l], router_gb[l], router_ew[l],
                         router_eb[l], exp_w_gate[l], exp_w_up[l], exp_w_down[l])
    return x


def setup_inputs(seed=0):
    out = dict(first_inputs(seed))
    for name, value in second_inputs(seed + 1).items():
        if name != "x":
            out[name + "_2"] = value
    return out


def reference(
    x, rel_bias, ev_mix_norm, ev_w_in, nsa_q_norm, nsa_k_norm, nsa_cmp_pos, nsa_cmp_w1,
    nsa_cmp_w2, mla_cq_norm, mla_ckv_norm, mla_w_uq, mla_w_ukv, mla_q_norm, mla_k_norm,
    ev_w_out, ev_ffn_norm, ffn_w_gate, ffn_w_up, ffn_w_down, od_mix_norm, od_w_in, conv_w,
    od_w_out, od_ffn_norm, moe_w_router, moe_b_router, moe_w_gate, moe_w_up, moe_w_down,
    norm1_g_2, w_in_2, conv_w_2, conv_b_2, lru_wa_2, lru_ba_2, lru_wx_2, lru_bx_2, lru_lambda_2,
    lru_norm_g_2, fox_fb_2, fox_qnorm_g_2, fox_knorm_g_2, fox_norm_g_2, rwkv_mu_2, rwkv_w0_2,
    rwkv_w2_2, rwkv_a0_2, rwkv_a2_2, rwkv_g2_2, rwkv_kk_2, rwkv_ka_2, rwkv_rk_2, rwkv_ln_g_2,
    rwkv_ln_b_2, w_out_2, norm2_g_2, router_gw_2, router_gb_2, router_ew_2, router_eb_2,
    exp_w_gate_2, exp_w_up_2, exp_w_down_2,
):
    x = first_block(
        x, rel_bias, ev_mix_norm, ev_w_in, nsa_q_norm, nsa_k_norm, nsa_cmp_pos, nsa_cmp_w1,
        nsa_cmp_w2, mla_cq_norm, mla_ckv_norm, mla_w_uq, mla_w_ukv, mla_q_norm, mla_k_norm,
        ev_w_out, ev_ffn_norm, ffn_w_gate, ffn_w_up, ffn_w_down, od_mix_norm, od_w_in, conv_w,
        od_w_out, od_ffn_norm, moe_w_router, moe_b_router, moe_w_gate, moe_w_up, moe_w_down,
    )
    return second_block(
        x, norm1_g_2, w_in_2, conv_w_2, conv_b_2, lru_wa_2, lru_ba_2, lru_wx_2, lru_bx_2,
        lru_lambda_2, lru_norm_g_2, fox_fb_2, fox_qnorm_g_2, fox_knorm_g_2, fox_norm_g_2,
        rwkv_mu_2, rwkv_w0_2, rwkv_w2_2, rwkv_a0_2, rwkv_a2_2, rwkv_g2_2, rwkv_kk_2, rwkv_ka_2,
        rwkv_rk_2, rwkv_ln_g_2, rwkv_ln_b_2, w_out_2, norm2_g_2, router_gw_2, router_gb_2,
        router_ew_2, router_eb_2, exp_w_gate_2, exp_w_up_2, exp_w_down_2,
    )


_drawn_inputs = setup_inputs


def setup_inputs(seed=0):
    import zlib

    import numpy as np

    out = dict(_drawn_inputs(seed))
    spreads = {}
    factors = {'nsa_q_norm': 6.854,
     'nsa_k_norm': 3.498,
     'mla_cq_norm': 3.376,
     'mla_ckv_norm': 3.224,
     'mla_q_norm': 4.216,
     'mla_k_norm': 4.639,
     'moe_b_router': 2.858,
     'norm1_g_2': 3.114,
     'lru_ba_2': 64.0,
     'lru_bx_2': 22.343,
     'lru_norm_g_2': 15.873,
     'fox_qnorm_g_2': 7.646,
     'fox_knorm_g_2': 7.891,
     'fox_norm_g_2': 14.781,
     'rwkv_w2_2': 8.0,
     'rwkv_a0_2': 5.802,
     'rwkv_kk_2': 145.45,
     'rwkv_ka_2': 6.065,
     'rwkv_ln_g_2': 33.444,
     'rwkv_ln_b_2': 35.089,
     'norm2_g_2': 3.843,
     'router_gb_2': 36.051,
     'router_eb_2': 37.465,
     'conv_b_2': 2.739}
    for name, (base, spread) in spreads.items():
        noise = np.random.default_rng([zlib.crc32(name.encode()), seed]).standard_normal(out[name].shape)
        drawn = base * np.exp(spread * noise) if base else spread * noise
        out[name] = jnp.asarray(drawn.astype(out[name].dtype))
    for name, factor in factors.items():
        out[name] = (out[name] * factor).astype(out[name].dtype)
    return out
```

```python
import math
from contextlib import ExitStack, contextmanager

import numpy as np

import concourse.bass as bass
from concourse import mybir

F32 = mybir.dt.float32
ALU = mybir.AluOpType
ACT = mybir.ActivationFunctionType
AX = mybir.AxisListType

P = 128
SEQ, DM = 512, 1024
NT = SEQ // P
KD = DM // P
EPS = 1e-6
NEG = -1e30


@contextmanager
def stage(nc, name, sems):
    handles = {s: nc.alloc_semaphore(f"{name}_{s}") for s in sems.split()}
    with nc.Block(name=name, no_gpsimd_drain=True) as block:
        yield block, handles
    nc.clear_and_free_semaphores(list(handles.values()))
    nc.all_engine_barrier(sem_only=True)


class Steps:

    def __init__(self, eng, sem):
        self.eng, self.sem, self.n = eng, sem, 0

    def __call__(self, ins):
        self.n += 1
        ins.then_inc(self.sem, 1)
        self.eng.wait_ge(self.sem, self.n)


def bcast(ap, shape):
    return ap.to_broadcast(shape)


def norm_transpose(nc, C, x, gain, xnT, xs, name):
    with ExitStack() as mem, stage(nc, name, "squared mean root rstd scaled turned") as (block, s):
        ss = mem.enter_context(nc.sbuf_tensor(name + "_ss", [P, 4, NT], F32))
        PS = C.PS

        @block.scalar
        def _(act):
            for t in range(NT):
                nc.scalar.activation(xs[:, t], x[:, t], ACT.Square, accum_out=ss[:, 0, t:t + 1]).then_inc(s["squared"], 1)
            act.wait_ge(s["mean"], 1)
            nc.scalar.activation(ss[:, 2], ss[:, 1], ACT.Sqrt).then_inc(s["root"], 1)

        @block.vector
        def _(dve):
            dve.wait_ge(s["squared"], NT)
            nc.vector.tensor_scalar(ss[:, 1], ss[:, 0], 1.0 / DM, EPS, ALU.mult, ALU.add).then_inc(s["mean"], 1)
            dve.wait_ge(s["root"], 1)
            nc.vector.reciprocal(ss[:, 3], ss[:, 2]).then_inc(s["rstd"], 1)
            dve.wait_ge(s["rstd"], 1)
            for t in range(NT):
                nc.vector.tensor_scalar(xs[:, t], x[:, t], ss[:, 3, t:t + 1], None, ALU.mult).then_inc(s["scaled"], 1)
            for t in range(NT):
                dve.wait_ge(s["turned"], t + 1)
                for h in range(2):
                    g = bcast(gain[:, 4 * h:4 * h + 4].unsqueeze(2), [P, 4, P])
                    nc.vector.tensor_tensor(xnT[:, 4 * h:4 * h + 4, t * P:(t + 1) * P],
                                            PS[:, 2 * t + h].rearrange("p (k c) -> p k c", k=4), g, ALU.mult)

        @block.tensor
        def _(pe):
            for t in range(NT):
                pe.wait_ge(s["scaled"], t + 1)
                for k in range(KD):
                    ins = nc.tensor.transpose(PS[:, 2 * t + k // 4, (k % 4) * P:(k % 4 + 1) * P],
                                              xs[:, t].rearrange("p (m k) -> p k m", k=KD)[:, k], C.ident[:, :])
                ins.then_inc(s["turned"], 1)


def products(nc, C, name, jobs, ready=None, chained=False):
    with stage(nc, name, "made taken steps") as (block, s):
        PS = C.PS

        @block.tensor
        def _(pe):
            for n, (pairs, rows, cols, take) in enumerate(jobs):
                if ready is not None:
                    for sem, value in ready(n):
                        pe.wait_ge(sem, value)
                if n >= 8:
                    pe.wait_ge(s["taken"], n - 7)
                for i, (lhsT, rhs) in enumerate(pairs):
                    ins = nc.tensor.matmul(PS[rows, n % 8, cols], lhsT, rhs, start=i == 0, stop=i == len(pairs) - 1)
                ins.then_inc(s["made"], 1)

        @block.vector
        def _(dve):
            steps = Steps(dve, s["steps"])
            for n, (pairs, rows, cols, take) in enumerate(jobs):
                dve.wait_ge(s["made"], n + 1)
                take(PS[rows, n % 8, cols], steps).then_inc(s["taken"], 1)
                if chained:
                    dve.wait_ge(s["taken"], n + 1)


def copy_to(nc, dst):
    return lambda ps, steps: nc.vector.tensor_copy(dst, ps)


def norm_features(nc, C, name, groups, eps=None):
    with ExitStack() as mem, stage(nc, name, "squared summed logged rstd normed") as (block, s):
        sq = mem.enter_context(nc.sbuf_tensor(name + "_sq", [P, 4, SEQ], F32))
        rs = mem.enter_context(nc.sbuf_tensor(name + "_rs", [P, 4, SEQ], F32))
        PS, eps = C.PS, C.eps if eps is None else eps
        first = [0]
        for g in groups:
            first.append(first[-1] + len(g["src"]))

        def part(ap):
            a = ap.start_partition() if callable(ap.start_partition) else ap.start_partition
            return slice(a, a + ap.shape[0]), ap.shape[1]

        @block.scalar
        def _(act):
            def squares(g):
                for i, src in enumerate(groups[g]["src"]):
                    m = first[g] + i
                    rows, n = part(src)
                    if m >= 4:
                        act.wait_ge(s["summed"], m - 3)
                    nc.scalar.activation(sq[rows, m % 4, 0:n], src, ACT.Square).then_inc(s["squared"], 1)

            squares(0)
            for g in range(len(groups)):
                if g + 1 < len(groups):
                    squares(g + 1)
                rows, n = part(groups[g]["src"][0])
                act.wait_ge(s["summed"], first[g + 1])
                if g >= 2:
                    act.wait_ge(s["normed"], first[g - 1])
                nc.scalar.activation(rs[rows, 2 + g % 2, 0:n], PS[rows, g % 2, 0:n], ACT.Ln,
                                     bias=eps[rows, 0:1], scale=1.0 / groups[g]["n"]).then_inc(s["logged"], 1)
                act.wait_ge(s["logged"], g + 1)
                nc.scalar.activation(rs[rows, g % 2, 0:n], rs[rows, 2 + g % 2, 0:n], ACT.Exp,
                                     scale=-0.5).then_inc(s["rstd"], 1)

        @block.tensor
        def _(pe):
            for g, grp in enumerate(groups):
                if g >= 2:
                    pe.wait_ge(s["logged"], g - 1)
                for i, src in enumerate(grp["src"]):
                    m = first[g] + i
                    rows, n = part(src)
                    pe.wait_ge(s["squared"], m + 1)
                    nc.tensor.matmul(PS[rows, g % 2, 0:n], grp["ones"], sq[rows, m % 4, 0:n],
                                     start=i == 0, stop=i == len(grp["src"]) - 1).then_inc(s["summed"], 1)

        @block.vector
        def _(dve):
            for g, grp in enumerate(groups):
                rows, n = part(grp["src"][0])
                dve.wait_ge(s["rstd"], g + 1)
                for src, gain, dst in zip(grp["src"], grp["gain"], grp["dst"]):
                    nc.vector.scalar_tensor_tensor(out=dst, in0=src, scalar=gain, in1=rs[rows, g % 2, 0:n],
                                                   op0=ALU.mult, op1=ALU.mult).then_inc(s["normed"], 1)


def attention(nc, C, name, jobs):
    U = NT * len(jobs)
    with ExitStack() as mem, stage(
            nc, name, "scored biased maxed exped inv coef scaled turned placed valued stored") as (block, s):
        pr = mem.enter_context(nc.sbuf_tensor(name + "_p", [P, 3, SEQ], F32))
        pn = mem.enter_context(nc.sbuf_tensor(name + "_pn", [P, 3, SEQ], F32))
        pT = mem.enter_context(nc.sbuf_tensor(name + "_pT", [P, 2, NT, SEQ], F32))
        st = mem.enter_context(nc.sbuf_tensor(name + "_st", [P, 4, 4], F32))
        PS = C.PS
        stores = [0]
        for job in jobs:
            stores.append(stores[-1] + (1 if job["stop"] else 0))

        @block.tensor
        def _(pe):
            def scores(u):
                job, i = jobs[u // NT], u % NT
                if u >= 2:
                    pe.wait_ge(s["exped"], u - 1)
                q, k = job["q"], job["k"]
                ins = nc.tensor.matmul(PS[:, u % 2, 0:(i + 1) * P], q[:, i * P:(i + 1) * P], k[:, 0:(i + 1) * P],
                                       start=True, stop=job["extra"] is None)
                if job["extra"] is not None:
                    ins = nc.tensor.matmul(PS[:, u % 2, 0:(i + 1) * P], job["extra"][0], job["extra"][1][:, 0:(i + 1) * P],
                                           start=False, stop=True)
                ins.then_inc(s["scored"], 1)

            def turn(u):
                i = u % NT
                pe.wait_ge(s["scaled"], u + 1)
                if u >= 2:
                    pe.wait_ge(s["placed"], u - 1)
                for kb in range(i + 1):
                    ins = nc.tensor.transpose(PS[:, 2 + u % 2, kb * P:(kb + 1) * P], pn[:, u % 3, kb * P:(kb + 1) * P],
                                              C.ident[:, :])
                ins.then_inc(s["turned"], 1)

            def values(j):
                job = jobs[j]
                pe.wait_ge(s["placed"], NT * (j + 1))
                rows, bank = job["rows"], 4 + job["bank"]
                if job["start"] and stores[j] >= 2:
                    pe.wait_ge(s["stored"], stores[j] - 1)
                if job["first"] is not None:
                    nc.tensor.matmul(PS[rows, bank, :], job["first"][0], job["first"][1], start=True, stop=False)
                for kb in range(NT):
                    ins = nc.tensor.matmul(PS[rows, bank, kb * P:SEQ], job["v"](kb), pT[:, j % 2, kb, kb * P:SEQ],
                                           start=kb == 0 and job["start"] and job["first"] is None,
                                           stop=kb == NT - 1 and job["stop"])
                ins.then_inc(s["valued"], 1)

            for u in range(U + 3):
                if u < U:
                    scores(u)
                if 0 <= u - 2 < U:
                    turn(u - 2)
                if u >= 3 and (u - 3) % NT == NT - 1:
                    values((u - 3) // NT)

        @block.scalar
        def _(act):
            def exps(u):
                i = u % NT
                act.wait_ge(s["maxed"], u + 1)
                if u >= 3:
                    act.wait_ge(s["scaled"], u - 2)
                nc.scalar.activation(pr[:, u % 3, 0:(i + 1) * P], PS[:, u % 2, 0:(i + 1) * P], ACT.Exp,
                                     bias=st[:, 0, u % 4:u % 4 + 1], accum_out=st[:, 1, u % 4:u % 4 + 1]).then_inc(s["exped"], 1)

            def scale(u):
                i = u % NT
                act.wait_ge(s["coef"], u + 1)
                if u >= 3:
                    act.wait_ge(s["turned"], u - 2)
                nc.scalar.activation(pn[:, u % 3, 0:(i + 1) * P], pr[:, u % 3, 0:(i + 1) * P], ACT.Copy,
                                     scale=st[:, 3, u % 4:u % 4 + 1]).then_inc(s["scaled"], 1)

            for u in range(U + 1):
                if u < U:
                    exps(u)
                if u >= 1:
                    scale(u - 1)

        @block.vector
        def _(dve):
            def biased(u):
                job, i = jobs[u // NT], u % NT
                w = min(job["bias"].shape[1], (i + 1) * P)
                wb = job["bias"].shape[1]
                dve.wait_ge(s["scored"], u + 1)
                cols = slice((i + 1) * P - w, (i + 1) * P)
                nc.vector.tensor_tensor(PS[:, u % 2, cols], PS[:, u % 2, cols], job["bias"][:, wb - w:wb],
                                        ALU.add).then_inc(s["biased"], 1)
                dve.wait_ge(s["biased"], u + 1)
                if u >= 4:
                    dve.wait_ge(s["exped"], u - 3)
                nc.vector.tensor_reduce(st[:, 0, u % 4:u % 4 + 1], PS[:, u % 2, 0:(i + 1) * P], AX.X, ALU.max,
                                        negate=True).then_inc(s["maxed"], 1)

            def coef(u):
                job, i = jobs[u // NT], u % NT
                dve.wait_ge(s["exped"], u + 1)
                if u >= 4:
                    dve.wait_ge(s["scaled"], u - 3)
                nc.vector.reciprocal(st[:, 2, u % 4:u % 4 + 1], st[:, 1, u % 4:u % 4 + 1]).then_inc(s["inv"], 1)
                dve.wait_ge(s["inv"], u + 1)
                gate = C.one[:, 0:1] if job["gate"] is None else job["gate"](i)
                nc.vector.tensor_tensor(st[:, 3, u % 4:u % 4 + 1], st[:, 2, u % 4:u % 4 + 1], gate,
                                        ALU.mult).then_inc(s["coef"], 1)

            def place(u):
                j, i = u // NT, u % NT
                dve.wait_ge(s["turned"], u + 1)
                if j >= 2:
                    dve.wait_ge(s["valued"], j - 1)
                nc.vector.tensor_copy(pT[:, j % 2, 0:i + 1, i * P:(i + 1) * P],
                                      PS[:, 2 + u % 2, 0:(i + 1) * P].rearrange("p (k c) -> p k c", c=P)).then_inc(s["placed"], 1)

            def store(j):
                job = jobs[j]
                if job["stop"]:
                    dve.wait_ge(s["valued"], j + 1)
                    nc.vector.tensor_copy(job["out"], PS[job["rows"], 4 + job["bank"], :]).then_inc(s["stored"], 1)

            for u in range(U + 4):
                if u < U:
                    biased(u)
                if 0 <= u - 1 < U:
                    coef(u - 1)
                if 0 <= u - 2 < U:
                    place(u - 2)
                if u >= 4 and (u - 4) % NT == NT - 1:
                    store((u - 4) // NT)
            for j in range(len(jobs)):
                if NT * j + NT - 1 + 4 >= U + 4:
                    store(j)


def add_projection(nc, C, name, yT, w, x, loaded):
    def take(t, h):
        def f(ps, steps):
            dst = x[:, t, h * 512:(h + 1) * 512]
            return nc.vector.tensor_tensor(dst, ps, dst, ALU.add)
        return f

    jobs = [([(yT[:, k, t * P:(t + 1) * P], w[:, k, h * 512:(h + 1) * 512]) for k in range(KD)],
             slice(0, P), slice(0, 512), take(t, h)) for t in range(NT) for h in range(2)]
    products(nc, C, name, jobs, lambda n: [loaded] if n == 0 else [])


def gated_parts(nc, C, name, xnT, x, parts, F, wg, wu, wd, weight):
    NF = F // P
    RING = min(5, NF)
    last_user = {}
    for c in range(NF):
        last_user[c % RING] = c
    uses = [len(range(r, NF, RING)) for r in range(RING)]
    sems = "up_free down_loaded made silu hidden y_made y_taken " + " ".join(f"up{r}" for r in range(RING))
    with ExitStack() as mem, stage(nc, name, sems) as (block, s):
        up = mem.enter_context(nc.sbuf_tensor(name + "_up", [P, RING, 2, KD, P], F32))
        down = mem.enter_context(nc.sbuf_tensor(name + "_down", [P, NF, DM], F32))
        sg = mem.enter_context(nc.sbuf_tensor(name + "_sg", [P, 2, SEQ], F32))
        hT = mem.enter_context(nc.sbuf_tensor(name + "_hT", [P, NF, SEQ], F32))
        PS = C.PS

        @block.sync
        def _(sp):
            with sp.Fori(0, parts) as e:
                for c in range(NF):
                    r = c % RING
                    before = c - RING + NF if c >= RING else last_user[r]
                    sp.wait_ge(s["up_free"], e * NF + before + 1)
                    sp.dma_start(up[:, r, 0], wg(e)[:, :, c * P:(c + 1) * P]).then_inc(s[f"up{r}"], 16)
                    sp.dma_start(up[:, r, 1], wu(e)[:, :, c * P:(c + 1) * P]).then_inc(s[f"up{r}"], 16)
                    if c == RING - 1:
                        sp.wait_ge(s["y_made"], e * 8 + 8)
                        sp.dma_start(down[:, :, :], wd(e)).then_inc(s["down_loaded"], 16)

        @block.tensor
        def _(pe):
            pe.sem_inc(s["up_free"], NF)
            pe.sem_inc(s["y_made"], 8)
            with pe.Fori(0, parts) as e:
                for c in range(NF):
                    r = c % RING
                    pe.wait_ge(s[f"up{r}"], (e * uses[r] + c // RING + 1) * 32)
                    pe.wait_ge(s["hidden"], e * NF + c + 1)
                    for m in range(2):
                        for k in range(KD):
                            ins = nc.tensor.matmul(PS[:, 2 * m + c % 2, :], up[:, r, m, k], xnT[:, k], start=k == 0,
                                                   stop=k == KD - 1)
                        ins.then_inc(s["made"] if m == 0 else s["up_free"], 1)
                pe.wait_ge(s["hidden"], e * NF + NF + 2)
                pe.wait_ge(s["down_loaded"], (e + 1) * 16)
                for t in range(NT):
                    for h in range(2):
                        b = 4 + (2 * t + h) % 4
                        pe.wait_ge(s["y_taken"], e * 8 + 2 * t + h + 1)
                        for c in range(NF):
                            ins = nc.tensor.matmul(PS[:, b, :], hT[:, c, t * P:(t + 1) * P],
                                                   down[:, c, h * 512:(h + 1) * 512], start=c == 0, stop=c == NF - 1)
                        ins.then_inc(s["y_made"], 1)

        @block.scalar
        def _(act):
            with act.Fori(0, parts) as e:
                for c in range(NF):
                    act.wait_ge(s["made"], e * NF + c + 1)
                    act.wait_ge(s["hidden"], e * NF + c + 1)
                    nc.scalar.activation(sg[:, c % 2], PS[:, c % 2, :], ACT.Silu).then_inc(s["silu"], 1)

        @block.vector
        def _(dve):
            dve.sem_inc(s["hidden"], 2)
            dve.sem_inc(s["y_taken"], 4)
            with dve.Fori(0, parts) as e:
                for c in range(NF):
                    dve.wait_ge(s["silu"], e * NF + c + 1)
                    dve.wait_ge(s["up_free"], NF + e * NF + c + 1)
                    nc.vector.tensor_tensor(hT[:, c], sg[:, c % 2], PS[:, 2 + c % 2, :], ALU.mult).then_inc(s["hidden"], 1)
                for t in range(NT):
                    for h in range(2):
                        dve.wait_ge(s["y_made"], e * 8 + 2 * t + h + 9)
                        dst = x[:, t, h * 512:(h + 1) * 512]
                        nc.vector.scalar_tensor_tensor(out=dst, in0=PS[:, 4 + (2 * t + h) % 4, :], scalar=weight(t, e),
                                                       in1=dst, op0=ALU.mult, op1=ALU.add).then_inc(s["y_taken"], 1)


class Consts:
    pass


def make_consts(nc, mem):
    C = Consts()
    C.PS = mem.enter_context(nc.psum_tensor("PS", [P, 8, 512], F32))
    C.ident = mem.enter_context(nc.sbuf_tensor("ident", [P, P], F32))
    C.ones = mem.enter_context(nc.sbuf_tensor("ones", [P, P], F32))
    C.ones64 = mem.enter_context(nc.sbuf_tensor("ones64", [P, P], F32))
    C.causal = mem.enter_context(nc.sbuf_tensor("causal", [P, P], F32))
    C.eps = mem.enter_context(nc.sbuf_tensor("eps", [P, 1], F32))
    C.gn_eps = mem.enter_context(nc.sbuf_tensor("gn_eps", [P, 1], F32))
    C.one = mem.enter_context(nc.sbuf_tensor("one", [P, 1], F32))
    with stage(nc, "consts", "zeroed") as (block, s):
        @block.gpsimd
        def _(pool):
            step = Steps(pool, s["zeroed"])
            for tile, value in ((C.ones, 1.0), (C.eps, EPS), (C.gn_eps, 64e-5), (C.one, 1.0), (C.ident, 0.0), (C.causal, 0.0), (C.ones64, 0.0)):
                step(nc.gpsimd.memset(tile[:, :], value))
            for a in (0, 64):
                step(nc.gpsimd.memset(C.ones64[a:a + 64, a:a + 64], 1.0))
            step(nc.gpsimd.affine_select(out=C.ident[:, :], in_=C.ident[:, :], compare_op=ALU.not_equal, fill=1.0,
                                         base=0, pattern=[[-1, P]], channel_multiplier=1))
            step(nc.gpsimd.affine_select(out=C.causal[:, :], in_=C.causal[:, :], compare_op=ALU.is_ge, fill=NEG,
                                         base=0, pattern=[[-1, P]], channel_multiplier=1))
    return C


def column(ap):
    return ap.rearrange("(p o) -> p o", o=1)


Q0, KC0, VC0, KS0, VS0, KW0, VW0, GT0, CQ0, CKV0, KR0, EV_W = (
    0, 512, 640, 768, 896, 1024, 1152, 1280, 1304, 1560, 1688, 1720)
NH, HD = 8, 64
CMP_L, CMP_S = 32, 16
NCMP = (SEQ - CMP_L) // CMP_S + 1
MQK, ROT = 96, 32
BUCKETS = 32
E_ZERO = SEQ + 16


def bucket_table():
    n = np.arange(SEQ)
    large = 16 + (np.log(np.maximum(n, 16).astype(np.float32) / np.float32(16)) / np.float32(math.log(8.0))
                  * np.float32(16)).astype(np.int32)
    b = np.where(n < 16, n, np.minimum(large, BUCKETS - 1))
    table = np.zeros((BUCKETS + 1, E_ZERO + SEQ), np.float32)
    table[b, E_ZERO + n] += 1.0
    table[BUCKETS - 1, E_ZERO:] -= 1.0
    table[BUCKETS, :E_ZERO] = NEG
    return table


def rope_tables():
    half = ROT // 2
    inv = (np.float32(10000.0) ** (-np.arange(half, dtype=np.float32) / np.float32(half))).astype(np.float32)
    ang = np.arange(SEQ, dtype=np.float32)[None, :] * inv[:, None]
    turn = np.zeros((ROT, ROT), np.float32)
    for m in range(half):
        turn[m + half, m] = -1.0
        turn[m, m + half] = 1.0
    return np.stack([np.tile(np.cos(ang), (2, 1)), np.tile(np.sin(ang), (2, 1))]).astype(np.float32), turn


def mixer_even(nc, C, D, x, xnT):
    with ExitStack() as mem:
        def sb(name, shape, m=mem):
            return m.enter_context(nc.sbuf_tensor("ev_" + name, shape, F32))

        yT = sb("yT", [P, 8, SEQ])
        q = sb("q", [P, 4, SEQ])
        ks, kw = sb("ks", [P, SEQ]), sb("kw", [P, SEQ])
        vsw = sb("vsw", [P, NT, 2, P])
        gate = sb("gate", [P, NT, 3 * NH])
        cq, ckv, kr = sb("cq", [P, 2, SEQ]), sb("ckv", [P, SEQ]), sb("kr", [P, SEQ])
        uq, ukv = sb("uq", [P, 2, NH * MQK]), sb("ukv", [P, NH * P])
        vblk = sb("vblk", [P, 2, 4, HD])
        pcT = sb("pcT", [P, 2, SEQ])
        T = sb("T", [P, NH, 2 * P])
        Tc = sb("Tc", [P, NT, NH, 32])
        relb = sb("relb", [BUCKETS + 1, NH])
        gx, gq, gk, gcq, gckv, gmq, gmk = (sb(n, [P, w]) for n, w in (
            ("gx", KD), ("gq", 1), ("gk", 3), ("gcq", 2), ("gckv", 1), ("gmq", 1), ("gmk", 1)))
        loaded = {n: nc.alloc_semaphore("ev_loaded_" + n) for n in "small tables w0 w1 w2 w3 w4 cmp mla rope out".split()}
        pieces = [(Q0, KC0), (KC0, KS0), (KS0, KW0), (KW0, CQ0), (CQ0, EV_W)]
        with ExitStack() as memB:
            kc, vc = sb("kc", [P, SEQ], memB), sb("vc", [P, SEQ], memB)
            X = sb("X", [P, 2, 16, 2, 32], memB)
            w1, w2, pos = sb("w1", [P, 2, 16, 256], memB), sb("w2", [P, 2, 2, P], memB), sb("pos", [P, 2, 16], memB)
            hid, kcT = sb("hid", [P, 2, 2, 64], memB), sb("kcT", [P, 64], memB)
            pair, hid4 = sb("pair", [P, 2, P], memB), sb("hid4", [P, 2, 2, 4, 32], memB)
            E = q[:, :, :].rearrange("p a b -> p (a b)")[0:BUCKETS + 1, 0:E_ZERO + SEQ]
            with ExitStack() as memW:
                W = sb("W", [P, KD, EV_W], memW)
                win = D["ev_w_in"][0].rearrange("(p k) n -> p k n", k=KD)
                small = 0
                with stage(nc, "ev_load", "zeroed") as (block, s):
                    @block.sync
                    def _(sp):
                        nonlocal small
                        sp.dma_start(x[:, :, :], D["x"][0].rearrange("(t p) d -> p t d", p=P)).then_inc(loaded["small"], 16)
                        sp.dma_start(E, D["bucket_table"]).then_inc(loaded["tables"], 16)
                        sp.dma_start(relb[0:BUCKETS, :], D["rel_bias"]).then_inc(loaded["tables"], 16)
                        sp.dma_start(relb[BUCKETS:BUCKETS + 1, :], D["ones_row"]).then_inc(loaded["tables"], 16)
                        smalls = [(gx[:, :], D["ev_mix_norm"][0].rearrange("(p k) -> p k", k=KD)),
                                  (gcq[:, :], D["mla_cq_norm"][0].rearrange("(k p) -> p k", p=P)),
                                  (gckv[:, :], column(D["mla_ckv_norm"][0])),
                                  (gmq[0:MQK, :], column(D["mla_q_norm"][0])),
                                  (gmk[0:MQK, :], column(D["mla_k_norm"][0]))]
                        for a in (0, HD):
                            smalls += [(gq[a:a + HD, :], column(D["nsa_q_norm"][0])),
                                       (gk[a:a + HD, :], D["nsa_k_norm"][0].rearrange("i p -> p i"))]
                        for v in range(2):
                            smalls += [(pos[:, v], D["nsa_cmp_pos"][0, v].rearrange("(j a) d -> (a d) j", a=2))]
                        for dst, src in smalls:
                            sp.dma_start(dst, src, allow_slow_non_contiguous=True).then_inc(loaded["small"], 16)
                        small = 16 * (len(smalls) + 1)
                        for i in range(2):
                            dst = W[:, :, 0:KC0].rearrange("p k (j s d) -> p k j s d", s=2, d=HD)[:, :, :, i]
                            for k in range(KD):
                                sp.dma_start(dst[:, k], win[:, k, i * 256:(i + 1) * 256].rearrange("p (j d) -> p j d", d=HD)) \
                                    .then_inc(loaded["w0"], 16)
                        for i, (a, b) in list(enumerate(pieces))[1:]:
                            sp.dma_start(W[:, :, a:b], win[:, :, a:b]).then_inc(loaded[f"w{i}"], 16)
                        for v in range(2):
                            sp.dma_start(w1[:, v], D["nsa_cmp_w1"][0, v].rearrange("(j p) n -> p j n", p=P)).then_inc(loaded["cmp"], 16)
                            for a in (0, HD):
                                sp.dma_start(w2[:, v, :, a:a + HD], D["nsa_cmp_w2"][0, v].rearrange("(a p) n -> p a n", p=P)).then_inc(loaded["cmp"], 16)
                        sp.dma_start(uq[:, :, :], D["mla_w_uq"][0].rearrange("(k p) n -> p k n", p=P)).then_inc(loaded["mla"], 16)
                        sp.dma_start(ukv[:, :], D["mla_w_ukv"][0]).then_inc(loaded["mla"], 16)

                    @block.gpsimd
                    def _(pool):
                        step = Steps(pool, s["zeroed"])
                        step(nc.gpsimd.memset(Tc[:, :, :, :], NEG))
                        step(nc.gpsimd.memset(X[:, :, :, :, :], 0.0))
                        step(nc.gpsimd.memset(vblk[:, :, :, :], 0.0))

                with stage(nc, "ev_bias", "made") as (block, s):
                    PS = C.PS

                    @block.tensor
                    def _(pe):
                        pe.wait_ge(loaded["tables"], 48)
                        for c in range(2 * P):
                            ins = nc.tensor.matmul(PS[:, c // 64, c % 64 * NH:(c % 64 + 1) * NH],
                                                   E[:, E_ZERO + P - c:E_ZERO + 2 * P - c], relb[:, :], start=True, stop=True)
                            if c % 64 == 63:
                                ins.then_inc(s["made"], 1)
                        for t in range(NT):
                            for c in range(NCMP):
                                a = E_ZERO + P * t - CMP_S * c - (CMP_L - 1)
                                o = t % 2 * 256 + c * NH
                                ins = nc.tensor.matmul(PS[:, 4 + t // 2, o:o + NH], E[:, a:a + P], relb[:, :],
                                                       start=True, stop=True)
                        ins.then_inc(s["made"], 1)

                    @block.vector
                    def _(dve):
                        for b in range(4):
                            dve.wait_ge(s["made"], b + 1)
                            nc.vector.tensor_copy(T[:, :, 64 * b:64 * b + 64],
                                                  PS[:, b, :].rearrange("p (c h) -> p h c", h=NH))
                        dve.wait_ge(s["made"], 5)
                        for t in range(NT):
                            nc.vector.tensor_copy(Tc[:, t, :, 0:NCMP], PS[:, 4 + t // 2, t % 2 * 256:t % 2 * 256 + NCMP * NH]
                                                  .rearrange("p (c h) -> p h c", h=NH))

                with stage(nc, "ev_wait", "scaled") as (block, s):
                    @block.vector
                    def _(dve):
                        dve.wait_ge(loaded["small"], small)
                        nc.vector.tensor_scalar(gq[:, :], gq[:, :], float(HD) ** -0.5, None, ALU.mult)
                        nc.vector.tensor_scalar(gmq[0:MQK, :], gmq[0:MQK, :], float(MQK) ** -0.5, None, ALU.mult)
                        for g in range(2):
                            nc.vector.tensor_copy(pair[:, g].rearrange("p (a d) -> p a d", a=2),
                                                  bcast(C.ident[:, g * HD:(g + 1) * HD].unsqueeze(1), [P, 2, HD]))

                norm_transpose(nc, C, x, gx, xnT, yT[:, :, :].rearrange("p (t a) b -> p t (a b)", a=2), "ev_norm")

                def features(lhsT, M, dst, r0=0):
                    return ([(lhsT(k), xnT[:, k]) for k in range(KD)], slice(r0, r0 + M), slice(0, SEQ), copy_to(nc, dst))

                def cols(a, M):
                    return lambda k: W[:, k, a:a + M]

                def take_vw(t):
                    def f(ps, steps):
                        nc.vector.tensor_copy(vsw[:, t, 1], ps[:, 0:P])
                        return nc.vector.tensor_copy(gate[:, t], ps[:, P:P + 3 * NH])
                    return f

                jobs, need = [], []
                for j in range(4):
                    jobs.append(features(lambda k, j=j: W[:, k, j * P:(j + 1) * P],
                                         P, q[:, j]))
                    need.append([0])
                for a, dst, w in ((KC0, kc, 1), (VC0, vc, 1), (KS0, ks, 2), (KW0, kw, 3)):
                    jobs.append(features(cols(a, P), P, dst[:, :]))
                    need.append([w])
                for t in range(NT):
                    tok = slice(t * P, (t + 1) * P)
                    jobs.append(([(xnT[:, k, tok], W[:, k, VS0:VS0 + P]) for k in range(KD)], slice(0, P), slice(0, P),
                                 copy_to(nc, vsw[:, t, 0])))
                    jobs.append(([(xnT[:, k, tok], W[:, k, VW0:VW0 + P + 3 * NH]) for k in range(KD)], slice(0, P),
                                 slice(0, P + 3 * NH), take_vw(t)))
                    need += [[2], [3]]
                for a, M, dst, r0 in ((CQ0, P, cq[:, 0], 0), (CQ0 + P, P, cq[:, 1], 0), (CKV0, P, ckv[:, :], 0),
                                      (KR0, ROT, kr[64:96, :], 64)):
                    jobs.append(features(cols(a, M), M, dst, r0))
                    need.append([4])
                products(nc, C, "ev_in", jobs, lambda n: [(loaded[f"w{i}"], 16 if i else 32 * KD) for i in need[n]])

            groups = [dict(src=[q[:, j]], gain=[gq[:, 0:1]], dst=[q[:, j]], ones=C.ones64[:, :], n=HD) for j in range(4)]
            groups += [dict(src=[k[:, :]], gain=[gk[:, i:i + 1]], dst=[k[:, :]], ones=C.ones64[:, :], n=HD)
                       for k, i in ((ks, 1), (kw, 2))]
            groups += [dict(src=[cq[:, 0], cq[:, 1]], gain=[gcq[:, 0:1], gcq[:, 1:2]], dst=[cq[:, 0], cq[:, 1]],
                            ones=C.ones[:, :], n=2 * P),
                       dict(src=[ckv[:, :]], gain=[gckv[:, 0:1]], dst=[ckv[:, :]], ones=C.ones[:, :], n=P)]
            norm_features(nc, C, "ev_norms", groups)

            def take_X(v, g):
                def f(ps, steps):
                    for a in range(2):
                        h = slice(a * HD, (a + 1) * HD)
                        src = ps[h].rearrange("p (c j a) -> p j c a", j=8, a=2)
                        for jh in range(2):
                            js = slice(8 * jh, 8 * jh + 8)
                            ins = nc.vector.tensor_tensor(X[h, v, js, g, 0:NCMP], src[:, :, jh:jh + NCMP, a],
                                                          bcast(pos[h, v, js].unsqueeze(2), [HD, 8, NCMP]), ALU.add)
                    return ins
                return f

            products(nc, C, "ev_X", [([(pair[:, g], (kc, vc)[v][:, :])], slice(0, P),
                                      slice(0, SEQ), take_X(v, g)) for v in range(2) for g in range(2)])
            products(nc, C, "ev_hid", [([(w1[:, v, j, a * P:(a + 1) * P], X[:, v, j].rearrange("p g c -> p (g c)")) for j in range(16)],
                                        slice(0, P), slice(0, 64), copy_to(nc, hid[:, v, a])) for v in range(2) for a in range(2)],
                     lambda n: [(loaded["cmp"], 96)] if n == 0 else [])
            with stage(nc, "ev_gelu", "gelu sigmoid") as (block, s):
                @block.scalar
                def _(act):
                    nc.scalar.activation(hid[:, :, :, :], hid[:, :, :, :], ACT.Gelu_apprx_tanh).then_inc(s["gelu"], 1)
                    nc.scalar.activation(gate[:, :, :], gate[:, :, :], ACT.Sigmoid).then_inc(s["sigmoid"], 1)

                @block.vector
                def _(dve):
                    dve.wait_ge(s["gelu"], 1)
                    for a in range(2):
                        for g in range(2):
                            nc.vector.tensor_copy(hid4[:, a, g], bcast(hid[:, 1, a, g * 32:g * 32 + 32].unsqueeze(1), [P, 4, 32]))

                @block.gpsimd
                def _(pool):
                    pool.wait_ge(s["sigmoid"], 1)
                    g0 = gate[:, 0].rearrange("p (h b) -> p h b", b=3)[:, :, 0]
                    nc.gpsimd.affine_select(out=g0, in_=g0, compare_op=ALU.is_ge, fill=0.0, base=-(CMP_L - 1),
                                            pattern=[[0, NH]], channel_multiplier=1)

            def take_vblk(g):
                def f(ps, steps):
                    for h in range(4):
                        ins = nc.vector.tensor_copy(vblk[32 * h:32 * h + 32, g, h], ps[32 * h:32 * h + 32])
                    return ins
                return f

            jobs = [([(w2[:, 0, a], hid[:, 0, a]) for a in range(2)], slice(0, P), slice(0, 64), copy_to(nc, kcT[:, :]))]
            jobs += [([(hid4[:, a, g].rearrange("p r c -> p (r c)"), w2[:, 1, a, 0:HD]) for a in range(2)], slice(0, P), slice(0, HD),
                      take_vblk(g)) for g in range(2)]
            products(nc, C, "ev_cmp", jobs)
            norm_features(nc, C, "ev_kc", [dict(src=[kcT[:, :]], gain=[gk[:, 0:1]], dst=[kcT[:, :]], ones=C.ones64[:, :], n=HD)])

            with ExitStack() as m2, stage(nc, "ev_pc", "scored steps exped turned") as (block, s):
                sc = sb("sc", [P, NT, NH, 32], m2)
                mx = sb("mx", [P, 3, NT, NH], m2)
                PS = C.PS

                @block.tensor
                def _(pe):
                    for t in range(NT):
                        for h in range(NH):
                            g = h // 4
                            half = slice(g * HD, (g + 1) * HD)
                            ins = nc.tensor.matmul(PS[:, 4 * g + t, h % 4 * 32:(h % 4 + 1) * 32], q[half, h % 4, t * P:(t + 1) * P],
                                                   kcT[half, g * 32:(g + 1) * 32], start=True, stop=True)
                            if h % 4 == 3:
                                ins.then_inc(s["scored"], 1)
                    pe.wait_ge(s["steps"], 2 * NT + 7)
                    for t in range(NT):
                        for g in range(2):
                            nc.tensor.transpose(PS[:, g, t * P:(t + 1) * P],
                                                sc[:, t, 4 * g:4 * g + 4].rearrange("p h c -> p (h c)"), C.ident[:, :])                                 .then_inc(s["turned"], 1)

                @block.scalar
                def _(act):
                    act.wait_ge(s["steps"], 2 * NT + 3)
                    nc.scalar.activation(sc[:, :, :, :], sc[:, :, :, :], ACT.Exp).then_inc(s["exped"], 1)

                @block.vector
                def _(dve):
                    step = Steps(dve, s["steps"])
                    for t in range(NT):
                        for g in range(2):
                            hs = slice(4 * g, 4 * g + 4)
                            dve.wait_ge(s["scored"], 2 * t + g + 1)
                            step(nc.vector.tensor_tensor(sc[:, t, hs].rearrange("p h c -> p (h c)"), PS[:, 4 * g + t, 0:P],
                                                         Tc[:, t, hs].rearrange("p h c -> p (h c)"), ALU.add))
                    rows = sc[:, :, :, :].rearrange("p t h c -> p (t h) c")
                    m = [mx[:, i].rearrange("p t h -> p (t h)") for i in range(3)]
                    step(nc.vector.tensor_reduce(m[0], rows, AX.X, ALU.max))
                    step(nc.vector.tensor_tensor(rows, rows, bcast(m[0].unsqueeze(2), [P, NT * NH, 32]), ALU.subtract))
                    dve.sem_inc(s["steps"], 1)
                    step.n += 1
                    dve.wait_ge(s["exped"], 1)
                    step(nc.vector.tensor_reduce(m[1], rows, AX.X, ALU.add))
                    step(nc.vector.reciprocal(m[2], m[1]))
                    g0 = gate[:, :, :].rearrange("p t (h b) -> p (t h) b", b=3)[:, :, 0]
                    step(nc.vector.tensor_tensor(m[2], m[2], g0, ALU.mult))
                    step(nc.vector.tensor_tensor(rows, rows, bcast(m[2].unsqueeze(2), [P, NT * NH, 32]), ALU.mult))
                    dve.wait_ge(s["turned"], 2 * NT)
                    nc.vector.tensor_copy(pcT[:, :, :], PS[:, 0:2, :])

        wout = sb("wout", [P, 8, DM])
        cosT, sinT, turn = sb("cos", [P, SEQ]), sb("sin", [P, SEQ]), sb("turn", [P, ROT])
        with stage(nc, "ev_out_load", "x") as (block, s):
            @block.sync
            def _(sp):
                for dst, src in ((cosT[64:96, :], D["rope_table"][0]), (sinT[64:96, :], D["rope_table"][1]),
                                 (turn[64:96, :], D["rope_turn"])):
                    sp.dma_start(dst, src).then_inc(loaded["rope"], 16)
                sp.dma_start(wout[:, :, :], D["ev_w_out"][0].rearrange("(k p) n -> p k n", p=P)).then_inc(loaded["out"], 16)

        jobs = []
        for h in range(NH):
            g, half = h // 4, slice(h // 4 * HD, (h // 4 + 1) * HD)
            out = slice(h % 2 * HD, (h % 2 + 1) * HD)
            for br, k in enumerate((ks, kw)):
                jobs.append(dict(q=q[half, h % 4], k=k[half, :], v=lambda kb, br=br, half=half: vsw[:, kb, br, half],
                                 bias=T[:, h], extra=None, gate=lambda i, h=h, br=br: gate[:, i, 3 * h + 1 + br:3 * h + 2 + br],
                                 first=(vblk[:, g, h % 4], pcT[:, g]) if br == 0 else None, start=br == 0, stop=br == 1,
                                 rows=out, bank=h // 2 % 2, out=yT[out, h // 2]))
        attention(nc, C, "ev_nsa", jobs)

        with ExitStack() as m3:
            km, vm = sb("km", [MQK, NH, SEQ], m3), sb("vm", [P, NT, 512], m3)
            qm = xnT[0:MQK]

            def take_k(h):
                def f(ps, steps):
                    nc.vector.tensor_copy(km[64:96, h], kr[64:96, :])
                    return nc.vector.tensor_copy(km[0:64, h], ps)
                return f

            jobs = []
            for h in range(NH):
                jobs.append(([(uq[:, k, MQK * h:MQK * (h + 1)], cq[:, k]) for k in range(2)], slice(0, MQK), slice(0, SEQ),
                             copy_to(nc, qm[:, h])))
                jobs.append(([(ukv[:, P * h:P * h + HD], ckv[:, :])], slice(0, HD), slice(0, SEQ), take_k(h)))
            vcols = ukv[:, :].rearrange("p (h d) -> p h d", d=P)[:, :, HD:P]
            for t in range(NT):
                jobs.append(([(ckv[:, t * P:(t + 1) * P], vcols)], slice(0, P), slice(0, SEQ), copy_to(nc, vm[:, t])))
            products(nc, C, "ev_mla_in", jobs, lambda n: [(loaded["mla"], 32)] if n == 0 else [])
            norm_features(nc, C, "ev_mla_norm", [
                dict(src=[t[0:MQK, h]], gain=[g[0:MQK, 0:1]], dst=[t[0:MQK, h]], ones=C.ones[0:MQK, 0:MQK], n=MQK)
                for h in range(NH) for t, g in ((qm, gmq), (km, gmk))])

            with stage(nc, "ev_rope", "turned steps") as (block, s):
                r = slice(64, 96)
                tiles = [t[r, h] for h in range(NH) for t in (qm, km)]
                PS = C.PS

                @block.tensor
                def _(pe):
                    pe.wait_ge(loaded["rope"], 48)
                    for n, tile in enumerate(tiles):
                        if n >= 8:
                            pe.wait_ge(s["steps"], 3 * (n - 7))
                        nc.tensor.matmul(PS[r, n % 8, :], turn[r, :], tile, start=True, stop=True).then_inc(s["turned"], 1)

                @block.vector
                def _(dve):
                    step = Steps(dve, s["steps"])
                    dve.wait_ge(loaded["rope"], 48)
                    for n, tile in enumerate(tiles):
                        dve.wait_ge(s["turned"], n + 1)
                        step(nc.vector.tensor_tensor(tile, tile, cosT[r, :], ALU.mult))
                        step(nc.vector.tensor_tensor(PS[r, n % 8, :], PS[r, n % 8, :], sinT[r, :], ALU.mult))
                        step(nc.vector.tensor_tensor(tile, tile, PS[r, n % 8, :], ALU.add))

            jobs = []
            for h in range(NH):
                out = slice(h % 2 * HD, (h % 2 + 1) * HD)
                jobs.append(dict(q=qm[:, h], k=km[:, h], v=lambda kb, h=h: vm[:, kb, h * HD:(h + 1) * HD],
                                 bias=C.causal[:, :], extra=None, gate=None, first=None, start=True, stop=True,
                                 rows=out, bank=h // 2 % 2, out=yT[out, 4 + h // 2]))
            attention(nc, C, "ev_mla", jobs)
        if "yT_out" in D:
            with stage(nc, "dbg", "l") as (block, s):
                @block.sync
                def _(sp):
                    sp.dma_start(D["yT_out"].rearrange("(k p) t -> p k t", p=P), yT[:, :, :]).then_inc(s["l"], 16)
                    sp.wait_ge(s["l"], 16)
        add_projection(nc, C, "ev_out", yT, wout, x, (loaded["out"], 16))
        nc.clear_and_free_semaphores(list(loaded.values()))
        nc.all_engine_barrier(sem_only=True)


def mixer_odd(nc, C, D, x, xnT):
    TAPS = 3
    with ExitStack() as mem:
        def sb(name, shape):
            return mem.enter_context(nc.sbuf_tensor("od_" + name, shape, F32))

        yT = sb("yT", [P, 8, SEQ])
        W = sb("W", [P, KD, 3 * DM])
        wout = sb("wout", [P, 8, DM])
        gx, taps = sb("gx", [P, KD]), sb("taps", [P, TAPS, 8])
        cg, cu, conv = sb("cg", [P, SEQ]), sb("cu", [P, 2, SEQ + TAPS - 1]), sb("conv", [P, 2, SEQ])
        loaded = {n: nc.alloc_semaphore("od_loaded_" + n) for n in "small w0 w1 w2 w3 out".split()}
        win = D["od_w_in"][0].rearrange("(p k) (s n) -> p k s n", k=KD, s=3)
        with stage(nc, "od_load", "zeroed") as (block, s):
            @block.sync
            def _(sp):
                sp.dma_start(gx[:, :], D["od_mix_norm"][0].rearrange("(p k) -> p k", k=KD)).then_inc(loaded["small"], 16)
                for i in range(TAPS):
                    sp.dma_start(taps[:, i], D["conv_w"][0, i].rearrange("(j p) -> p j", p=P),
                                 allow_slow_non_contiguous=True).then_inc(loaded["small"], 16)
                for i in range(4):
                    for part in range(3):
                        sp.dma_start(W[:, :, part * DM + i * 256:part * DM + i * 256 + 256],
                                     win[:, :, part, i * 256:i * 256 + 256]).then_inc(loaded[f"w{i}"], 16)
                sp.dma_start(wout[:, :, :], D["od_w_out"][0].rearrange("(k p) n -> p k n", p=P)).then_inc(loaded["out"], 16)

            @block.vector
            def _(dve):
                nc.vector.memset(cu[:, :, 0:TAPS - 1], 0.0)
                dve.wait_ge(loaded["small"], 16 * (TAPS + 1))

        norm_transpose(nc, C, x, gx, xnT, yT[:, :, :].rearrange("p (t a) b -> p t (a b)", a=2), "od_norm")

        def take_cu(j):
            def f(ps, steps):
                steps(nc.vector.tensor_tensor(cu[:, j % 2, TAPS - 1:], cg[:, :], ps, ALU.mult))
                steps(nc.vector.tensor_scalar(conv[:, j % 2], cu[:, j % 2, 0:SEQ], taps[:, 0, j:j + 1], None, ALU.mult))
                for i in range(1, TAPS - 1):
                    steps(nc.vector.scalar_tensor_tensor(out=conv[:, j % 2], in0=cu[:, j % 2, i:i + SEQ], scalar=taps[:, i, j:j + 1],
                                                         in1=conv[:, j % 2], op0=ALU.mult, op1=ALU.add))
                i = TAPS - 1
                return nc.vector.scalar_tensor_tensor(out=conv[:, j % 2], in0=cu[:, j % 2, i:i + SEQ], scalar=taps[:, i, j:j + 1],
                                                      in1=conv[:, j % 2], op0=ALU.mult, op1=ALU.add)
            return f

        jobs = []
        for j in range(8):
            for part, take in ((1, copy_to(nc, cg[:, :])), (2, take_cu(j)),
                               (0, lambda ps, steps, j=j: nc.vector.tensor_tensor(yT[:, j], ps, conv[:, j % 2], ALU.mult))):
                a = part * DM + j * P
                jobs.append(([(W[:, k, a:a + P], xnT[:, k]) for k in range(KD)], slice(0, P), slice(0, SEQ), take))
        products(nc, C, "od_in", jobs, lambda n: [(loaded[f"w{n // 6}"], 48)], chained=True)
        add_projection(nc, C, "od_out", yT, wout, x, (loaded["out"], 16))
        nc.clear_and_free_semaphores(list(loaded.values()))
        nc.all_engine_barrier(sem_only=True)


def first_max(nc, step, scores, index, low, top, at, hit, shape):
    step(nc.vector.tensor_reduce(top, scores, AX.X, ALU.max))
    step(nc.vector.tensor_tensor(hit, scores, bcast(top.unsqueeze(2), shape), ALU.is_equal))
    step(nc.vector.scalar_tensor_tensor(out=hit, in0=hit, scalar=-16.0, in1=index, op0=ALU.mult, op1=ALU.add))
    step(nc.vector.tensor_reduce(at, hit, AX.X, ALU.min))
    step(nc.vector.tensor_tensor(hit, low, bcast(at.unsqueeze(2), shape), ALU.is_equal))


def make_index(nc, name, mem, n):
    index, low = (mem.enter_context(nc.sbuf_tensor(name + s, [P, NT, n], F32)) for s in ("_index", "_low"))
    with stage(nc, name, "made") as (block, s):
        @block.gpsimd
        def _(pool):
            nc.gpsimd.iota(index[:, :, :], pattern=[[0, NT], [1, n]], base=0, channel_multiplier=0,
                           allow_small_or_imprecise_dtypes=True).then_inc(s["made"], 1)
            pool.wait_ge(s["made"], 1)
            nc.gpsimd.tensor_scalar(low[:, :, :], index[:, :, :], 16.0, None, ALU.subtract)
    return index, low


def two_of(nc, C, name, mem, scores, n, factor=None):
    def sb(s, shape):
        return mem.enter_context(nc.sbuf_tensor(name + s, shape, F32))

    index, low = make_index(nc, name + "_index", mem, n)
    one, two, rest, w = (sb(a, [P, NT, n]) for a in ("_one", "_two", "_rest", "_w"))
    t = sb("_t", [P, 6, NT])
    shape = [P, NT, n]
    with stage(nc, name, "steps exped") as (block, s):
        @block.vector
        def _(dve):
            step = Steps(dve, s["steps"])
            first_max(nc, step, scores, index[:, :, :], low[:, :, :], t[:, 0], t[:, 1], one[:, :, :], shape)
            step(nc.vector.scalar_tensor_tensor(out=rest[:, :, :], in0=one[:, :, :], scalar=NEG, in1=scores, op0=ALU.mult, op1=ALU.add))
            first_max(nc, step, rest[:, :, :], index[:, :, :], low[:, :, :], t[:, 2], t[:, 1], two[:, :, :], shape)
            step(nc.vector.tensor_tensor(t[:, 3], t[:, 2], t[:, 0], ALU.subtract))
            dve.wait_ge(s["exped"], 1)
            step(nc.vector.tensor_scalar(t[:, 1], t[:, 4], 1.0, None, ALU.add))
            step(nc.vector.reciprocal(t[:, 0], t[:, 1]))
            step(nc.vector.tensor_tensor(t[:, 2], t[:, 4], t[:, 0], ALU.mult))
            step(nc.vector.tensor_tensor(one[:, :, :], one[:, :, :], bcast(t[:, 0].unsqueeze(2), shape), ALU.mult))
            step(nc.vector.tensor_tensor(two[:, :, :], two[:, :, :], bcast(t[:, 2].unsqueeze(2), shape), ALU.mult))
            step(nc.vector.tensor_tensor(w[:, :, :], one[:, :, :], two[:, :, :], ALU.add))

        @block.scalar
        def _(act):
            act.wait_ge(s["steps"], 12)
            nc.scalar.activation(t[:, 4], t[:, 3], ACT.Exp).then_inc(s["exped"], 1)
    return w


def logits(nc, C, name, xnT, w, bias, out, n):
    jobs = [([(xnT[:, k, t * P:(t + 1) * P], w[:, k]) for k in range(KD)], slice(0, P), slice(0, n),
             lambda ps, steps, t=t: nc.vector.tensor_tensor(out[:, t], ps, bias, ALU.add)) for t in range(NT)]
    products(nc, C, name, jobs)


def moe_top2(nc, C, D, x, xnT):
    NE, F = D["moe_w_gate"].shape[1], D["moe_w_gate"].shape[3]
    with ExitStack() as mem:
        def sb(name, shape):
            return mem.enter_context(nc.sbuf_tensor("moe_" + name, shape, F32))

        gx, wr, br, score = sb("gx", [P, KD]), sb("wr", [P, KD, NE]), sb("br", [P, NE]), sb("score", [P, NT, NE])
        with stage(nc, "moe_load", "loaded") as (block, s):
            @block.sync
            def _(sp):
                sp.dma_start(gx[:, :], D["od_ffn_norm"][0].rearrange("(p k) -> p k", k=KD)).then_inc(s["loaded"], 16)
                sp.dma_start(wr[:, :, :], D["moe_w_router"][0].rearrange("(p k) n -> p k n", k=KD)).then_inc(s["loaded"], 16)
                sp.dma_start(br[:, :], D["moe_b_router"].partition_broadcast(P).rearrange("p a n -> p (a n)")).then_inc(s["loaded"], 16)
                sp.wait_ge(s["loaded"], 48)
        with ExitStack() as m2:
            xs = m2.enter_context(nc.sbuf_tensor("moe_xs", [P, NT, DM], F32))
            norm_transpose(nc, C, x, gx, xnT, xs, "moe_norm")
        logits(nc, C, "moe_logits", xnT, wr, br[:, :], score, NE)
        w = two_of(nc, C, "moe_route", mem, score[:, :, :], NE)
        gv, uv = (D[n][0].rearrange("e (p k) f -> e p k f", k=KD) for n in ("moe_w_gate", "moe_w_up"))
        dv = D["moe_w_down"][0].rearrange("e (c p) d -> e p c d", p=P)
        gated_parts(nc, C, "moe", xnT, x, NE, F, lambda e: gv[e], lambda e: uv[e], lambda e: dv[e],
                    lambda t, e: w[:, t, bass.ds(e, 1)])


def ffn(nc, C, D, x, xnT):
    with ExitStack() as mem:
        gx = mem.enter_context(nc.sbuf_tensor("ffn_gx", [P, KD], F32))
        with stage(nc, "ffn_load", "loaded") as (block, s):
            @block.sync
            def _(sp):
                sp.dma_start(gx[:, :], D["ev_ffn_norm"][0].rearrange("(p k) -> p k", k=KD)).then_inc(s["loaded"], 16)
                sp.wait_ge(s["loaded"], 16)
        with ExitStack() as m2:
            xs = m2.enter_context(nc.sbuf_tensor("ffn_xs", [P, NT, DM], F32))
            norm_transpose(nc, C, x, gx, xnT, xs, "ffn_norm")
        parts = 2
        F = D["ffn_w_gate"].shape[2] // parts
        gv, uv = (D[n][0].rearrange("(p k) (e f) -> e p k f", k=KD, f=F) for n in ("ffn_w_gate", "ffn_w_up"))
        dv = D["ffn_w_down"][0].rearrange("(e c p) d -> e p c d", e=parts, p=P)
        gated_parts(nc, C, "ffn", xnT, x, parts, F, lambda e: gv[e], lambda e: uv[e], lambda e: dv[e], lambda t, e: C.one[:, 0:1])


def moe_groups(nc, C, D, x, xnT):
    NE, F = D["exp_w_gate_2"].shape[1], D["exp_w_gate_2"].shape[3]
    NG = D["router_gw_2"].shape[2]
    PG = NE // NG
    with ExitStack() as mem:
        def sb(name, shape):
            return mem.enter_context(nc.sbuf_tensor("hm_" + name, shape, F32))

        gx, wr, br, score = sb("gx", [P, KD]), sb("wr", [P, KD, NG + NE]), sb("br", [P, NG + NE]), sb("score", [P, NT, NG + NE])
        with stage(nc, "hm_load", "loaded") as (block, s):
            @block.sync
            def _(sp):
                sp.dma_start(gx[:, :], D["norm2_g_2"][0].rearrange("(p k) -> p k", k=KD)).then_inc(s["loaded"], 16)
                for w, b, a, n in (("router_gw_2", "router_gb_2", 0, NG), ("router_ew_2", "router_eb_2", NG, NE)):
                    sp.dma_start(wr[:, :, a:a + n], D[w][0].rearrange("(p k) n -> p k n", k=KD)).then_inc(s["loaded"], 16)
                    sp.dma_start(br[:, a:a + n], D[b].partition_broadcast(P).rearrange("p a n -> p (a n)")).then_inc(s["loaded"], 16)
                sp.wait_ge(s["loaded"], 80)
        with ExitStack() as m2:
            xs = m2.enter_context(nc.sbuf_tensor("hm_xs", [P, NT, DM], F32))
            norm_transpose(nc, C, x, gx, xnT, xs, "hm_norm")
        logits(nc, C, "hm_logits", xnT, wr, br[:, :], score, NG + NE)
        index, low = make_index(nc, "hm_index", mem, NG)
        group, ex, sel, t = sb("group", [P, NT, NG]), sb("ex", [P, NT, NG]), sb("sel", [P, NT, PG]), sb("t", [P, 4, NT])
        chosen = sb("chosen", [P, NT, NG, PG])
        W = sb("W", [P, NT, NG, PG])
        shape = [P, NT, NG]
        with stage(nc, "hm_group", "steps exped") as (block, s):
            @block.vector
            def _(dve):
                step = Steps(dve, s["steps"])
                first_max(nc, step, score[:, :, 0:NG], index[:, :, :], low[:, :, :], t[:, 0], t[:, 1], group[:, :, :], shape)
                step(nc.vector.tensor_tensor(ex[:, :, :], score[:, :, 0:NG], bcast(t[:, 0].unsqueeze(2), shape), ALU.subtract))
                el = score[:, :, NG:NG + NE].rearrange("p t (g e) -> p t g e", g=NG)
                for i in range(NT):
                    nc.vector.tensor_tensor(chosen[:, i], el[:, i], bcast(group[:, i].unsqueeze(2), [P, NG, PG]), ALU.mult)
                step(nc.vector.tensor_copy(t[:, 1], t[:, 0]))
                step(nc.vector.tensor_reduce(sel[:, :, :], chosen[:, :, :, :].rearrange("p t g e -> p t e g"), AX.X, ALU.add))
                dve.wait_ge(s["exped"], 1)
                step(nc.vector.tensor_reduce(t[:, 2], ex[:, :, :], AX.X, ALU.add))
                step(nc.vector.reciprocal(t[:, 3], t[:, 2]))

            @block.scalar
            def _(act):
                act.wait_ge(s["steps"], 6)
                nc.scalar.activation(ex[:, :, :], ex[:, :, :], ACT.Exp).then_inc(s["exped"], 1)
        w = two_of(nc, C, "hm_route", mem, sel[:, :, :], PG)
        with stage(nc, "hm_weights", "steps") as (block, s):
            @block.vector
            def _(dve):
                step = Steps(dve, s["steps"])
                step(nc.vector.tensor_tensor(w[:, :, :], w[:, :, :], bcast(t[:, 3].unsqueeze(2), [P, NT, PG]), ALU.mult))
                for i in range(NT):
                    nc.vector.tensor_tensor(W[:, i], bcast(w[:, i].unsqueeze(1), [P, NG, PG]),
                                            bcast(group[:, i].unsqueeze(2), [P, NG, PG]), ALU.mult)
        Wf = W[:, :, :, :].rearrange("p t g e -> p t (g e)")
        gv, uv = (D[n][0].rearrange("e (p k) f -> e p k f", k=KD) for n in ("exp_w_gate_2", "exp_w_up_2"))
        dv = D["exp_w_down_2"][0].rearrange("e (c p) d -> e p c d", p=P)
        gated_parts(nc, C, "hm", xnT, x, NE, F, lambda e: gv[e], lambda e: uv[e], lambda e: dv[e],
                    lambda t, e: Wf[:, t, bass.ds(e, 1)])


LW, FW, RW = 256, 512, 256
XA0, GA0, FQ0, FK0, FV0, FL0, PC0, IN_W = 0, 256, 512, 1024, 1536, 2048, 2056, 2952
CHUNK = 64
SUB = 16


def wkv_masks():
    r, c = np.arange(P)[:, None], np.arange(P)[None, :]
    same = lambda n: (r // n) == (c // n)
    return np.stack([same(SUB) & (r > c), same(SUB) & (r < c), same(2 * SUB) & ~same(SUB) & (r > c),
                     same(CHUNK) & ~same(2 * SUB) & (r > c), same(CHUNK) & (r < c), same(CHUNK) & (r <= c)]).astype(np.float32)


def chunk_restart():
    return np.broadcast_to((np.arange(SEQ) % CHUNK != 0).astype(np.float32), (P, SEQ)).copy()


def mixer_second(nc, C, D, x, xnT):
    with ExitStack() as mem:
        def sb(name, shape, m=mem):
            return m.enter_context(nc.sbuf_tensor("s_" + name, shape, F32))

        yT = sb("yT", [P, 8, SEQ])
        pm = sb("pm", [P, 7, SEQ + 1])
        cols = {}
        for n, w in (("gx", KD), ("lng", 2), ("cb", 2), ("ba", 2), ("bx", 2), ("lam", 2), ("fqg", 1), ("fkg", 1), ("fng", 4),
                     ("mu", 7), ("w0", 2), ("a0", 2), ("kk", 2), ("ka", 2), ("rk", 2), ("rlg", 2), ("rlb", 2), ("fb", 1)):
            cols[n] = sb(n, [P, w])
        taps = sb("taps", [P, 4, 2])
        wa, wx = sb("wa", [P, 2, P]), sb("wx", [P, 2, P])
        low = sb("low", [P, 3, RW])
        loaded = {n: nc.alloc_semaphore("s_loaded_" + n) for n in "small w0 w1 w2 w3 w4 w5 wkv out".split()}
        pieces = [(XA0, FQ0), (FQ0, FK0), (FK0, FV0), (FV0, FL0), (FL0, PC0 + 448), (PC0 + 448, IN_W)]
        memF = ExitStack()
        xa, ga = sb("xa", [P, 2, SEQ + 3], memF), sb("ga", [P, 2, SEQ], memF)
        fq, fk, fv, fl = sb("fq", [P, 4, SEQ], memF), sb("fk", [P, 4, SEQ], memF), sb("fv", [P, NT, SEQ], memF), sb("fl", [8, SEQ], memF)
        small = 0
        with ExitStack() as memW:
            W = sb("W", [P, KD, IN_W], memW)
            win = D["w_in_2"][0].rearrange("(p k) n -> p k n", k=KD)
            with stage(nc, "s_load", "zeroed") as (block, s):
                @block.sync
                def _(sp):
                    nonlocal small
                    sp.wait_ge(s["zeroed"], 2)
                    tiles = lambda n: D[n][0].rearrange("(i p) -> p i", p=P)
                    smalls = [(cols["gx"][:, :], D["norm1_g_2"][0].rearrange("(p k) -> p k", k=KD))]
                    smalls += [(cols[c][:, :], tiles(n)) for c, n in (
                        ("lng", "lru_norm_g_2"), ("cb", "conv_b_2"), ("ba", "lru_ba_2"), ("bx", "lru_bx_2"), ("lam", "lru_lambda_2"),
                        ("fng", "fox_norm_g_2"), ("mu", "rwkv_mu_2"), ("w0", "rwkv_w0_2"), ("a0", "rwkv_a0_2"), ("kk", "rwkv_kk_2"),
                        ("ka", "rwkv_ka_2"), ("rlg", "rwkv_ln_g_2"), ("rlb", "rwkv_ln_b_2"))]
                    smalls += [(cols["rk"][:, :], D["rwkv_rk_2"][0].rearrange("(i a) d -> (a d) i", a=2)),
                               (cols["fb"][0:8, :], column(D["fox_fb_2"][0]))]
                    for a in (0, HD):
                        smalls += [(cols["fqg"][a:a + HD, :], column(D["fox_qnorm_g_2"][0])),
                                   (cols["fkg"][a:a + HD, :], column(D["fox_knorm_g_2"][0]))]
                        for i in range(2):
                            smalls += [(wa[a:a + HD, i, a:a + HD], D["lru_wa_2"][0, 2 * i + a // HD]),
                                       (wx[a:a + HD, i, a:a + HD], D["lru_wx_2"][0, 2 * i + a // HD])]
                    smalls += [(taps[:, i], D["conv_w_2"][0, i].rearrange("(j p) -> p j", p=P)) for i in range(4)]
                    smalls += [(low[0:32, 0], D["rwkv_w2_2"][0]), (low[32:64, 1], D["rwkv_a2_2"][0]), (low[64:128, 2], D["rwkv_g2_2"][0])]
                    for dst, src in smalls:
                        sp.dma_start(dst, src, allow_slow_non_contiguous=True).then_inc(loaded["small"], 16)
                    small = 16 * len(smalls)
                    for i, (a, b) in enumerate(pieces):
                        sp.dma_start(W[:, :, a:b], win[:, :, a:b]).then_inc(loaded[f"w{i}"], 16)

                @block.vector
                def _(dve):
                    nc.vector.memset(wa[:, :, :], 0.0).then_inc(s["zeroed"], 1)
                    nc.vector.memset(wx[:, :, :], 0.0).then_inc(s["zeroed"], 1)
                    nc.vector.memset(xa[:, :, 0:3], 0.0)
                    nc.vector.memset(pm[:, :, 0:1], 0.0)
                    dve.wait_ge(loaded["small"], small)
                    nc.vector.tensor_scalar(cols["fqg"][:, :], cols["fqg"][:, :], float(HD) ** -0.5, None, ALU.mult)

            norm_transpose(nc, C, x, cols["gx"], xnT, yT[:, :, :].rearrange("p (t a) b -> p t (a b)", a=2), "s_norm")

            jobs, need = [], []

            def features(a, M, dst, w):
                jobs.append(([(W[:, k, a:a + M], xnT[:, k]) for k in range(KD)], slice(0, M), slice(0, SEQ), copy_to(nc, dst)))
                need.append(w)

            for i in range(2):
                features(XA0 + i * P, P, xa[:, i, 3:], [0])
                features(GA0 + i * P, P, ga[:, i], [0])
            for i in range(4):
                features(FQ0 + i * P, P, fq[:, i], [1])
            for i in range(4):
                features(FK0 + i * P, P, fk[:, i], [2])
            for t in range(NT):
                jobs.append(([(xnT[:, k, t * P:(t + 1) * P], W[:, k, FV0:FV0 + FW]) for k in range(KD)], slice(0, P), slice(0, FW),
                             copy_to(nc, fv[:, t])))
                need.append([3])
            features(FL0, 8, fl[:, :], [4])
            for i in range(7):
                features(PC0 + i * P, P, pm[:, i, 1:], [4, 5])
            products(nc, C, "s_in", jobs, lambda n: [(loaded[f"w{i}"], 16) for i in need[n]])

        with ExitStack() as m:
            xc, r, i_, la, h = (sb(n, [P, 2, SEQ], m) for n in ("xc", "r", "i", "la", "h"))
            lc = sb("lc", [P, 6, 2], m)
            both = [P, 2 * SEQ]
            flat = lambda ap: ap.rearrange("p a b -> p (a b)")
            with stage(nc, "s_conv", "steps") as (block, s):
                @block.vector
                def _(dve):
                    step = Steps(dve, s["steps"])
                    for i in range(2):
                        step(nc.vector.tensor_scalar(xc[:, i], xa[:, i, 0:SEQ], taps[:, 0, i:i + 1], cols["cb"][:, i:i + 1], ALU.mult, ALU.add))
                        for j in range(1, 4):
                            step(nc.vector.scalar_tensor_tensor(out=xc[:, i], in0=xa[:, i, j:j + SEQ], scalar=taps[:, j, i:i + 1],
                                                                in1=xc[:, i], op0=ALU.mult, op1=ALU.add))
            products(nc, C, "s_lru_gates", [([(w[:, i], xc[:, i])], slice(0, P), slice(0, SEQ), copy_to(nc, dst[:, i]))
                                            for w, dst in ((wa, r), (wx, i_)) for i in range(2)])
            with stage(nc, "s_lru", "steps act") as (block, s):
                @block.scalar
                def _(act):
                    step = Steps(act, s["act"])
                    for i in range(2):
                        nc.scalar.activation(r[:, i], r[:, i], ACT.Sigmoid, bias=cols["ba"][:, i:i + 1])
                        nc.scalar.activation(i_[:, i], i_[:, i], ACT.Sigmoid, bias=cols["bx"][:, i:i + 1])
                    act.wait_ge(s["steps"], 2)
                    step(nc.scalar.activation(lc[:, 2], lc[:, 1], ACT.Exp))
                    step(nc.scalar.activation(lc[:, 3], lc[:, 2], ACT.Ln, bias=C.one[:, 0:1]))
                    act.wait_ge(s["steps"], 6)
                    step(nc.scalar.activation(flat(h[:, :, :]), flat(la[:, :, :]), ACT.Tanh))
                    step(nc.scalar.activation(flat(la[:, :, :]), flat(la[:, :, :]), ACT.Exp))
                    act.wait_ge(s["steps"], 10)
                    step(nc.scalar.activation(flat(h[:, :, :]), flat(h[:, :, :]), ACT.Sqrt))
                    step(nc.scalar.activation(flat(ga[:, :, :]), flat(ga[:, :, :]), ACT.Gelu_apprx_tanh))

                @block.vector
                def _(dve):
                    step = Steps(dve, s["steps"])
                    lam = cols["lam"][:, :]
                    step(nc.vector.tensor_scalar(lc[:, 0], lam, -1.0, 0.0, ALU.mult, ALU.max))
                    step(nc.vector.scalar_tensor_tensor(out=lc[:, 1], in0=lc[:, 0], scalar=-2.0, in1=lam, op0=ALU.mult, op1=ALU.subtract))
                    dve.wait_ge(s["act"], 2)
                    step(nc.vector.tensor_tensor(lc[:, 4], lc[:, 0], lc[:, 3], ALU.add))
                    step(nc.vector.tensor_scalar(lc[:, 5], lc[:, 4], -8.0, None, ALU.mult))
                    for i in range(2):
                        step(nc.vector.tensor_scalar(la[:, i], r[:, i], lc[:, 5, i:i + 1], None, ALU.mult))
                    dve.wait_ge(s["act"], 4)
                    step(nc.vector.tensor_tensor(flat(r[:, :, :]), flat(la[:, :, :]), flat(la[:, :, :]), ALU.mult))
                    step(nc.vector.tensor_scalar(flat(r[:, :, :]), flat(r[:, :, :]), -1.0, -1.0, ALU.mult, ALU.add))
                    step(nc.vector.tensor_tensor(flat(h[:, :, :]), flat(h[:, :, :]), flat(r[:, :, :]), ALU.mult))
                    step(nc.vector.tensor_tensor(flat(i_[:, :, :]), flat(i_[:, :, :]), flat(xc[:, :, :]), ALU.mult))
                    dve.wait_ge(s["act"], 5)
                    step(nc.vector.tensor_tensor(flat(i_[:, :, :]), flat(i_[:, :, :]), flat(h[:, :, :]), ALU.mult))
                    for i in range(2):
                        step(nc.vector.tensor_tensor_scan(xc[:, i], la[:, i], i_[:, i], 0.0, ALU.mult, ALU.add))
                    dve.wait_ge(s["act"], 6)
                    for i in range(2):
                        step(nc.vector.tensor_tensor(yT[:, i], xc[:, i], ga[:, i], ALU.mult))
            norm_features(nc, C, "s_lru_norm", [dict(src=[yT[:, i] for i in range(2)], gain=[cols["lng"][:, i:i + 1] for i in range(2)],
                                                     dst=[yT[:, i] for i in range(2)], ones=C.ones[:, :], n=LW)])

        with ExitStack() as m:
            decay, lf, pick = sb("decay", [P, SEQ], m), sb("lf", [8, 4, SEQ], m), sb("pick", [P, 8, P], m)
            with stage(nc, "s_decay", "steps act") as (block, s):
                @block.vector
                def _(dve):
                    step = Steps(dve, s["steps"])
                    step(nc.vector.memset(decay[:, :], 0.0))
                    step(nc.vector.memset(lf[:, 3], 1.0))
                    step(nc.vector.tensor_scalar(fl[:, :], fl[:, :], cols["fb"][0:8, 0:1], None, ALU.add))
                    step(nc.vector.tensor_scalar(lf[:, 0], fl[:, :], -1.0, 0.0, ALU.mult, ALU.max))
                    step(nc.vector.scalar_tensor_tensor(out=lf[:, 1], in0=lf[:, 0], scalar=-2.0, in1=fl[:, :], op0=ALU.mult, op1=ALU.subtract))
                    nc.vector.tensor_copy(pick[:, :, :], bcast(C.ident[:, 0:8].unsqueeze(2), [P, 8, P]))
                    dve.wait_ge(s["act"], 2)
                    step(nc.vector.tensor_tensor(lf[:, 0], lf[:, 0], lf[:, 2], ALU.add))
                    step(nc.vector.tensor_tensor_scan(decay[0:8, :], lf[:, 3], lf[:, 0], 0.0, ALU.mult, ALU.add))

                @block.scalar
                def _(act):
                    act.wait_ge(s["steps"], 5)
                    nc.scalar.activation(lf[:, 1], lf[:, 1], ACT.Exp).then_inc(s["act"], 1)
                    act.wait_ge(s["act"], 1)
                    nc.scalar.activation(lf[:, 2], lf[:, 1], ACT.Ln, bias=C.one[0:8, 0:1]).then_inc(s["act"], 1)
            norm_features(nc, C, "s_fox_qk", [dict(src=[t[:, i]], gain=[cols[g][:, 0:1]], dst=[t[:, i]], ones=C.ones64[:, :], n=HD)
                                              for i in range(4) for t, g in ((fq, "fqg"), (fk, "fkg"))])
            jobs = []
            for h in range(8):
                half = slice(h % 2 * HD, h % 2 * HD + HD)
                jobs.append(dict(q=fq[half, h // 2], k=fk[half, h // 2], v=lambda kb, h=h: fv[:, kb, h * HD:(h + 1) * HD],
                                 bias=C.causal[:, :], extra=(pick[:, h], decay[:, :]), gate=None, first=None, start=True, stop=True,
                                 rows=half, bank=h // 2 % 2, out=yT[half, 2 + h // 2]))
            attention(nc, C, "s_fox", jobs)
            norm_features(nc, C, "s_fox_norm", [dict(src=[yT[:, 2 + i] for i in range(4)], gain=[cols["fng"][:, i:i + 1] for i in range(4)],
                                                     dst=[yT[:, 2 + i] for i in range(4)], ones=C.ones[:, :], n=FW)])
        memF.close()
        rwkv(nc, C, D, yT, xnT, pm, cols, low, loaded["wkv"])

        if "yT_out" in D:
            with stage(nc, "dbg2", "l") as (block, s):
                @block.sync
                def _(sp):
                    sp.dma_start(D["yT_out"].rearrange("(k p) t -> p k t", p=P), yT[:, :, :]).then_inc(s["l"], 16)
                    sp.wait_ge(s["l"], 16)
        wout = sb("wout", [P, 8, DM])
        with stage(nc, "s_out_load", "x") as (block, s):
            @block.sync
            def _(sp):
                sp.dma_start(wout[:, :, :], D["w_out_2"][0].rearrange("(k p) n -> p k n", p=P)).then_inc(loaded["out"], 16)
        add_projection(nc, C, "s_out", yT, wout, x, (loaded["out"], 16))
        nc.clear_and_free_semaphores(list(loaded.values()))
        nc.all_engine_barrier(sem_only=True)


def paired(nc, C, name, jobs):
    with stage(nc, name, "made taken steps") as (block, s):
        PS = C.PS

        @block.tensor
        def _(pe):
            for n, (after, items, take) in enumerate(jobs):
                need = max(after, n - 3)
                if need > 0:
                    pe.wait_ge(s["taken"], need)
                for bank, cols, rows, lhsT, rhs, start, stop in items:
                    out = PS[rows, 2 * (n % 4) + bank, cols]
                    if start == "turn":
                        ins = nc.tensor.transpose(out, lhsT, rhs)
                    else:
                        ins = nc.tensor.matmul(out, lhsT, rhs, start=start, stop=stop)
                ins.then_inc(s["made"], 1)

        @block.vector
        def _(dve):
            steps = Steps(dve, s["steps"])
            for n, (after, items, take) in enumerate(jobs):
                dve.wait_ge(s["made"], n + 1)
                take(PS[:, 2 * (n % 4):2 * (n % 4) + 2, :], steps).then_inc(s["taken"], 1)
                dve.wait_ge(s["taken"], n + 1)


def rwkv(nc, C, D, yT, xnT, pm, cols, low, loaded):
    PR, HH = 2, 4
    with ExitStack() as mem:
        def sb(name, shape, m=mem):
            return m.enter_context(nc.sbuf_tensor("rw_" + name, shape, F32))

        At, Bt, Kt, Rt, al, gl, bonus, rs, eLx, enL = (sb(n, [P, 2, SEQ]) for n in (
            "At", "Bt", "Kt", "Rt", "al", "gl", "bonus", "rs", "eLx", "enL"))
        eL = sb("eL", [P, 2, SEQ])
        masks, restart = sb("masks", [P, 6, P]), sb("restart", [P, SEQ])
        ocol = sb("ocol", [P, 2])
        flat = lambda ap: ap.rearrange("p a b -> p (a b)")
        p = pm[:, :, 1:]
        with stage(nc, "rw_mix", "steps act diff") as (block, s):
            @block.sync
            def _(sp):
                sp.dma_start(masks[:, :, :], D["wkv_masks"].rearrange("m p c -> p m c")).then_inc(loaded, 16)
                sp.dma_start(restart[:, :], D["chunk_restart"]).then_inc(loaded, 16)

            @block.vector
            def _(dve):
                step = Steps(dve, s["steps"])
                for i in (6, 0, 1, 2, 3, 4, 5):
                    step(nc.vector.tensor_tensor(rs[:, 0], pm[:, i, 0:SEQ], pm[:, i, 1:], ALU.subtract))
                    step(nc.vector.scalar_tensor_tensor(out=pm[:, i, 1:], in0=rs[:, 0], scalar=cols["mu"][:, i:i + 1], in1=pm[:, i, 1:],
                                                        op0=ALU.mult, op1=ALU.add))
                nc.vector.tensor_scalar(ocol[:, :], cols["ka"][:, :], -1.0, 1.0, ALU.mult, ALU.add)
                for i in range(2):
                    step(nc.vector.tensor_scalar(At[:, i], p[:, 2 + i], cols["kk"][:, i:i + 1], None, ALU.mult))
                step(nc.vector.tensor_tensor(flat(bonus[:, :, :]), flat(At[:, :, :]), flat(At[:, :, :]), ALU.mult))

            @block.scalar
            def _(act):
                act.wait_ge(s["steps"], 2)
                nc.scalar.activation(p[0:32, 6], p[0:32, 6], ACT.Tanh)
                nc.scalar.activation(p[64:P, 6], p[64:P, 6], ACT.Sigmoid)
        jobs = []
        for i in range(2):
            c = slice(i * P, (i + 1) * P)
            jobs += [([(low[0:32, 0, c], p[0:32, 6])], slice(0, P), slice(0, SEQ), copy_to(nc, enL[:, i])),
                     ([(low[32:64, 1, c], p[32:64, 6])], slice(0, P), slice(0, SEQ), copy_to(nc, al[:, i])),
                     ([(low[64:P, 2, c], p[64:P, 6])], slice(0, P), slice(0, SEQ), copy_to(nc, gl[:, i])),
                     ([(C.ones64[:, :], bonus[:, i])], slice(0, P), slice(0, SEQ), copy_to(nc, rs[:, i]))]
        products(nc, C, "rw_low", jobs)
        with stage(nc, "rw_decay", "steps act") as (block, s):
            @block.scalar
            def _(act):
                step = Steps(act, s["act"])
                for i in range(2):
                    step(nc.scalar.activation(enL[:, i], enL[:, i], ACT.Sigmoid, bias=cols["w0"][:, i:i + 1]))
                for i in range(2):
                    step(nc.scalar.activation(al[:, i], al[:, i], ACT.Sigmoid, bias=cols["a0"][:, i:i + 1]))
                step(nc.scalar.activation(flat(rs[:, :, :]), flat(rs[:, :, :]), ACT.Sqrt))
                act.wait_ge(s["steps"], 4)
                step(nc.scalar.activation(flat(eLx[:, :, :]), flat(eLx[:, :, :]), ACT.Exp))
                step(nc.scalar.activation(flat(enL[:, :, :]), flat(eL[:, :, :]), ACT.Exp, scale=-1.0))
                step(nc.scalar.activation(flat(eL[:, :, :]), flat(eL[:, :, :]), ACT.Exp))

            @block.vector
            def _(dve):
                step = Steps(dve, s["steps"])
                dve.wait_ge(loaded, 32)
                dve.wait_ge(s["act"], 2)
                step(nc.vector.tensor_scalar(flat(enL[:, :, :]), flat(enL[:, :, :]), -math.exp(-0.5), None, ALU.mult))
                for i in range(2):
                    step(nc.vector.tensor_tensor_scan(eL[:, i], restart[:, :], enL[:, i], 0.0, ALU.mult, ALU.add))
                step(nc.vector.tensor_tensor(flat(eLx[:, :, :]), flat(eL[:, :, :]), flat(enL[:, :, :]), ALU.subtract))
                dve.wait_ge(s["act"], 5)
                step(nc.vector.tensor_scalar(flat(rs[:, :, :]), flat(rs[:, :, :]), 1e-12, None, ALU.max))
                step(nc.vector.reciprocal(flat(rs[:, :, :]), flat(rs[:, :, :])))
                step(nc.vector.tensor_tensor(flat(At[:, :, :]), flat(At[:, :, :]), flat(rs[:, :, :]), ALU.mult))
                step(nc.vector.tensor_tensor(flat(Bt[:, :, :]), flat(At[:, :, :]), flat(al[:, :, :]), ALU.mult))
                for i in range(2):
                    step(nc.vector.tensor_scalar(al[:, i], al[:, i], cols["ka"][:, i:i + 1], ocol[:, i:i + 1], ALU.mult, ALU.add))
                    step(nc.vector.tensor_tensor(al[:, i], al[:, i], p[:, 2 + i], ALU.mult))
                    step(nc.vector.scalar_tensor_tensor(out=bonus[:, i], in0=al[:, i], scalar=cols["rk"][:, i:i + 1], in1=p[:, i],
                                                        op0=ALU.mult, op1=ALU.mult))
                dve.wait_ge(s["act"], 8)
                step(nc.vector.scalar_tensor_tensor(out=flat(At[:, :, :]), in0=flat(At[:, :, :]), scalar=-1.0, in1=flat(eLx[:, :, :]),
                                                    op0=ALU.mult, op1=ALU.mult))
                step(nc.vector.tensor_tensor(flat(Bt[:, :, :]), flat(Bt[:, :, :]), flat(enL[:, :, :]), ALU.mult))
                step(nc.vector.tensor_tensor(flat(Kt[:, :, :]), flat(al[:, :, :]), flat(enL[:, :, :]), ALU.mult))
                for i in range(2):
                    step(nc.vector.tensor_tensor(Rt[:, i], p[:, i], eL[:, i], ALU.mult))
        products(nc, C, "rw_bonus", [([(C.ones64[:, :], bonus[:, i])], slice(0, P), slice(0, SEQ),
                                      lambda ps, steps, i=i: nc.vector.tensor_tensor(bonus[:, i], ps, p[:, 4 + i], ALU.mult)) for i in range(2)])

        with ExitStack() as m:
            MA, UA, MB, UB, Y, M1, M2, NTr = (sb(n, [P, NT, HH, P], m) for n in (
                "MA", "UA", "MB", "UB", "Y", "M1", "M2", "NT"))
            QB, QK = MB, UB
            tok = sb("tok", [P, NT, 3, HH, HD], m)
            free = xnT[:, :, :].rearrange("p a b -> p (a b)")
            AN = free[:, 0:2048].rearrange("p (t h c) -> p t h c", t=NT, h=HH)
            AZ = AN
            GF = free[:, 2048:4096].rearrange("p (c a b d) -> p c a b d", c=8, a=2, b=PR)
            ApT = al
            SA = eLx[:, :, :].rearrange("p a (b h d) -> p (a b) h d", h=HH, d=HD)
            AT = enL[:, :, :].rearrange("p a (b h d) -> p (a b) h d", h=HH, d=HD)
            S = sb("S", [P, 9, PR, HD], m)
            SF = sb("SF", [P, PR, HD], m)
            full = slice(0, P)

            def half(hp):
                return slice(hp * HD, (hp + 1) * HD)

            def bank_view(ps, w):
                return ps[:, :, 0:2 * w].rearrange("p a (b c) -> p a b c", b=2)

            def rows4(T, t):
                return T[:, t].rearrange("p (a b) c -> p a b c", a=2)

            def masked(ps, steps, t, *outs):
                for T, mk in outs:
                    for hp in range(2):
                        ins = nc.vector.tensor_tensor(T[:, t, 2 * hp:2 * hp + 2], ps[:, hp, 0:256].rearrange("p (b c) -> p b c", b=2),
                                                      bcast(masks[:, mk].unsqueeze(1), [P, 2, P]), ALU.mult)
                return ins

            def put(T, t):
                return lambda ps, steps: nc.vector.tensor_copy(rows4(T, t), bank_view(ps, P))

            jobs = []

            def gram(t, left, right, take, after=0):
                c = slice(t * P, (t + 1) * P)
                items = [(hp, slice(pr * P, (pr + 1) * P), full, left[half(hp), pr, c], right[half(hp), pr, c], True, True)
                         for hp in range(2) for pr in range(PR)]
                jobs.append((after, items, take))

            def mul(after, t, left, right, take, w=P):
                items = [(hp, slice(pr * w, (pr + 1) * w), full, left(2 * hp + pr), right(2 * hp + pr), True, True)
                         for hp in range(2) for pr in range(PR)]
                jobs.append((after, items, take))

            for t in range(NT):
                gram(t, At, Bt, lambda ps, st, t=t: masked(ps, st, t, (MA, 0), (M1, 2), (M2, 3)))
            for t in range(NT):
                def take_u(ps, st, t=t):
                    st(masked(ps, st, t, (UA, 1)))
                    return nc.vector.tensor_tensor(Y[:, t], UA[:, t], bcast(C.ident[:, :].unsqueeze(1), [P, HH, P]), ALU.add)
                gram(t, Bt, At, take_u)
            for t in range(NT):
                gram(t, Kt, At, lambda ps, st, t=t: masked(ps, st, t, (NTr, 4)))
            for t in range(NT):
                c = slice(t * P, (t + 1) * P)
                for qi, T in enumerate((At, Bt, Kt, None)):
                    src = lambda pr: (T[:, pr, c] if T is not None else p[:, 4 + pr, c])
                    items = [(0, slice(pr * P, (pr + 1) * P), full, src(pr), C.ident[:, :], "turn", True) for pr in range(PR)]

                    def take_tok(ps, st, t=t, qi=qi):
                        v = ps[:, 0, 0:256].rearrange("p (b a d) -> p a b d", b=2, a=2)
                        if qi == 0:
                            nc.vector.tensor_copy(rows4(AT, t), v)
                            return nc.vector.tensor_copy(rows4(AN, t)[:, :, :, 0:HD], v)
                        return nc.vector.tensor_copy(tok[:, t, qi - 1].rearrange("p (a b) d -> p a b d", a=2), v)
                    jobs.append((0, items, take_tok))

            def accumulate(t):
                return lambda ps, st: nc.vector.tensor_tensor(rows4(Y, t), rows4(Y, t), bank_view(ps, P), ALU.add)

            def level(make):
                done = len(jobs)
                for t in range(NT):
                    make(done, t)

            for (Mo, Uo), (Mn, Un), last in (((MA, UA), (MB, UB), False), ((MB, UB), (MA, UA), False), ((MA, UA), (MB, UB), True)):
                level(lambda d, t: mul(d, t, lambda h: Uo[:, t, h], lambda h: Mo[:, t, h], put(Mn, t)))
                if not last:
                    level(lambda d, t: mul(d - NT, t, lambda h: Mo[:, t, h], lambda h: Uo[:, t, h], put(Un, t)))
                level(lambda d, t: mul(d, t, lambda h: Mn[:, t, h], lambda h: Y[:, t, h], accumulate(t)))
            done = len(jobs)
            for t in range(NT):
                gram(t, Bt, Rt, lambda ps, st, t=t: masked(ps, st, t, (QB, 5)), done)
                gram(t, Kt, Rt, lambda ps, st, t=t: masked(ps, st, t, (QK, 5)), done)
            for Moff in (M1, M2):
                level(lambda d, t: jobs.append((d, [(h // 2, slice(h % 2 * P, (h % 2 + 1) * P), full, Y[:, t, h], C.ident[:, :], "turn", True)
                                                    for h in range(HH)], put(MA, t))))
                level(lambda d, t: mul(d - NT, t, lambda h: Moff[:, t, h], lambda h: Y[:, t, h], put(UA, t)))
                level(lambda d, t: mul(d, t, lambda h: MA[:, t, h], lambda h: UA[:, t, h], accumulate(t)))
            level(lambda d, t: mul(d, t, lambda h: NTr[:, t, h], lambda h: tok[:, t, 2, h],
                                   lambda ps, st: nc.vector.tensor_copy(rows4(AN, t)[:, :, :, HD:P], bank_view(ps, HD)), HD))
            level(lambda d, t: mul(d, t, lambda h: Y[:, t, h], lambda h: AN[:, t, h], put(AZ, t)))

            def apt(d, t):
                items = [(pr, slice(0, P), half(hp), AT[:, t, 2 * hp + pr], Y[:, t, 2 * hp + pr], True, True)
                         for pr in range(PR) for hp in range(2)]
                jobs.append((d - NT, items, lambda ps, st: nc.vector.tensor_copy(ApT[:, :, t * P:(t + 1) * P], ps[:, :, 0:P])))
            level(apt)
            done = len(jobs)
            for c in range(8):
                t, cr = c // 2, half(c % 2)
                items = []
                for hp in range(2):
                    for pr in range(PR):
                        h = 2 * hp + pr
                        items.append((c % 2, slice(pr * HD, (pr + 1) * HD), half(hp), AZ[cr, t, h, 0:HD], tok[cr, t, 0, h], True, True))
                        o = slice((2 + pr) * HD, (3 + pr) * HD)
                        items.append((c % 2, o, half(hp), tok[cr, t, 0, h], AZ[cr, t, h, HD:P], True, False))
                        items.append((c % 2, o, half(hp), tok[cr, t, 1, h], tok[cr, t, 2, h], False, True))
                jobs.append((done, items, lambda ps, st, c=c: nc.vector.tensor_copy(
                    GF[:, c].rearrange("p a b d -> p (a b d)"), ps[:, c % 2, 0:256])))
            paired(nc, C, "rw_chunks", jobs)

            with stage(nc, "rw_states", "made steps") as (block, s):
                PS = C.PS

                @block.tensor
                def _(pe):
                    for c in range(8):
                        pe.wait_ge(s["steps"], 1 + 3 * c)
                        for hp in range(2):
                            for pr in range(PR):
                                ins = nc.tensor.matmul(PS[half(hp), 2 * (c % 2) + hp, pr * HD:(pr + 1) * HD], GF[half(hp), c, 0, pr],
                                                       S[half(hp), c, pr], start=True, stop=True)
                        ins.then_inc(s["made"], 1)

                @block.vector
                def _(dve):
                    step = Steps(dve, s["steps"])
                    step(nc.vector.memset(S[:, 0], 0.0))
                    for c in range(8):
                        step(nc.vector.tensor_tensor(SF[:, :, :], S[:, c], GF[:, c, 1], ALU.add))
                        dve.wait_ge(s["made"], c + 1)
                        for hp in range(2):
                            ins = nc.vector.tensor_tensor(SF[half(hp)], SF[half(hp)], PS[half(hp), 2 * (c % 2) + hp, 0:P]
                                                          .rearrange("p (b d) -> p b d", b=2), ALU.add)
                        step(ins)
                        end = (c + 1) * CHUNK - 1
                        step(nc.vector.tensor_tensor(S[:, c + 1], SF[:, :, :], bcast(eL[:, :, end:end + 1], [P, PR, HD]), ALU.mult))

            jobs = []
            for t in range(NT):
                items = []
                for hp in range(2):
                    for pr in range(PR):
                        for c in (2 * t, 2 * t + 1):
                            items.append((hp, slice(pr * HD, (pr + 1) * HD), half(c % 2), ApT[half(hp), pr, c * CHUNK:(c + 1) * CHUNK],
                                          S[half(hp), c, pr], True, True))
                jobs.append((0, items, lambda ps, st, t=t: nc.vector.tensor_tensor(
                    rows4(SA, t), bank_view(ps, HD), rows4(AZ, t)[:, :, :, HD:P], ALU.add)))
            done = len(jobs)
            for t in range(NT):
                items = []
                for pr in range(PR):
                    for hp in range(2):
                        h = 2 * hp + pr
                        cs = slice(0, P)
                        items.append((pr, cs, half(hp), SA[:, t, h], QB[:, t, h], True, False))
                        items.append((pr, cs, half(hp), tok[:, t, 2, h], QK[:, t, h], False, False))
                        for c in (2 * t, 2 * t + 1):
                            items.append((pr, slice(c % 2 * CHUNK, (c % 2 + 1) * CHUNK), half(hp), S[half(hp), c, pr],
                                          Rt[half(hp), pr, c * CHUNK:(c + 1) * CHUNK], False, c % 2 == 1))
                jobs.append((done, items, lambda ps, st, t=t: nc.vector.tensor_copy(At[:, :, t * P:(t + 1) * P], ps[:, :, 0:P])))
            paired(nc, C, "rw_outputs", jobs)

        o = At
        products(nc, C, "rw_mean", [([(C.ones64[:, :], o[:, i])], slice(0, P), slice(0, SEQ), lambda ps, steps, i=i:
                                     nc.vector.scalar_tensor_tensor(out=Bt[:, i], in0=ps, scalar=-1.0 / HD, in1=o[:, i], op0=ALU.mult,
                                                                    op1=ALU.add)) for i in range(2)])
        norm_features(nc, C, "rw_gn", [dict(src=[Bt[:, i]], gain=[cols["rlg"][:, i:i + 1]], dst=[Bt[:, i]], ones=C.ones64[:, :], n=HD)
                                       for i in range(2)], eps=C.gn_eps)
        with stage(nc, "rw_end", "steps") as (block, s):
            @block.vector
            def _(dve):
                step = Steps(dve, s["steps"])
                for i in range(2):
                    step(nc.vector.scalar_tensor_tensor(out=Bt[:, i], in0=Bt[:, i], scalar=cols["rlb"][:, i:i + 1], in1=bonus[:, i],
                                                        op0=ALU.add, op1=ALU.add))
                    step(nc.vector.tensor_tensor(yT[:, 6 + i], Bt[:, i], gl[:, i], ALU.mult))


CONSTANTS = {"bucket_table": bucket_table, "rope_table": lambda: rope_tables()[0], "rope_turn": lambda: rope_tables()[1],
             "ones_row": lambda: np.ones((1, NH), np.float32), "wkv_masks": wkv_masks, "chunk_restart": chunk_restart}


def two_blocks(nc, D, out):
    stored = nc.alloc_semaphore("out_stored")
    with ExitStack() as mem:
        x = mem.enter_context(nc.sbuf_tensor("x", [P, NT, DM], F32))
        xnT = mem.enter_context(nc.sbuf_tensor("xnT", [P, KD, SEQ], F32))
        C = make_consts(nc, mem)
        mixer_even(nc, C, D, x, xnT)
        ffn(nc, C, D, x, xnT)
        mixer_odd(nc, C, D, x, xnT)
        moe_top2(nc, C, D, x, xnT)
        mixer_second(nc, C, D, x, xnT)
        moe_groups(nc, C, D, x, xnT)
        with nc.Block(name="store", no_gpsimd_drain=True) as block:
            @block.sync
            def _(sp):
                sp.dma_start(out[0].rearrange("(t p) d -> p t d", p=P), x[:, :, :]).then_inc(stored, 16)
                sp.wait_ge(stored, 16)


def kernel(**inputs):
    import concourse.bacc as bacc
    from concourse.bass_utils import run_bass_kernel_spmd

    nc = bacc.Bacc("TRN2", target_bir_lowering=False, num_devices=1)
    arrays, D = {}, {}
    for name, a in list(inputs.items()) + [(n, f()) for n, f in CONSTANTS.items()]:
        arrays[f"in_{name}"] = np.ascontiguousarray(a)
        D[name] = nc.dram_tensor(f"in_{name}", arrays[f"in_{name}"].shape, F32, kind="ExternalInput").ap()
    out = nc.dram_tensor("out_x", (1, SEQ, DM), F32, kind="ExternalOutput").ap()
    two_blocks(nc, D, out)
    result = run_bass_kernel_spmd(nc, [arrays], core_ids=[0])
    return result.results[0]["out_x"]
```

```python
import math
from contextlib import ExitStack, contextmanager

import numpy as np

import concourse.bass as bass
from concourse import mybir

F32 = mybir.dt.float32
ALU = mybir.AluOpType
ACT = mybir.ActivationFunctionType
AX = mybir.AxisListType

P = 128
SEQ, DM = 512, 1024
NT = SEQ // P
KD = DM // P
EPS = 1e-6
NEG = -1e30


@contextmanager
def stage(nc, name, sems):
    handles = {s: nc.alloc_semaphore(f"{name}_{s}") for s in sems.split()}
    with nc.Block(name=name, no_gpsimd_drain=True) as block:
        yield block, handles
    nc.clear_and_free_semaphores(list(handles.values()))
    nc.all_engine_barrier(sem_only=True)


class Steps:

    def __init__(self, eng, sem):
        self.eng, self.sem, self.n = eng, sem, 0

    def __call__(self, ins):
        self.n += 1
        ins.then_inc(self.sem, 1)
        self.eng.wait_ge(self.sem, self.n)


def bcast(ap, shape):
    return ap.to_broadcast(shape)


def norm_transpose(nc, C, x, gain, xnT, xs, name, loads=None, gain_loaded=None):
    with ExitStack() as mem, stage(nc, name, "squared_a squared_v mean root rstd scaled turned") as (block, s):
        ss = mem.enter_context(nc.sbuf_tensor(name + "_ss", [P, 4, NT], F32))
        PS = C.PS

        if loads is not None:
            @block.sync
            def _(sp):
                loads(sp)

        @block.scalar
        def _(act):
            for t in (0, 1):
                nc.scalar.activation(xs[:, t], x[:, t], ACT.Square, accum_out=ss[:, 0, t:t + 1]).then_inc(s["squared_a"], 1)
            act.wait_ge(s["mean"], 1)
            nc.scalar.activation(ss[:, 2], ss[:, 1], ACT.Sqrt).then_inc(s["root"], 1)
            act.wait_ge(s["rstd"], 1)
            for t in range(NT):
                nc.scalar.activation(xs[:, t], x[:, t], ACT.Copy, scale=ss[:, 3, t:t + 1]).then_inc(s["scaled"], 1)

        @block.vector
        def _(dve):
            for t in (2, 3):
                nc.vector.tensor_tensor_reduce(out=xs[:, t], in0=x[:, t], in1=x[:, t], scale=1.0, scalar=0.0, op0=ALU.mult,
                                               op1=ALU.add, accum_out=ss[:, 0, t:t + 1]).then_inc(s["squared_v"], 1)
            dve.wait_ge(s["squared_a"], 2)
            dve.wait_ge(s["squared_v"], 2)
            nc.vector.tensor_scalar(ss[:, 1], ss[:, 0], 1.0 / DM, EPS, ALU.mult, ALU.add).then_inc(s["mean"], 1)
            dve.wait_ge(s["root"], 1)
            nc.vector.reciprocal(ss[:, 3], ss[:, 2]).then_inc(s["rstd"], 1)
            if gain_loaded is not None:
                dve.wait_ge(*gain_loaded)
            for t in range(NT):
                dve.wait_ge(s["turned"], t + 1)
                for h in range(2):
                    g = bcast(gain[:, 4 * h:4 * h + 4].unsqueeze(2), [P, 4, P])
                    nc.vector.tensor_tensor(xnT[:, 4 * h:4 * h + 4, t * P:(t + 1) * P],
                                            PS[:, 2 * t + h].rearrange("p (k c) -> p k c", k=4), g, ALU.mult)

        @block.tensor
        def _(pe):
            for t in range(NT):
                pe.wait_ge(s["scaled"], t + 1)
                for k in range(KD):
                    ins = nc.tensor.transpose(PS[:, 2 * t + k // 4, (k % 4) * P:(k % 4 + 1) * P],
                                              xs[:, t].rearrange("p (m k) -> p k m", k=KD)[:, k], C.ident[:, :])
                ins.then_inc(s["turned"], 1)


def products(nc, C, name, jobs, ready=None, chained=False, loads=None):
    with stage(nc, name, "made taken steps") as (block, s):
        PS = C.PS

        if loads is not None:
            @block.sync
            def _(sp):
                loads(sp)

        @block.tensor
        def _(pe):
            for n, (pairs, rows, cols, take) in enumerate(jobs):
                if ready is not None:
                    for sem, value in ready(n):
                        pe.wait_ge(sem, value)
                if n >= 8:
                    pe.wait_ge(s["taken"], n - 7)
                for i, (lhsT, rhs) in enumerate(pairs):
                    ins = nc.tensor.matmul(PS[rows, n % 8, cols], lhsT, rhs, start=i == 0, stop=i == len(pairs) - 1)
                ins.then_inc(s["made"], 1)

        @block.vector
        def _(dve):
            steps = Steps(dve, s["steps"])
            for n, (pairs, rows, cols, take) in enumerate(jobs):
                dve.wait_ge(s["made"], n + 1)
                take(PS[rows, n % 8, cols], steps).then_inc(s["taken"], 1)
                if chained:
                    dve.wait_ge(s["taken"], n + 1)


def copy_to(nc, dst):
    return lambda ps, steps: nc.vector.tensor_copy(dst, ps)


def norm_features(nc, C, name, groups, eps=EPS):
    B = 4
    G = len(groups)
    batches = [range(a, min(a + B, G)) for a in range(0, G, B)]
    with ExitStack() as mem, stage(nc, name, "squared summed logged rstd steps normed") as (block, s):
        sq = mem.enter_context(nc.sbuf_tensor(name + "_sq", [P, 4, SEQ], F32))
        rs = mem.enter_context(nc.sbuf_tensor(name + "_rs", [P, 2 * B, SEQ], F32))
        tt = mem.enter_context(nc.sbuf_tensor(name + "_tt", [P, 2, SEQ], F32))
        ec = mem.enter_context(nc.sbuf_tensor(name + "_eps", [P, 1], F32))
        PS = C.PS
        first = [0]
        for g in groups:
            first.append(first[-1] + len(g["src"]))

        def part(ap):
            a = ap.start_partition() if callable(ap.start_partition) else ap.start_partition
            return slice(a, a + ap.shape[0]), ap.shape[1]

        @block.gpsimd
        def _(pool):
            nc.gpsimd.memset(ec[:, :], eps).then_inc(s["squared"], 1)
            for g, grp in enumerate(groups):
                for i, src in enumerate(grp["src"]):
                    m = first[g] + i
                    rows, n = part(src)
                    pool.wait_ge(s["squared"], m + 1)
                    if m >= 4:
                        pool.wait_ge(s["summed"], m - 3)
                    nc.gpsimd.tensor_tensor(sq[rows, m % 4, 0:n], src, src, ALU.mult).then_inc(s["squared"], 1)

        @block.scalar
        def _(act):
            act.wait_ge(s["squared"], 1)
            for batch in batches:
                for g in batch:
                    rows, n = part(groups[g]["src"][0])
                    act.wait_ge(s["summed"], first[g + 1])
                    if g >= 2 * B:
                        act.wait_ge(s["normed"], first[g - 2 * B + 1])
                    nc.scalar.activation(rs[rows, g % (2 * B), 0:n], PS[rows, g % 8, 0:n], ACT.Ln,
                                         bias=ec[rows, 0:1], scale=1.0 / groups[g]["n"]).then_inc(s["logged"], 1)
                for g in batch:
                    rows, n = part(groups[g]["src"][0])
                    act.wait_ge(s["logged"], g + 1)
                    nc.scalar.activation(rs[rows, g % (2 * B), 0:n], rs[rows, g % (2 * B), 0:n], ACT.Exp,
                                         scale=-0.5).then_inc(s["rstd"], 1)

        @block.tensor
        def _(pe):
            for g, grp in enumerate(groups):
                if g >= 8:
                    pe.wait_ge(s["normed"], first[g - 7])
                for i, src in enumerate(grp["src"]):
                    m = first[g] + i
                    rows, n = part(src)
                    pe.wait_ge(s["squared"], m + 2)
                    nc.tensor.matmul(PS[rows, g % 8, 0:n], grp["ones"], sq[rows, m % 4, 0:n],
                                     start=i == 0, stop=i == len(grp["src"]) - 1).then_inc(s["summed"], 1)

        @block.vector
        def _(dve):
            step = Steps(dve, s["steps"])

            def newton(gs, k):
                for g in gs:
                    rows, n = part(groups[g]["src"][0])
                    y, t, N = rs[rows, g % (2 * B), 0:n], tt[rows, g % 2, 0:n], groups[g]["n"]
                    if k == 0:
                        dve.wait_ge(s["rstd"], g + 1)
                        ins = nc.vector.scalar_tensor_tensor(out=t, in0=PS[rows, g % 8, 0:n], scalar=N * eps, in1=y, op0=ALU.add, op1=ALU.mult)
                    elif k == 1:
                        ins = nc.vector.scalar_tensor_tensor(out=t, in0=t, scalar=-0.5 / N, in1=y, op0=ALU.mult, op1=ALU.mult)
                    else:
                        ins = nc.vector.scalar_tensor_tensor(out=y, in0=t, scalar=1.5, in1=y, op0=ALU.add, op1=ALU.mult)
                    ins.then_inc(s["steps"], 1)
                    step.n += 1
                dve.wait_ge(s["steps"], step.n)

            for a in range(0, G, 2):
                gs = range(a, min(a + 2, G))
                for k in range(3):
                    newton(gs, k)
                for g in gs:
                    rows, n = part(groups[g]["src"][0])
                    for src, gain, dst in zip(groups[g]["src"], groups[g]["gain"], groups[g]["dst"]):
                        nc.vector.scalar_tensor_tensor(out=dst, in0=src, scalar=gain, in1=rs[rows, g % (2 * B), 0:n],
                                                       op0=ALU.mult, op1=ALU.mult).then_inc(s["normed"], 1)
                dve.wait_ge(s["normed"], first[gs[-1] + 1])


def attention(nc, C, name, jobs):
    U = NT * len(jobs)
    LAG = 3
    pairs = len(jobs) // 2
    with ExitStack() as mem, stage(
            nc, name, "scored biased maxed exped inv coef scaled turned placed valued stored") as (block, s):
        pr = mem.enter_context(nc.sbuf_tensor(name + "_p", [P, 3, SEQ], F32))
        pn = mem.enter_context(nc.sbuf_tensor(name + "_pn", [P, 3, SEQ], F32))
        pT = mem.enter_context(nc.sbuf_tensor(name + "_pT", [P, 4, NT, SEQ], F32))
        st = mem.enter_context(nc.sbuf_tensor(name + "_st", [P, 4, 8], F32))
        PS = C.PS
        stores = [0]
        for m in range(pairs):
            stores.append(stores[-1] + (1 if jobs[2 * m]["stop"] else 0))

        @block.tensor
        def _(pe):
            def scores(u):
                job, i = jobs[u // NT], u % NT
                if u >= 3:
                    pe.wait_ge(s["exped"], u - 2)
                q, k = job["q"], job["k"]
                ins = nc.tensor.matmul(PS[:, u % 3, 0:(i + 1) * P], q[:, i * P:(i + 1) * P], k[:, 0:(i + 1) * P],
                                       start=True, stop=job["extra"] is None)
                if job["extra"] is not None:
                    ins = nc.tensor.matmul(PS[:, u % 3, 0:(i + 1) * P], job["extra"][0], job["extra"][1][:, 0:(i + 1) * P],
                                           start=False, stop=True)
                ins.then_inc(s["scored"], 1)

            def turn(u):
                i = u % NT
                pe.wait_ge(s["scaled"], u + 1)
                if u >= 2:
                    pe.wait_ge(s["placed"], u - 1)
                for kb in range(i + 1):
                    ins = nc.tensor.transpose(PS[:, 3 + u % 2, kb * P:(kb + 1) * P], pn[:, u % 3, kb * P:(kb + 1) * P],
                                              C.ident[:, :])
                ins.then_inc(s["turned"], 1)

            def values(m):
                both = jobs[2 * m], jobs[2 * m + 1]
                pe.wait_ge(s["placed"], NT * (2 * m + 2))
                bank, start, stop = 5 + both[0]["bank"], both[0]["start"], both[0]["stop"]
                if start and stores[m] >= 2:
                    pe.wait_ge(s["stored"], stores[m] - 1)
                if both[0]["first"] is not None:
                    for job in both:
                        nc.tensor.matmul(PS[job["rows"], bank, :], job["first"][0], job["first"][1], start=True, stop=False)
                for kb in range(NT):
                    for n, job in enumerate(both):
                        ins = nc.tensor.matmul(PS[job["rows"], bank, kb * P:SEQ], job["v"](kb), pT[:, (2 * m + n) % 4, kb, kb * P:SEQ],
                                               start=kb == 0 and start and job["first"] is None, stop=kb == NT - 1 and stop)
                        if kb == NT - 1:
                            ins.then_inc(s["valued"], 1)

            for u in range(U + LAG + 1):
                if u < U:
                    scores(u)
                if 0 <= u - LAG < U:
                    turn(u - LAG)
                v = u - LAG - 1
                if v >= 0 and v % (2 * NT) == 2 * NT - 1:
                    values(v // (2 * NT))

        @block.scalar
        def _(act):
            def exps(u):
                i = u % NT
                act.wait_ge(s["maxed"], u + 1)
                if u >= 3:
                    act.wait_ge(s["scaled"], u - 2)
                nc.scalar.activation(pr[:, u % 3, 0:(i + 1) * P], PS[:, u % 3, 0:(i + 1) * P], ACT.Exp,
                                     bias=st[:, 0, u % 8:u % 8 + 1], accum_out=st[:, 1, u % 8:u % 8 + 1]).then_inc(s["exped"], 1)

            def scale(u):
                i = u % NT
                act.wait_ge(s["coef"], u + 1)
                if u >= 3:
                    act.wait_ge(s["turned"], u - 2)
                nc.scalar.activation(pn[:, u % 3, 0:(i + 1) * P], pr[:, u % 3, 0:(i + 1) * P], ACT.Copy,
                                     scale=st[:, 3, u % 8:u % 8 + 1]).then_inc(s["scaled"], 1)

            def place(u):
                if u % 4 != 1:
                    return
                j, i = u // NT, u % NT
                act.wait_ge(s["turned"], u + 1)
                act.wait_ge(s["placed"], u)
                if j >= 4:
                    act.wait_ge(s["valued"], (j // 2 - 1) * 2)
                nc.scalar.activation(pT[:, j % 4, 0:i + 1, i * P:(i + 1) * P],
                                     PS[:, 3 + u % 2, 0:(i + 1) * P].rearrange("p (k c) -> p k c", c=P), ACT.Copy).then_inc(s["placed"], 1)

            for u in range(U + LAG + 1):
                if u < U:
                    exps(u)
                if 0 <= u - 1 < U:
                    scale(u - 1)
                if 0 <= u - LAG < U:
                    place(u - LAG)

        @block.vector
        def _(dve):
            def biased(u):
                job, i = jobs[u // NT], u % NT
                wb = job["bias"].shape[1]
                w = min(wb, (i + 1) * P)
                dve.wait_ge(s["scored"], u + 1)
                cols = slice((i + 1) * P - w, (i + 1) * P)
                nc.vector.tensor_tensor(PS[:, u % 3, cols], PS[:, u % 3, cols], job["bias"][:, wb - w:wb],
                                        ALU.add).then_inc(s["biased"], 1)

            def maxed(u):
                i = u % NT
                dve.wait_ge(s["biased"], u + 1)
                nc.vector.tensor_reduce(st[:, 0, u % 8:u % 8 + 1], PS[:, u % 3, 0:(i + 1) * P], AX.X, ALU.max,
                                        negate=True).then_inc(s["maxed"], 1)

            def coef(u):
                job, i = jobs[u // NT], u % NT
                dve.wait_ge(s["exped"], u + 1)
                nc.vector.reciprocal(st[:, 2, u % 8:u % 8 + 1], st[:, 1, u % 8:u % 8 + 1]).then_inc(s["inv"], 1)
                dve.wait_ge(s["inv"], u + 1)
                gate = C.one[:, 0:1] if job["gate"] is None else job["gate"](i)
                nc.vector.tensor_tensor(st[:, 3, u % 8:u % 8 + 1], st[:, 2, u % 8:u % 8 + 1], gate,
                                        ALU.mult).then_inc(s["coef"], 1)

            def place(u):
                if u % 4 == 1:
                    return
                j, i = u // NT, u % NT
                dve.wait_ge(s["turned"], u + 1)
                if u >= 1:
                    dve.wait_ge(s["placed"], u)
                if j >= 4:
                    dve.wait_ge(s["valued"], (j // 2 - 1) * 2)
                nc.vector.tensor_copy(pT[:, j % 4, 0:i + 1, i * P:(i + 1) * P],
                                      PS[:, 3 + u % 2, 0:(i + 1) * P].rearrange("p (k c) -> p k c", c=P)).then_inc(s["placed"], 1)

            def store(m):
                if jobs[2 * m]["stop"]:
                    dve.wait_ge(s["valued"], 2 * m + 2)
                    nc.vector.tensor_copy(jobs[2 * m]["out"], PS[:, 5 + jobs[2 * m]["bank"], :]).then_inc(s["stored"], 1)

            done = 0
            for u in range(U + LAG + 3):
                if u < U:
                    biased(u)
                if 0 <= u - 1 < U:
                    coef(u - 1)
                if u < U:
                    maxed(u)
                if 0 <= u - LAG < U:
                    place(u - LAG)
                v = u - LAG - 2
                if v >= 0 and v % (2 * NT) == 2 * NT - 1:
                    store(v // (2 * NT))
                    done += 1
            assert done == pairs


def add_projection(nc, C, name, yT, w, x, loaded):
    def take(t, h):
        def f(ps, steps):
            dst = x[:, t, h * 512:(h + 1) * 512]
            return nc.vector.tensor_tensor(dst, ps, dst, ALU.add)
        return f

    jobs = [([(yT[:, k, t * P:(t + 1) * P], w[:, k, h * 512:(h + 1) * 512]) for k in range(KD)],
             slice(0, P), slice(0, 512), take(t, h)) for t in range(NT) for h in range(2)]
    products(nc, C, name, jobs, lambda n: [loaded] if n == 0 else [])


def gated_parts(nc, C, name, xnT, x, parts, F, wg, wu, wd, weight):
    NF = F // P
    RING = min(5, NF)
    last_user = {}
    for c in range(NF):
        last_user[c % RING] = c
    uses = [len(range(r, NF, RING)) for r in range(RING)]
    sems = "up_free down_loaded made silu hidden y_made y_taken " + " ".join(f"up{r}" for r in range(RING))
    with ExitStack() as mem, stage(nc, name, sems) as (block, s):
        up = mem.enter_context(nc.sbuf_tensor(name + "_up", [P, RING, 2, KD, P], F32))
        down = mem.enter_context(nc.sbuf_tensor(name + "_down", [P, NF, DM], F32))
        sg = mem.enter_context(nc.sbuf_tensor(name + "_sg", [P, 2, SEQ], F32))
        hT = mem.enter_context(nc.sbuf_tensor(name + "_hT", [P, NF, SEQ], F32))
        PS = C.PS

        @block.sync
        def _(sp):
            with sp.Fori(0, parts) as e:
                for c in range(NF):
                    r = c % RING
                    before = c - RING + NF if c >= RING else last_user[r]
                    sp.wait_ge(s["up_free"], e * NF + before + 1)
                    sp.dma_start(up[:, r, 0], wg(e)[:, :, c * P:(c + 1) * P]).then_inc(s[f"up{r}"], 16)
                    sp.dma_start(up[:, r, 1], wu(e)[:, :, c * P:(c + 1) * P]).then_inc(s[f"up{r}"], 16)
                    if c == RING - 1:
                        sp.wait_ge(s["y_made"], e * 8 + 8)
                        sp.dma_start(down[:, :, :], wd(e)).then_inc(s["down_loaded"], 16)

        @block.tensor
        def _(pe):
            pe.sem_inc(s["up_free"], NF)
            pe.sem_inc(s["y_made"], 8)
            with pe.Fori(0, parts) as e:
                for c in range(NF):
                    r = c % RING
                    pe.wait_ge(s[f"up{r}"], (e * uses[r] + c // RING + 1) * 32)
                    pe.wait_ge(s["hidden"], e * NF + c + 1)
                    for m in range(2):
                        for k in range(KD):
                            ins = nc.tensor.matmul(PS[:, 2 * m + c % 2, :], up[:, r, m, k], xnT[:, k], start=k == 0,
                                                   stop=k == KD - 1)
                        ins.then_inc(s["made"] if m == 0 else s["up_free"], 1)
                pe.wait_ge(s["hidden"], e * NF + NF + 2)
                pe.wait_ge(s["down_loaded"], (e + 1) * 16)
                for t in range(NT):
                    for h in range(2):
                        b = 4 + (2 * t + h) % 4
                        pe.wait_ge(s["y_taken"], e * 8 + 2 * t + h + 1)
                        for c in range(NF):
                            ins = nc.tensor.matmul(PS[:, b, :], hT[:, c, t * P:(t + 1) * P],
                                                   down[:, c, h * 512:(h + 1) * 512], start=c == 0, stop=c == NF - 1)
                        ins.then_inc(s["y_made"], 1)

        @block.scalar
        def _(act):
            with act.Fori(0, parts) as e:
                for c in range(NF):
                    act.wait_ge(s["made"], e * NF + c + 1)
                    act.wait_ge(s["hidden"], e * NF + c + 1)
                    nc.scalar.activation(sg[:, c % 2], PS[:, c % 2, :], ACT.Silu).then_inc(s["silu"], 1)

        @block.vector
        def _(dve):
            dve.sem_inc(s["hidden"], 2)
            dve.sem_inc(s["y_taken"], 4)
            with dve.Fori(0, parts) as e:
                for c in range(NF):
                    dve.wait_ge(s["silu"], e * NF + c + 1)
                    dve.wait_ge(s["up_free"], NF + e * NF + c + 1)
                    nc.vector.tensor_tensor(hT[:, c], sg[:, c % 2], PS[:, 2 + c % 2, :], ALU.mult).then_inc(s["hidden"], 1)
                for t in range(NT):
                    for h in range(2):
                        dve.wait_ge(s["y_made"], e * 8 + 2 * t + h + 9)
                        dst = x[:, t, h * 512:(h + 1) * 512]
                        nc.vector.scalar_tensor_tensor(out=dst, in0=PS[:, 4 + (2 * t + h) % 4, :], scalar=weight(t, e),
                                                       in1=dst, op0=ALU.mult, op1=ALU.add).then_inc(s["y_taken"], 1)


I32 = mybir.dt.int32
FAR = 4096.0


def plan_passes(nc, C, name, mem, mask, NE):
    Q = 8 * NT * 2 // 4 if NE == 4 else 2 * NE
    def sb(n, shape, m=mem, dt=F32):
        return m.enter_context(nc.sbuf_tensor(name + n, shape, dt))

    rank, table, slots = sb("_rank", [P, NT, 4 * NE]), sb("_table", [P, 2 * Q + 1], dt=I32), sb("_slots", [P, P])
    with ExitStack() as m2, stage(nc, name, "zeroed counted steps") as (block, s):
        before = sb("_before", [P, P], m2)
        cnt, t, le, qi = sb("_cnt", [P, NE], m2), sb("_t", [P, 4, NE], m2), sb("_le", [P, Q, NE], m2), sb("_qi", [P, Q], m2)
        tf = sb("_tf", [P, 3, Q], m2)
        PS = C.PS

        @block.gpsimd
        def _(pool):
            step = Steps(pool, s["zeroed"])
            step(nc.gpsimd.memset(before[:, :], 1.0))
            step(nc.gpsimd.affine_select(out=before[:, :], in_=before[:, :], compare_op=ALU.is_gt, fill=0.0, base=0,
                                         pattern=[[1, P]], channel_multiplier=-1))
            step(nc.gpsimd.iota(slots[:, :], pattern=[[1, P]], base=0, channel_multiplier=0, allow_small_or_imprecise_dtypes=True))
            step(nc.gpsimd.iota(qi[:, :], pattern=[[1, Q]], base=0, channel_multiplier=0, allow_small_or_imprecise_dtypes=True))

        @block.tensor
        def _(pe):
            pe.wait_ge(s["zeroed"], 4)
            for i in range(NT + 1):
                for j in range(i):
                    nc.tensor.matmul(PS[:, i, 0:NE], C.ones[:, :], mask[:, j], start=j == 0, stop=i == NT and j == NT - 1) \
                        .then_inc(s["counted"], 1)
                if i < NT:
                    nc.tensor.matmul(PS[:, i, 0:NE], before[:, :], mask[:, i], start=i == 0, stop=True).then_inc(s["counted"], 1)

        @block.vector
        def _(dve):
            step = Steps(dve, s["steps"])
            dve.wait_ge(s["zeroed"], 4)
            dve.wait_ge(s["counted"], 2 * NT + NT * (NT - 1) // 2)
            for i in range(NT):
                r0 = rank[:, i, 0:NE]
                step(nc.vector.tensor_scalar(r0, mask[:, i], -FAR, FAR, ALU.mult, ALU.add))
                step(nc.vector.tensor_tensor(r0, r0, PS[:, i, 0:NE], ALU.add))
                for b in range(1, 4):
                    step(nc.vector.tensor_scalar(rank[:, i, b * NE:(b + 1) * NE], r0, -128.0 * b, None, ALU.add))
            step(nc.vector.tensor_copy(cnt[:, :], PS[:, NT, 0:NE]))
            step(nc.vector.tensor_scalar(t[:, 0], cnt[:, :], 0.0, None, ALU.is_gt))
            for b in range(1, 4):
                step(nc.vector.scalar_tensor_tensor(out=t[:, 0], in0=cnt[:, :], scalar=128.0 * b, in1=t[:, 0], op0=ALU.is_gt, op1=ALU.add))
            step(nc.vector.memset(t[:, 2], 1.0))
            step(nc.vector.tensor_tensor_scan(t[:, 1], t[:, 2], t[:, 0], 0.0, ALU.mult, ALU.add))
            full = [P, Q, NE]
            step(nc.vector.tensor_tensor(le[:, :, :], bcast(t[:, 1].unsqueeze(1), full), bcast(qi[:, :].unsqueeze(2), full), ALU.is_le))
            step(nc.vector.tensor_reduce(tf[:, 0], le[:, :, :], AX.X, ALU.add))
            step(nc.vector.tensor_tensor(le[:, :, :], le[:, :, :], bcast(t[:, 0].unsqueeze(1), full), ALU.mult))
            step(nc.vector.tensor_reduce(tf[:, 1], le[:, :, :], AX.X, ALU.add))
            step(nc.vector.tensor_scalar(tf[:, 0], tf[:, 0], NE - 1.0, None, ALU.min))
            step(nc.vector.tensor_tensor(tf[:, 1], qi[:, :], tf[:, 1], ALU.subtract))
            step(nc.vector.tensor_scalar(tf[:, 1], tf[:, 1], 3.0, None, ALU.min))
            step(nc.vector.scalar_tensor_tensor(out=tf[:, 2], in0=tf[:, 1], scalar=float(NE), in1=tf[:, 0], op0=ALU.mult, op1=ALU.add))
            nc.vector.tensor_copy(table[:, 0:Q], tf[:, 0])
            nc.vector.tensor_copy(table[:, Q:2 * Q], tf[:, 2])
            nc.vector.tensor_copy(table[:, 2 * Q:2 * Q + 1], t[:, 1, NE - 1:NE])
    return rank, table, slots, Q


def routed_passes(nc, C, name, x, xs, xnT, gain, plan, NE, F, wg, wu, wd, weights, NW):
    rank, table, slots, Q = plan
    NF = F // P
    chunks = [(f, min(512, F - f)) for f in range(0, F, 512)]
    NC = len(chunks)
    part = F // NW
    pieces = [[(max(f, j * part), min(f + n, (j + 1) * part), j) for j in range(NW) if max(f, j * part) < min(f + n, (j + 1) * part)]
              for f, n in chunks]
    ybank = (2, 3, 1)
    sems = ("sel gathered xg pt_made pt g_made u_made silu hid turned hT_done o_made o_taken y_made y_taken down "
            + " ".join(f"up{c}" for c in range(NC)))
    with ExitStack() as mem, stage(nc, name, sems) as (block, s):
        def sb(n, shape):
            return mem.enter_context(nc.sbuf_tensor(name + n, shape, F32))

        up = [sb(f"_up{c}", [P, 2, KD, n]) for c, (f, n) in enumerate(chunks)]
        down, hT, O, sel = sb("_down", [P, NF, DM]), sb("_hT", [P, NF, P]), sb("_O", [P, DM]), sb("_sel", [P, NT, P])
        cw = sb("_cw", [P, NW])
        free = xnT[:, :, :].rearrange("p a b -> p (a b)")
        sg, h = (free[:, a:a + 1024].rearrange("p (c f) -> p c f", c=2) for a in (0, 1024))
        xg = free[:, 2048:3072].rearrange("p (k s) -> p k s", k=KD)
        selT = free[:, 3072:3584]
        PS = C.PS

        def passes(eng):
            return eng.value_load(table[0:1, 2 * Q:2 * Q + 1], min_val=1, max_val=Q - 1)

        def expert(eng, q):
            return eng.value_load(table[0:1, bass.ds(q, 1)], min_val=0, max_val=NE - 1)

        @block.sync
        def _(sp):
            n = passes(sp)
            with sp.Fori(0, n) as q:
                e = expert(sp, q)
                for c in range(NC):
                    sp.wait_ge(s["u_made"], q * NC + c + 1)
                    sp.dma_start(up[c][:, 0], wg(e, c)).then_inc(s[f"up{c}"], 16)
                    sp.dma_start(up[c][:, 1], wu(e, c)).then_inc(s[f"up{c}"], 16)
                sp.wait_ge(s["o_made"], q * 2 + 2)
                sp.dma_start(down[:, :, :], wd(e)).then_inc(s["down"], 16)

        @block.tensor
        def _(pe):
            def gather(q):
                pe.wait_ge(s["sel"], q + 1)
                e = expert(pe, q) if NW == 1 else 0
                for t in range(NT):
                    nc.tensor.matmul(PS[:, 1, 0:NW], sel[:, t], weights(t, e), start=t == 0, stop=t == NT - 1)
                for k in range(KD):
                    for t in range(NT):
                        ins = nc.tensor.matmul(PS[:, 4 + k // 4, k % 4 * P:(k % 4 + 1) * P],
                                               xs[:, t].rearrange("p (m k) -> p k m", k=KD)[:, k], sel[:, t],
                                               start=t == 0, stop=t == NT - 1)
                ins.then_inc(s["gathered"], 1)

            def turn_sel():
                for t in range(NT):
                    ins = nc.tensor.transpose(PS[:, 6, t * P:(t + 1) * P], sel[:, t], C.ident[:, :])
                ins.then_inc(s["pt_made"], 1)

            pe.sem_inc(s["u_made"], NC)
            pe.sem_inc(s["o_made"], 2)
            n = passes(pe)
            gather(0)
            turn_sel()
            with pe.Fori(0, n) as q:
                def turn(c):
                    f, width = chunks[c]
                    pe.wait_ge(s["hid"], q * NC + c + 1)
                    if c >= 2:
                        pe.wait_ge(s["hT_done"], q * NC + c - 1)
                    for i in range(width // P):
                        ins = nc.tensor.transpose(PS[:, 4 + c % 2, i * P:(i + 1) * P], h[:, c % 2, i * P:(i + 1) * P], C.ident[:, :])
                    ins.then_inc(s["turned"], 1)

                pe.wait_ge(s["xg"], q + 1)
                pe.wait_ge(s["y_taken"], q * 8 + 8)
                for c, (f, width) in enumerate(chunks):
                    pe.wait_ge(s[f"up{c}"], q * 32 + 32)
                    if c >= 2:
                        pe.wait_ge(s["hid"], q * NC + c - 1)
                    for m, made in ((0, "g_made"), (1, "u_made")):
                        for k in range(KD):
                            ins = nc.tensor.matmul(PS[:, 2 * m + c % 2, 0:width], xg[:, k], up[c][:, m, k], start=k == 0, stop=k == KD - 1)
                        ins.then_inc(s[made], 1)
                    if c >= 1:
                        turn(c - 1)
                turn(NC - 1)
                pe.wait_ge(s["down"], q * 16 + 16)
                pe.wait_ge(s["pt"], q + 1)
                for c, (f, width) in enumerate(chunks):
                    pe.wait_ge(s["hT_done"], q * NC + c + 1)
                    for i in range(f // P, (f + width) // P):
                        for half in range(2):
                            ins = nc.tensor.matmul(PS[:, 6 + half, :], hT[:, i], down[:, i, half * 512:(half + 1) * 512],
                                                   start=i == 0, stop=i == NF - 1)
                            if i == NF - 1:
                                ins.then_inc(s["o_made"], 1)
                gather(q + 1)
                pe.wait_ge(s["o_taken"], q * 2 + 2)
                for i in range(8):
                    t, half = i // 2, i % 2
                    if i == 2:
                        pe.wait_ge(s["xg"], q + 2)
                    if i >= 3:
                        pe.wait_ge(s["y_taken"], q * 8 + i + 6)
                    nc.tensor.matmul(PS[:, ybank[i % 3], :], selT[:, t * P:(t + 1) * P], O[:, half * 512:(half + 1) * 512],
                                     start=True, stop=True).then_inc(s["y_made"], 1)
                turn_sel()

        @block.scalar
        def _(act):
            n = passes(act)
            with act.Fori(0, n) as q:
                act.wait_ge(s["pt_made"], q + 1)
                nc.scalar.activation(selT, PS[:, 6, :], ACT.Copy).then_inc(s["pt"], 1)

                def place(c):
                    f, width = chunks[c]
                    act.wait_ge(s["turned"], q * NC + c + 1)
                    nc.scalar.activation(hT[:, f // P:(f + width) // P].rearrange("p a b -> p (a b)"), PS[:, 4 + c % 2, 0:width],
                                         ACT.Copy).then_inc(s["hT_done"], 1)

                for c, (f, width) in enumerate(chunks):
                    act.wait_ge(s["g_made"], q * NC + c + 1)
                    if c >= 2:
                        act.wait_ge(s["hid"], q * NC + c - 1)
                    nc.scalar.activation(sg[:, c % 2, 0:width], PS[:, c % 2, 0:width], ACT.Silu).then_inc(s["silu"], 1)
                    if c >= 1:
                        place(c - 1)
                place(NC - 1)
                for half in range(2):
                    act.wait_ge(s["o_made"], q * 2 + half + 3)
                    nc.scalar.activation(O[:, half * 512:(half + 1) * 512], PS[:, 6 + half, :], ACT.Copy).then_inc(s["o_taken"], 1)

        @block.vector
        def _(dve):
            def select(q):
                at = dve.value_load(table[0:1, bass.ds(q + Q, 1)], min_val=0, max_val=4 * NE - 1)
                for t in range(NT):
                    ins = nc.vector.tensor_scalar(sel[:, t], slots[:, :], rank[:, t, bass.ds(at, 1)], None, ALU.is_equal)
                ins.then_inc(s["sel"], 1)

            def place(q):
                dve.wait_ge(s["gathered"], q + 1)
                nc.vector.tensor_copy(cw[:, :], PS[:, 1, 0:NW])
                for i in range(2):
                    ins = nc.vector.tensor_tensor(xg[:, 4 * i:4 * i + 4], PS[:, 4 + i, :].rearrange("p (k c) -> p k c", k=4),
                                                  bcast(gain[:, 4 * i:4 * i + 4].unsqueeze(2), [P, 4, P]), ALU.mult)
                ins.then_inc(s["xg"], 1)

            dve.sem_inc(s["y_taken"], 8)
            n = passes(dve)
            select(0)
            place(0)
            with dve.Fori(0, n) as q:
                dve.wait_ge(s["xg"], q + 1)
                for c in range(NC):
                    dve.wait_ge(s["silu"], q * NC + c + 1)
                    dve.wait_ge(s["u_made"], q * NC + c + 1 + NC)
                    if c >= 2:
                        dve.wait_ge(s["turned"], q * NC + c - 1)
                    for a, b, j in pieces[c]:
                        w = slice(a - chunks[c][0], b - chunks[c][0])
                        ins = nc.vector.scalar_tensor_tensor(out=h[:, c % 2, w], in0=sg[:, c % 2, w], scalar=cw[:, j:j + 1],
                                                             in1=PS[:, 2 + c % 2, w], op0=ALU.mult, op1=ALU.mult)
                    ins.then_inc(s["hid"], 1)
                dve.wait_ge(s["pt_made"], q + 1)
                select(q + 1)
                place(q + 1)
                for i in range(8):
                    t, half = i // 2, i % 2
                    dve.wait_ge(s["y_made"], q * 8 + i + 1)
                    dst = x[:, t, half * 512:(half + 1) * 512]
                    nc.vector.tensor_tensor(dst, PS[:, ybank[i % 3], :], dst, ALU.add).then_inc(s["y_taken"], 1)


class Consts:
    pass


def make_consts(nc, mem):
    C = Consts()
    C.PS = mem.enter_context(nc.psum_tensor("PS", [P, 8, 512], F32))
    C.ident = mem.enter_context(nc.sbuf_tensor("ident", [P, P], F32))
    C.ones = mem.enter_context(nc.sbuf_tensor("ones", [P, P], F32))
    C.ones64 = mem.enter_context(nc.sbuf_tensor("ones64", [P, P], F32))
    C.causal = mem.enter_context(nc.sbuf_tensor("causal", [P, P], F32))
    C.one = mem.enter_context(nc.sbuf_tensor("one", [P, 1], F32))
    with stage(nc, "consts", "zeroed") as (block, s):
        @block.gpsimd
        def _(pool):
            step = Steps(pool, s["zeroed"])
            for tile, value in ((C.ones, 1.0), (C.one, 1.0), (C.ident, 0.0), (C.causal, 0.0), (C.ones64, 0.0)):
                step(nc.gpsimd.memset(tile[:, :], value))
            for a in (0, 64):
                step(nc.gpsimd.memset(C.ones64[a:a + 64, a:a + 64], 1.0))
            step(nc.gpsimd.affine_select(out=C.ident[:, :], in_=C.ident[:, :], compare_op=ALU.not_equal, fill=1.0,
                                         base=0, pattern=[[-1, P]], channel_multiplier=1))
            step(nc.gpsimd.affine_select(out=C.causal[:, :], in_=C.causal[:, :], compare_op=ALU.is_ge, fill=NEG,
                                         base=0, pattern=[[-1, P]], channel_multiplier=1))
    return C


def column(ap):
    return ap.rearrange("(p o) -> p o", o=1)


Q0, KC0, VC0, KS0, VS0, KW0, VW0, GT0, CQ0, CKV0, KR0, EV_W = (
    0, 512, 640, 768, 896, 1024, 1152, 1280, 1304, 1560, 1688, 1720)
NH, HD = 8, 64
CMP_L, CMP_S = 32, 16
NCMP = (SEQ - CMP_L) // CMP_S + 1
MQK, ROT = 96, 32
BUCKETS = 32
REV_ZERO, FWD_ZERO = 2 * P - 1, 527


def bucket_table():
    n = np.arange(SEQ)
    large = 16 + (np.log(np.maximum(n, 16).astype(np.float32) / np.float32(16)) / np.float32(math.log(8.0))
                  * np.float32(16)).astype(np.int32)
    bucket = np.where(n < 16, n, np.minimum(large, BUCKETS - 1))
    d = np.concatenate([REV_ZERO - np.arange(SEQ), np.arange(2 * SEQ) - FWD_ZERO])
    seen = (d >= 0) & (d < SEQ)
    table = np.zeros((BUCKETS + 1, d.size), np.float32)
    table[bucket[d[seen]], np.nonzero(seen)[0]] += 1.0
    table[BUCKETS - 1, seen] -= 1.0
    table[BUCKETS, d < 0] = NEG
    return table


def rope_tables():
    half = ROT // 2
    inv = (np.float32(10000.0) ** (-np.arange(half, dtype=np.float32) / np.float32(half))).astype(np.float32)
    ang = np.arange(SEQ, dtype=np.float32)[None, :] * inv[:, None]
    turn = np.zeros((ROT, ROT), np.float32)
    for m in range(half):
        turn[m + half, m] = -1.0
        turn[m, m + half] = 1.0
    return np.stack([np.tile(np.cos(ang), (2, 1)), np.tile(np.sin(ang), (2, 1))]).astype(np.float32), turn


def mixer_even(nc, C, D, x, xnT):
    with ExitStack() as mem:
        def sb(name, shape, m=mem):
            return m.enter_context(nc.sbuf_tensor("ev_" + name, shape, F32))

        yT = sb("yT", [P, 8, SEQ])
        q = sb("q", [P, 4, SEQ])
        ks, kw = sb("ks", [P, SEQ]), sb("kw", [P, SEQ])
        vsw = sb("vsw", [P, NT, 2, P])
        gate = sb("gate", [P, NT, 3 * NH])
        cq6 = sb("latent", [P, 4, SEQ])
        cq, ckv, kr = cq6[:, 0:2], cq6[:, 2], cq6[:, 3]
        uq, ukv = sb("uq", [P, 2, NH * MQK]), sb("ukv", [P, NH * P])
        vblk = sb("vblk", [P, 2, 4, HD])
        pcT = sb("pcT", [P, 2, SEQ])
        T = sb("T", [P, NH, 2 * P])
        TcT = sb("TcT", [P, 2, SEQ])
        relb = sb("relb", [BUCKETS + 1, NH])
        gx, gq, gk, gcq, gckv, gmq, gmk = (sb(n, [P, w]) for n, w in (
            ("gx", KD), ("gq", 1), ("gk", 3), ("gcq", 2), ("gckv", 1), ("gmq", 1), ("gmk", 1)))
        loaded = {n: nc.alloc_semaphore("ev_loaded_" + n) for n in "small x tables scratch bias w0 w1 w2 w3 w4 cmp mla rope out".split()}
        pieces = [(Q0, KC0), (KC0, KS0), (KS0, KW0), (KW0, CQ0), (CQ0, EV_W)]
        with ExitStack() as memB:
            kc, vc = sb("kc", [P, SEQ], memB), sb("vc", [P, SEQ], memB)
            X = sb("X", [P, 2, 16, 2, 32], memB)
            w1, w2, pos = sb("w1", [P, 2, 16, 256], memB), sb("w2", [P, 2, 2, P], memB), sb("pos", [P, 2, 16], memB)
            hid, kcT = sb("hid", [P, 2, 2, 64], memB), sb("kcT", [P, 64], memB)
            pair, hid4 = sb("pair", [P, 2, P], memB), sb("hid4", [P, 2, 2, 4, 32], memB)
            E = q[:, :, :].rearrange("p a b -> p (a b)")[0:BUCKETS + 1, 0:3 * SEQ]
            with ExitStack() as memW:
                W = sb("W", [P, KD, EV_W], memW)
                win = D["ev_w_in"][0].rearrange("(p k) n -> p k n", k=KD)
                small = 0
                with stage(nc, "ev_load", "zeroed") as (block, s):
                    @block.sync
                    def _(sp):
                        nonlocal small
                        sp.dma_start(x[:, :, :], D["x"][0].rearrange("(t p) d -> p t d", p=P)).then_inc(loaded["x"], 16)
                        sp.dma_start(E, D["bucket_table"]).then_inc(loaded["tables"], 16)
                        sp.dma_start(relb[0:BUCKETS, :], D["rel_bias"]).then_inc(loaded["tables"], 16)
                        sp.dma_start(relb[BUCKETS:BUCKETS + 1, :], D["ones_row"]).then_inc(loaded["tables"], 16)
                        smalls = [(gx[:, :], D["ev_mix_norm"][0].rearrange("(p k) -> p k", k=KD)),
                                  (gcq[:, :], D["mla_cq_norm"][0].rearrange("(k p) -> p k", p=P)),
                                  (gckv[:, :], column(D["mla_ckv_norm"][0])),
                                  (gmq[0:MQK, :], column(D["mla_q_norm"][0])),
                                  (gmk[0:MQK, :], column(D["mla_k_norm"][0]))]
                        for a in (0, HD):
                            smalls += [(gq[a:a + HD, :], column(D["nsa_q_norm"][0])),
                                       (gk[a:a + HD, :], D["nsa_k_norm"][0].rearrange("i p -> p i"))]
                        for v in range(2):
                            smalls += [(pos[:, v], D["nsa_cmp_pos"][0, v].rearrange("(j a) d -> (a d) j", a=2))]
                        for dst, src in smalls:
                            sp.dma_start(dst, src, allow_slow_non_contiguous=True).then_inc(loaded["small"], 16)
                        small = 16 * len(smalls)
                        for i in range(2):
                            dst = W[:, :, 0:KC0].rearrange("p k (j s d) -> p k j s d", s=2, d=HD)[:, :, :, i]
                            for k in range(KD):
                                sp.dma_start(dst[:, k], win[:, k, i * 256:(i + 1) * 256].rearrange("p (j d) -> p j d", d=HD)) \
                                    .then_inc(loaded["w0"], 16)
                        for i, (a, b) in list(enumerate(pieces))[1:]:
                            sp.dma_start(W[:, :, a:b], win[:, :, a:b]).then_inc(loaded[f"w{i}"], 16)
                        for v in range(2):
                            sp.dma_start(w1[:, v], D["nsa_cmp_w1"][0, v].rearrange("(j p) n -> p j n", p=P)).then_inc(loaded["cmp"], 16)
                            for a in (0, HD):
                                sp.dma_start(w2[:, v, :, a:a + HD], D["nsa_cmp_w2"][0, v].rearrange("(a p) n -> p a n", p=P)).then_inc(loaded["cmp"], 16)
                        sp.dma_start(uq[:, :, :], D["mla_w_uq"][0].rearrange("(k p) n -> p k n", p=P)).then_inc(loaded["mla"], 16)
                        sp.dma_start(ukv[:, :], D["mla_w_ukv"][0]).then_inc(loaded["mla"], 16)

                    @block.gpsimd
                    def _(pool):
                        step = Steps(pool, s["zeroed"])
                        step(nc.gpsimd.memset(X[:, :, :, :, :], 0.0))
                        step(nc.gpsimd.memset(vblk[:, :, :, :], 0.0))

                scratch = nc.dram_tensor("bias_by_distance", [NH, 3 * SEQ], F32, kind="Internal").ap()
                with stage(nc, "ev_bias", "made copied") as (block, s):
                    PS = C.PS
                    by_head = cq6[0:NH, 0:3]

                    @block.tensor
                    def _(pe):
                        pe.wait_ge(loaded["tables"], 48)
                        for i in range(3):
                            nc.tensor.matmul(PS[0:NH, i, :], relb[:, :], E[:, i * SEQ:(i + 1) * SEQ], start=True, stop=True) \
                                .then_inc(s["made"], 1)

                    @block.vector
                    def _(dve):
                        dve.wait_ge(s["made"], 3)
                        for i in range(3):
                            ins = nc.vector.tensor_copy(by_head[:, i], PS[0:NH, i, :])
                        ins.then_inc(s["copied"], 1)

                    @block.sync
                    def _(sp):
                        sp.wait_ge(s["copied"], 1)
                        sp.dma_start(scratch, by_head.rearrange("p a b -> p (a b)")).then_inc(loaded["scratch"], 16)
                        sp.wait_ge(loaded["scratch"], 16)
                        for h in range(NH):
                            src = bass.AP(scratch.tensor, h * 3 * SEQ + SEQ + FWD_ZERO - (CMP_L - 1) - 31 * CMP_S, [[CMP_S, 32], [1, SEQ]])
                            sp.dma_start(TcT[h % 4 * 32:h % 4 * 32 + 32, h // 4], src).then_inc(loaded["bias"], 16)

                with stage(nc, "ev_wait", "scaled") as (block, s):
                    @block.vector
                    def _(dve):
                        dve.wait_ge(loaded["small"], small)
                        dve.wait_ge(loaded["x"], 16)
                        nc.vector.tensor_scalar(gq[:, :], gq[:, :], float(HD) ** -0.5, None, ALU.mult)
                        nc.vector.tensor_scalar(gmq[0:MQK, :], gmq[0:MQK, :], float(MQK) ** -0.5, None, ALU.mult)
                        for g in range(2):
                            nc.vector.tensor_copy(pair[:, g].rearrange("p (a d) -> p a d", a=2),
                                                  bcast(C.ident[:, g * HD:(g + 1) * HD].unsqueeze(1), [P, 2, HD]))

                norm_transpose(nc, C, x, gx, xnT, yT[:, :, :].rearrange("p (t a) b -> p t (a b)", a=2), "ev_norm")

                def features(lhsT, M, dst, r0=0):
                    return ([(lhsT(k), xnT[:, k]) for k in range(KD)], slice(r0, r0 + M), slice(0, SEQ), copy_to(nc, dst))

                def cols(a, M):
                    return lambda k: W[:, k, a:a + M]

                def take_vw(t):
                    def f(ps, steps):
                        nc.vector.tensor_copy(vsw[:, t, 1], ps[:, 0:P])
                        return nc.vector.tensor_copy(gate[:, t], ps[:, P:P + 3 * NH])
                    return f

                jobs, need = [], []
                for j in range(4):
                    jobs.append(features(lambda k, j=j: W[:, k, j * P:(j + 1) * P],
                                         P, q[:, j]))
                    need.append([0])
                for a, dst, w in ((KC0, kc, 1), (VC0, vc, 1), (KS0, ks, 2), (KW0, kw, 3)):
                    jobs.append(features(cols(a, P), P, dst[:, :]))
                    need.append([w])
                for t in range(NT):
                    tok = slice(t * P, (t + 1) * P)
                    jobs.append(([(xnT[:, k, tok], W[:, k, VS0:VS0 + P]) for k in range(KD)], slice(0, P), slice(0, P),
                                 copy_to(nc, vsw[:, t, 0])))
                    jobs.append(([(xnT[:, k, tok], W[:, k, VW0:VW0 + P + 3 * NH]) for k in range(KD)], slice(0, P),
                                 slice(0, P + 3 * NH), take_vw(t)))
                    need += [[2], [3]]
                for a, M, dst, r0 in ((CQ0, P, cq[:, 0], 0), (CQ0 + P, P, cq[:, 1], 0), (CKV0, P, ckv, 0),
                                      (KR0, ROT, kr[64:96, :], 64)):
                    jobs.append(features(cols(a, M), M, dst, r0))
                    need.append([4])
                products(nc, C, "ev_in", jobs, lambda n: [(loaded[f"w{i}"], 16 if i else 32 * KD) for i in need[n]])

            groups = [dict(src=[q[:, j]], gain=[gq[:, 0:1]], dst=[q[:, j]], ones=C.ones64[:, :], n=HD) for j in range(4)]
            groups += [dict(src=[k[:, :]], gain=[gk[:, i:i + 1]], dst=[k[:, :]], ones=C.ones64[:, :], n=HD)
                       for k, i in ((ks, 1), (kw, 2))]
            groups += [dict(src=[cq[:, 0], cq[:, 1]], gain=[gcq[:, 0:1], gcq[:, 1:2]], dst=[cq[:, 0], cq[:, 1]],
                            ones=C.ones[:, :], n=2 * P),
                       dict(src=[ckv], gain=[gckv[:, 0:1]], dst=[ckv], ones=C.ones[:, :], n=P)]
            norm_features(nc, C, "ev_norms", groups)

            flip, flip32 = yT[:, 0, 0:P], yT[:, 0, P:2 * P]
            Tr = xnT[:, 0:4].rearrange("p k (a c) -> p (k a) c", c=2 * P)
            def take_X(v, g):
                def f(ps, steps):
                    for a in range(2):
                        h = slice(a * HD, (a + 1) * HD)
                        src = ps[h].rearrange("p (c j a) -> p j c a", j=8, a=2)
                        for jh in range(2):
                            js = slice(8 * jh, 8 * jh + 8)
                            ins = nc.vector.tensor_tensor(X[h, v, js, g, 0:NCMP], src[:, :, jh:jh + NCMP, a],
                                                          bcast(pos[h, v, js].unsqueeze(2), [HD, 8, NCMP]), ALU.add)
                    return ins
                return f

            products(nc, C, "ev_X", [([(pair[:, g], (kc, vc)[v][:, :])], slice(0, P),
                                      slice(0, SEQ), take_X(v, g)) for v in range(2) for g in range(2)],
                     loads=lambda sp: sp.dma_start(
                         Tr, bass.AP(scratch.tensor, REV_ZERO - (2 * P - 1), [[1, P], [3 * SEQ, NH], [1, 2 * P]])
                     ).then_inc(loaded["bias"], 16))
            products(nc, C, "ev_hid", [([(w1[:, v, j, a * P:(a + 1) * P], X[:, v, j].rearrange("p g c -> p (g c)")) for j in range(16)],
                                        slice(0, P), slice(0, 64), copy_to(nc, hid[:, v, a])) for v in range(2) for a in range(2)],
                     lambda n: [(loaded["cmp"], 96)] if n == 0 else [])
            with stage(nc, "ev_gelu", "gelu sigmoid steps") as (block, s):
                @block.scalar
                def _(act):
                    nc.scalar.activation(hid[:, :, :, :], hid[:, :, :, :], ACT.Gelu_apprx_tanh).then_inc(s["gelu"], 1)
                    nc.scalar.activation(gate[:, :, :], gate[:, :, :], ACT.Sigmoid).then_inc(s["sigmoid"], 1)

                @block.vector
                def _(dve):
                    dve.wait_ge(s["gelu"], 1)
                    for a in range(2):
                        for g in range(2):
                            nc.vector.tensor_copy(hid4[:, a, g], bcast(hid[:, 1, a, g * 32:g * 32 + 32].unsqueeze(1), [P, 4, 32]))

                @block.gpsimd
                def _(pool):
                    step = Steps(pool, s["steps"])
                    for tile in (flip, flip32):
                        step(nc.gpsimd.memset(tile, 0.0))
                    step(nc.gpsimd.affine_select(out=flip, in_=flip, compare_op=ALU.not_equal, fill=1.0,
                                                 base=-(P - 1), pattern=[[1, P]], channel_multiplier=1))
                    step(nc.gpsimd.affine_select(out=flip32, in_=flip32, compare_op=ALU.not_equal, fill=1.0,
                                                 base=-31, pattern=[[-32, 4], [1, 32]], channel_multiplier=1))
                    pool.wait_ge(s["sigmoid"], 1)
                    g0 = gate[:, 0].rearrange("p (h b) -> p h b", b=3)[:, :, 0]
                    nc.gpsimd.affine_select(out=g0, in_=g0, compare_op=ALU.is_ge, fill=0.0, base=-(CMP_L - 1),
                                            pattern=[[0, NH]], channel_multiplier=1)

            def take_vblk(g):
                def f(ps, steps):
                    for h in range(4):
                        ins = nc.vector.tensor_copy(vblk[32 * h:32 * h + 32, g, h], ps[32 * h:32 * h + 32])
                    return ins
                return f

            jobs = [([(w2[:, 0, a], hid[:, 0, a]) for a in range(2)], slice(0, P), slice(0, 64), copy_to(nc, kcT[:, :]))]
            jobs += [([(hid4[:, a, g].rearrange("p r c -> p (r c)"), w2[:, 1, a, 0:HD]) for a in range(2)], slice(0, P), slice(0, HD),
                      take_vblk(g)) for g in range(2)]
            jobs += [([(flip, Tr[:, i:i + 2].rearrange("p a b -> p (a b)"))], slice(0, P), slice(0, SEQ),
                      copy_to(nc, T[:, i:i + 2].rearrange("p a b -> p (a b)"))) for i in range(0, NH, 2)]
            products(nc, C, "ev_cmp", jobs, lambda n: [(loaded["bias"], 16 * (NH + 1))] if n == 0 else [])
            norm_features(nc, C, "ev_kc", [dict(src=[kcT[:, :]], gain=[gk[:, 0:1]], dst=[kcT[:, :]], ones=C.ones64[:, :], n=HD)])

            with ExitStack() as m2, stage(nc, "ev_pc", "scored steps exped turned") as (block, s):
                sc = sb("sc", [P, NT, NH, 32], m2)
                mx = sb("mx", [P, 3, NT, NH], m2)
                PS = C.PS

                @block.tensor
                def _(pe):
                    pe.wait_ge(loaded["bias"], 16 * (NH + 1))
                    for t in range(NT):
                        for h in range(NH):
                            g = h // 4
                            if h % 4 == 0:
                                nc.tensor.matmul(PS[:, 4 * g + t, 0:P], TcT[:, g, t * P:(t + 1) * P], flip32, start=True, stop=False)
                            half = slice(g * HD, (g + 1) * HD)
                            ins = nc.tensor.matmul(PS[:, 4 * g + t, h % 4 * 32:(h % 4 + 1) * 32], q[half, h % 4, t * P:(t + 1) * P],
                                                   kcT[half, g * 32:(g + 1) * 32], start=False, stop=h % 4 == 3)
                            if h % 4 == 3:
                                ins.then_inc(s["scored"], 1)
                    pe.wait_ge(s["steps"], 2 * NT + 7)
                    for t in range(NT):
                        for g in range(2):
                            nc.tensor.transpose(PS[:, g, t * P:(t + 1) * P],
                                                sc[:, t, 4 * g:4 * g + 4].rearrange("p h c -> p (h c)"), C.ident[:, :])                                 .then_inc(s["turned"], 1)

                @block.scalar
                def _(act):
                    act.wait_ge(s["steps"], 2 * NT + 3)
                    nc.scalar.activation(sc[:, :, :, :], sc[:, :, :, :], ACT.Exp).then_inc(s["exped"], 1)

                @block.vector
                def _(dve):
                    step = Steps(dve, s["steps"])
                    for t in range(NT):
                        for g in range(2):
                            hs = slice(4 * g, 4 * g + 4)
                            dve.wait_ge(s["scored"], 2 * t + g + 1)
                            step(nc.vector.tensor_copy(sc[:, t, hs].rearrange("p h c -> p (h c)"), PS[:, 4 * g + t, 0:P]))
                    rows = sc[:, :, :, :].rearrange("p t h c -> p (t h) c")
                    m = [mx[:, i].rearrange("p t h -> p (t h)") for i in range(3)]
                    step(nc.vector.tensor_reduce(m[0], rows, AX.X, ALU.max))
                    step(nc.vector.tensor_tensor(rows, rows, bcast(m[0].unsqueeze(2), [P, NT * NH, 32]), ALU.subtract))
                    dve.sem_inc(s["steps"], 1)
                    step.n += 1
                    dve.wait_ge(s["exped"], 1)
                    step(nc.vector.tensor_reduce(m[1], rows, AX.X, ALU.add))
                    step(nc.vector.reciprocal(m[2], m[1]))
                    g0 = gate[:, :, :].rearrange("p t (h b) -> p (t h) b", b=3)[:, :, 0]
                    step(nc.vector.tensor_tensor(m[2], m[2], g0, ALU.mult))
                    step(nc.vector.tensor_tensor(rows, rows, bcast(m[2].unsqueeze(2), [P, NT * NH, 32]), ALU.mult))
                    dve.wait_ge(s["turned"], 2 * NT)
                    nc.vector.tensor_copy(pcT[:, :, :], PS[:, 0:2, :])

        wout = sb("wout", [P, 8, DM])
        cosT, sinT, turn = sb("cos", [P, SEQ]), sb("sin", [P, SEQ]), sb("turn", [P, ROT])
        qz = xnT
        with stage(nc, "ev_out_load", "x") as (block, s):
            @block.gpsimd
            def _(pool):
                nc.gpsimd.memset(qz[HD:P, 0:4], 0.0)

            @block.scalar
            def _(act):
                nc.scalar.activation(qz[0:HD, 0:4], q[0:HD], ACT.Copy)

            @block.vector
            def _(dve):
                nc.vector.memset(qz[0:HD, 4:8], 0.0)
                nc.vector.tensor_copy(qz[HD:P, 4:8], q[HD:P])

            @block.sync
            def _(sp):
                for dst, src in ((cosT[64:96, :], D["rope_table"][0]), (sinT[64:96, :], D["rope_table"][1]),
                                 (turn[64:96, :], D["rope_turn"])):
                    sp.dma_start(dst, src).then_inc(loaded["rope"], 16)
                sp.dma_start(wout[:, :, :], D["ev_w_out"][0].rearrange("(k p) n -> p k n", p=P)).then_inc(loaded["out"], 16)

        jobs = []
        for m in range(NH // 2):
            for br, k in enumerate((ks, kw)):
                for h in (2 * m, 2 * m + 1):
                    g, half = h // 4, slice(h // 4 * HD, (h // 4 + 1) * HD)
                    jobs.append(dict(q=qz[:, h], k=k[:, :], v=lambda kb, br=br, half=half: vsw[:, kb, br, half],
                                     bias=T[:, h], extra=None, gate=lambda i, h=h, br=br: gate[:, i, 3 * h + 1 + br:3 * h + 2 + br],
                                     first=(vblk[:, g, h % 4], pcT[:, g]) if br == 0 else None, start=br == 0, stop=br == 1,
                                     rows=slice(h % 2 * HD, (h % 2 + 1) * HD), bank=m % 2, out=yT[:, m]))
        attention(nc, C, "ev_nsa", jobs)

        with ExitStack() as m3:
            km, vm = sb("km", [MQK, NH, SEQ], m3), sb("vm", [P, NT, 512], m3)
            qm = xnT[0:MQK]

            def take_k(h):
                def f(ps, steps):
                    nc.vector.tensor_copy(km[64:96, h], kr[64:96, :])
                    return nc.vector.tensor_copy(km[0:64, h], ps)
                return f

            jobs = []
            for h in range(NH):
                jobs.append(([(uq[:, k, MQK * h:MQK * (h + 1)], cq[:, k]) for k in range(2)], slice(0, MQK), slice(0, SEQ),
                             copy_to(nc, qm[:, h])))
                jobs.append(([(ukv[:, P * h:P * h + HD], ckv)], slice(0, HD), slice(0, SEQ), take_k(h)))
            vcols = ukv[:, :].rearrange("p (h d) -> p h d", d=P)[:, :, HD:P]
            for t in range(NT):
                jobs.append(([(ckv[:, t * P:(t + 1) * P], vcols)], slice(0, P), slice(0, SEQ), copy_to(nc, vm[:, t])))
            products(nc, C, "ev_mla_in", jobs, lambda n: [(loaded["mla"], 32)] if n == 0 else [])
            norm_features(nc, C, "ev_mla_norm", [
                dict(src=[t[0:MQK, h]], gain=[g[0:MQK, 0:1]], dst=[t[0:MQK, h]], ones=C.ones[0:MQK, 0:MQK], n=MQK)
                for h in range(NH) for t, g in ((qm, gmq), (km, gmk))])

            with stage(nc, "ev_rope", "turned steps") as (block, s):
                r = slice(64, 96)
                tiles = [t[r, h] for h in range(NH) for t in (qm, km)]
                PS = C.PS

                @block.tensor
                def _(pe):
                    pe.wait_ge(loaded["rope"], 48)
                    for n, tile in enumerate(tiles):
                        if n >= 8:
                            pe.wait_ge(s["steps"], 3 * (n - 7))
                        nc.tensor.matmul(PS[r, n % 8, :], turn[r, :], tile, start=True, stop=True).then_inc(s["turned"], 1)

                @block.vector
                def _(dve):
                    step = Steps(dve, s["steps"])
                    dve.wait_ge(loaded["rope"], 48)
                    for n, tile in enumerate(tiles):
                        dve.wait_ge(s["turned"], n + 1)
                        step(nc.vector.tensor_tensor(tile, tile, cosT[r, :], ALU.mult))
                        step(nc.vector.tensor_tensor(PS[r, n % 8, :], PS[r, n % 8, :], sinT[r, :], ALU.mult))
                        step(nc.vector.tensor_tensor(tile, tile, PS[r, n % 8, :], ALU.add))

            jobs = []
            for h in range(NH):
                jobs.append(dict(q=qm[:, h], k=km[:, h], v=lambda kb, h=h: vm[:, kb, h * HD:(h + 1) * HD],
                                 bias=C.causal[:, :], extra=None, gate=None, first=None, start=True, stop=True,
                                 rows=slice(h % 2 * HD, (h % 2 + 1) * HD), bank=h // 2 % 2, out=yT[:, 4 + h // 2]))
            attention(nc, C, "ev_mla", jobs)
        if "yT_out" in D:
            with stage(nc, "dbg", "l") as (block, s):
                @block.sync
                def _(sp):
                    sp.dma_start(D["yT_out"].rearrange("(k p) t -> p k t", p=P), yT[:, :, :]).then_inc(s["l"], 16)
                    sp.wait_ge(s["l"], 16)
        add_projection(nc, C, "ev_out", yT, wout, x, (loaded["out"], 16))
        nc.clear_and_free_semaphores(list(loaded.values()))
        nc.all_engine_barrier(sem_only=True)


def mixer_odd(nc, C, D, x, xnT):
    TAPS = 3
    with ExitStack() as mem:
        def sb(name, shape):
            return mem.enter_context(nc.sbuf_tensor("od_" + name, shape, F32))

        yT = sb("yT", [P, 8, SEQ])
        W = sb("W", [P, KD, 3 * DM])
        wout = sb("wout", [P, 8, DM])
        gx, taps = sb("gx", [P, KD]), sb("taps", [P, TAPS, 8])
        cg, cu, conv = sb("cg", [P, SEQ]), sb("cu", [P, 2, SEQ + TAPS - 1]), sb("conv", [P, 2, SEQ])
        loaded = {n: nc.alloc_semaphore("od_loaded_" + n) for n in "small w0 w1 w2 w3 out".split()}
        win = D["od_w_in"][0].rearrange("(p k) (s n) -> p k s n", k=KD, s=3)
        with stage(nc, "od_load", "zeroed") as (block, s):
            @block.sync
            def _(sp):
                sp.dma_start(gx[:, :], D["od_mix_norm"][0].rearrange("(p k) -> p k", k=KD)).then_inc(loaded["small"], 16)
                for i in range(TAPS):
                    sp.dma_start(taps[:, i], D["conv_w"][0, i].rearrange("(j p) -> p j", p=P),
                                 allow_slow_non_contiguous=True).then_inc(loaded["small"], 16)
                for i in range(4):
                    for part in range(3):
                        sp.dma_start(W[:, :, part * DM + i * 256:part * DM + i * 256 + 256],
                                     win[:, :, part, i * 256:i * 256 + 256]).then_inc(loaded[f"w{i}"], 16)
                sp.dma_start(wout[:, :, :], D["od_w_out"][0].rearrange("(k p) n -> p k n", p=P)).then_inc(loaded["out"], 16)

            @block.vector
            def _(dve):
                nc.vector.memset(cu[:, :, 0:TAPS - 1], 0.0)
                dve.wait_ge(loaded["small"], 16 * (TAPS + 1))

        norm_transpose(nc, C, x, gx, xnT, yT[:, :, :].rearrange("p (t a) b -> p t (a b)", a=2), "od_norm")

        def take_cu(j):
            def f(ps, steps):
                steps(nc.vector.tensor_tensor(cu[:, j % 2, TAPS - 1:], cg[:, :], ps, ALU.mult))
                steps(nc.vector.tensor_scalar(conv[:, j % 2], cu[:, j % 2, 0:SEQ], taps[:, 0, j:j + 1], None, ALU.mult))
                for i in range(1, TAPS - 1):
                    steps(nc.vector.scalar_tensor_tensor(out=conv[:, j % 2], in0=cu[:, j % 2, i:i + SEQ], scalar=taps[:, i, j:j + 1],
                                                         in1=conv[:, j % 2], op0=ALU.mult, op1=ALU.add))
                i = TAPS - 1
                return nc.vector.scalar_tensor_tensor(out=conv[:, j % 2], in0=cu[:, j % 2, i:i + SEQ], scalar=taps[:, i, j:j + 1],
                                                      in1=conv[:, j % 2], op0=ALU.mult, op1=ALU.add)
            return f

        jobs = []
        for j in range(8):
            for part, take in ((1, copy_to(nc, cg[:, :])), (2, take_cu(j)),
                               (0, lambda ps, steps, j=j: nc.vector.tensor_tensor(yT[:, j], ps, conv[:, j % 2], ALU.mult))):
                a = part * DM + j * P
                jobs.append(([(W[:, k, a:a + P], xnT[:, k]) for k in range(KD)], slice(0, P), slice(0, SEQ), take))
        products(nc, C, "od_in", jobs, lambda n: [(loaded[f"w{n // 6}"], 48)], chained=True)
        add_projection(nc, C, "od_out", yT, wout, x, (loaded["out"], 16))
        nc.clear_and_free_semaphores(list(loaded.values()))
        nc.all_engine_barrier(sem_only=True)


def first_max(nc, step, scores, index, low, top, at, hit, shape):
    step(nc.vector.tensor_reduce(top, scores, AX.X, ALU.max))
    step(nc.vector.tensor_tensor(hit, scores, bcast(top.unsqueeze(2), shape), ALU.is_equal))
    step(nc.vector.scalar_tensor_tensor(out=hit, in0=hit, scalar=-16.0, in1=index, op0=ALU.mult, op1=ALU.add))
    step(nc.vector.tensor_reduce(at, hit, AX.X, ALU.min))
    step(nc.vector.tensor_tensor(hit, low, bcast(at.unsqueeze(2), shape), ALU.is_equal))


def make_index(nc, name, mem, n):
    index, low = (mem.enter_context(nc.sbuf_tensor(name + s, [P, NT, n], F32)) for s in ("_index", "_low"))
    with stage(nc, name, "made") as (block, s):
        @block.gpsimd
        def _(pool):
            nc.gpsimd.iota(index[:, :, :], pattern=[[0, NT], [1, n]], base=0, channel_multiplier=0,
                           allow_small_or_imprecise_dtypes=True).then_inc(s["made"], 1)
            pool.wait_ge(s["made"], 1)
            nc.gpsimd.tensor_scalar(low[:, :, :], index[:, :, :], 16.0, None, ALU.subtract)
    return index, low


def two_of(nc, C, name, mem, scores, n, factor=None):
    def sb(s, shape):
        return mem.enter_context(nc.sbuf_tensor(name + s, shape, F32))

    index, low = make_index(nc, name + "_index", mem, n)
    one, two, rest, w = (sb(a, [P, NT, n]) for a in ("_one", "_two", "_rest", "_w"))
    t = sb("_t", [P, 6, NT])
    shape = [P, NT, n]
    with stage(nc, name, "steps exped") as (block, s):
        @block.vector
        def _(dve):
            step = Steps(dve, s["steps"])
            first_max(nc, step, scores, index[:, :, :], low[:, :, :], t[:, 0], t[:, 1], one[:, :, :], shape)
            step(nc.vector.scalar_tensor_tensor(out=rest[:, :, :], in0=one[:, :, :], scalar=NEG, in1=scores, op0=ALU.mult, op1=ALU.add))
            first_max(nc, step, rest[:, :, :], index[:, :, :], low[:, :, :], t[:, 2], t[:, 1], two[:, :, :], shape)
            step(nc.vector.tensor_tensor(t[:, 3], t[:, 2], t[:, 0], ALU.subtract))
            dve.wait_ge(s["exped"], 1)
            step(nc.vector.tensor_scalar(t[:, 1], t[:, 4], 1.0, None, ALU.add))
            step(nc.vector.reciprocal(t[:, 0], t[:, 1]))
            step(nc.vector.tensor_tensor(t[:, 2], t[:, 4], t[:, 0], ALU.mult))
            step(nc.vector.tensor_tensor(one[:, :, :], one[:, :, :], bcast(t[:, 0].unsqueeze(2), shape), ALU.mult))
            step(nc.vector.tensor_tensor(two[:, :, :], two[:, :, :], bcast(t[:, 2].unsqueeze(2), shape), ALU.mult))
            step(nc.vector.tensor_tensor(w[:, :, :], one[:, :, :], two[:, :, :], ALU.add))

        @block.scalar
        def _(act):
            act.wait_ge(s["steps"], 12)
            nc.scalar.activation(t[:, 4], t[:, 3], ACT.Exp).then_inc(s["exped"], 1)
    return w


def logits(nc, C, name, xnT, w, bias, out, n):
    jobs = [([(xnT[:, k, t * P:(t + 1) * P], w[:, k]) for k in range(KD)], slice(0, P), slice(0, n),
             lambda ps, steps, t=t: nc.vector.tensor_tensor(out[:, t], ps, bias, ALU.add)) for t in range(NT)]
    products(nc, C, name, jobs)


def moe_top2(nc, C, D, x, xnT):
    NE, F = D["moe_w_gate"].shape[1], D["moe_w_gate"].shape[3]
    with ExitStack() as mem:
        def sb(name, shape):
            return mem.enter_context(nc.sbuf_tensor("moe_" + name, shape, F32))

        gx, wr, br, score = sb("gx", [P, KD]), sb("wr", [P, KD, NE]), sb("br", [P, NE]), sb("score", [P, NT, NE])
        with stage(nc, "moe_load", "loaded") as (block, s):
            @block.sync
            def _(sp):
                sp.dma_start(gx[:, :], D["od_ffn_norm"][0].rearrange("(p k) -> p k", k=KD)).then_inc(s["loaded"], 16)
                sp.dma_start(wr[:, :, :], D["moe_w_router"][0].rearrange("(p k) n -> p k n", k=KD)).then_inc(s["loaded"], 16)
                sp.dma_start(br[:, :], D["moe_b_router"].partition_broadcast(P).rearrange("p a n -> p (a n)")).then_inc(s["loaded"], 16)
                sp.wait_ge(s["loaded"], 48)
        xs = sb("xs", [P, NT, DM])
        norm_transpose(nc, C, x, gx, xnT, xs, "moe_norm")
        logits(nc, C, "moe_logits", xnT, wr, br[:, :], score, NE)
        w = two_of(nc, C, "moe_route", mem, score[:, :, :], NE)
        gv, uv = (D[n][0].rearrange("e (p k) f -> e p k f", k=KD) for n in ("moe_w_gate", "moe_w_up"))
        dv = D["moe_w_down"][0].rearrange("e (c p) d -> e p c d", p=P)
        mask = sb("mask", [P, NT, NE])
        with stage(nc, "moe_mask", "x") as (block, s):
            @block.vector
            def _(dve):
                nc.vector.tensor_scalar(mask[:, :, :], w[:, :, :], 0.0, None, ALU.is_gt)
        plan = plan_passes(nc, C, "moe_plan", mem, mask, NE)
        cut = lambda v: lambda e, c: v[e][:, :, c * 512:min((c + 1) * 512, F)]
        routed_passes(nc, C, "moe_pass", x, xs, xnT, gx, plan, NE, F, cut(gv), cut(uv), lambda e: dv[e],
                      lambda t, e: w[:, t, bass.ds(e, 1)], 1)


def ffn(nc, C, D, x, xnT):
    with ExitStack() as mem:
        gx = mem.enter_context(nc.sbuf_tensor("ffn_gx", [P, KD], F32))
        with stage(nc, "ffn_load", "loaded") as (block, s):
            @block.sync
            def _(sp):
                sp.dma_start(gx[:, :], D["ev_ffn_norm"][0].rearrange("(p k) -> p k", k=KD)).then_inc(s["loaded"], 16)
                sp.wait_ge(s["loaded"], 16)
        with ExitStack() as m2:
            xs = m2.enter_context(nc.sbuf_tensor("ffn_xs", [P, NT, DM], F32))
            norm_transpose(nc, C, x, gx, xnT, xs, "ffn_norm")
        parts = 2
        F = D["ffn_w_gate"].shape[2] // parts
        gv, uv = (D[n][0].rearrange("(p k) (e f) -> e p k f", k=KD, f=F) for n in ("ffn_w_gate", "ffn_w_up"))
        dv = D["ffn_w_down"][0].rearrange("(e c p) d -> e p c d", e=parts, p=P)
        gated_parts(nc, C, "ffn", xnT, x, parts, F, lambda e: gv[e], lambda e: uv[e], lambda e: dv[e], lambda t, e: C.one[:, 0:1])


def moe_groups(nc, C, D, x, xnT):
    NE, F = D["exp_w_gate_2"].shape[1], D["exp_w_gate_2"].shape[3]
    NG = D["router_gw_2"].shape[2]
    PG = NE // NG
    with ExitStack() as mem:
        def sb(name, shape):
            return mem.enter_context(nc.sbuf_tensor("hm_" + name, shape, F32))

        gx, wr, br, score = sb("gx", [P, KD]), sb("wr", [P, KD, NG + NE]), sb("br", [P, NG + NE]), sb("score", [P, NT, NG + NE])
        with stage(nc, "hm_load", "loaded") as (block, s):
            @block.sync
            def _(sp):
                sp.dma_start(gx[:, :], D["norm2_g_2"][0].rearrange("(p k) -> p k", k=KD)).then_inc(s["loaded"], 16)
                for w, b, a, n in (("router_gw_2", "router_gb_2", 0, NG), ("router_ew_2", "router_eb_2", NG, NE)):
                    sp.dma_start(wr[:, :, a:a + n], D[w][0].rearrange("(p k) n -> p k n", k=KD)).then_inc(s["loaded"], 16)
                    sp.dma_start(br[:, a:a + n], D[b].partition_broadcast(P).rearrange("p a n -> p (a n)")).then_inc(s["loaded"], 16)
                sp.wait_ge(s["loaded"], 80)
        xs = sb("xs", [P, NT, DM])
        norm_transpose(nc, C, x, gx, xnT, xs, "hm_norm")
        logits(nc, C, "hm_logits", xnT, wr, br[:, :], score, NG + NE)
        index, low = make_index(nc, "hm_index", mem, NG)
        group, ex, sel, t = sb("group", [P, NT, NG]), sb("ex", [P, NT, NG]), sb("sel", [P, NT, PG]), sb("t", [P, 4, NT])
        chosen = sb("chosen", [P, NT, NG, PG])
        shape = [P, NT, NG]
        with stage(nc, "hm_group", "steps exped") as (block, s):
            @block.vector
            def _(dve):
                step = Steps(dve, s["steps"])
                first_max(nc, step, score[:, :, 0:NG], index[:, :, :], low[:, :, :], t[:, 0], t[:, 1], group[:, :, :], shape)
                step(nc.vector.tensor_tensor(ex[:, :, :], score[:, :, 0:NG], bcast(t[:, 0].unsqueeze(2), shape), ALU.subtract))
                el = score[:, :, NG:NG + NE].rearrange("p t (g e) -> p t g e", g=NG)
                for i in range(NT):
                    nc.vector.tensor_tensor(chosen[:, i], el[:, i], bcast(group[:, i].unsqueeze(2), [P, NG, PG]), ALU.mult)
                step(nc.vector.tensor_copy(t[:, 1], t[:, 0]))
                step(nc.vector.tensor_reduce(sel[:, :, :], chosen[:, :, :, :].rearrange("p t g e -> p t e g"), AX.X, ALU.add))
                dve.wait_ge(s["exped"], 1)
                step(nc.vector.tensor_reduce(t[:, 2], ex[:, :, :], AX.X, ALU.add))
                step(nc.vector.reciprocal(t[:, 3], t[:, 2]))

            @block.scalar
            def _(act):
                act.wait_ge(s["steps"], 6)
                nc.scalar.activation(ex[:, :, :], ex[:, :, :], ACT.Exp).then_inc(s["exped"], 1)
        w = two_of(nc, C, "hm_route", mem, sel[:, :, :], PG)
        with stage(nc, "hm_weights", "steps") as (block, s):
            @block.vector
            def _(dve):
                step = Steps(dve, s["steps"])
                step(nc.vector.tensor_tensor(w[:, :, :], w[:, :, :], bcast(t[:, 3].unsqueeze(2), [P, NT, PG]), ALU.mult))
        plan = plan_passes(nc, C, "hm_plan", mem, group, NG)
        gv, uv = (D[n][0].rearrange("(g h e) (p k) f -> g h p k e f", g=NG, h=2, k=KD) for n in ("exp_w_gate_2", "exp_w_up_2"))
        dv = D["exp_w_down_2"][0].rearrange("(g e) (c p) d -> g p (e c) d", g=NG, p=P)
        routed_passes(nc, C, "hm_pass", x, xs, xnT, gx, plan, NG, PG * F, lambda e, c: gv[e, c], lambda e, c: uv[e, c], lambda e: dv[e],
                      lambda t, e: w[:, t], PG)


LW, FW, RW = 256, 512, 256
XA0, GA0, FQ0, FK0, FV0, FL0, PC0, IN_W = 0, 256, 512, 1024, 1536, 2048, 2056, 2952
CHUNK = 64
SUB = 16


def wkv_masks():
    r, c = np.arange(P)[:, None], np.arange(P)[None, :]
    same = lambda n: (r // n) == (c // n)
    return np.stack([same(SUB) & (r > c), same(SUB) & (r < c), same(2 * SUB) & ~same(SUB) & (r > c),
                     same(CHUNK) & ~same(2 * SUB) & (r > c), same(CHUNK) & (r < c), same(CHUNK) & (r <= c)]).astype(np.float32)


def chunk_restart():
    return np.broadcast_to((np.arange(SEQ) % CHUNK != 0).astype(np.float32), (P, SEQ)).copy()


def mixer_second(nc, C, D, x, xnT):
    with ExitStack() as mem:
        def sb(name, shape, m=mem):
            return m.enter_context(nc.sbuf_tensor("s_" + name, shape, F32))

        yT = sb("yT", [P, 8, SEQ])
        pm = sb("pm", [P, 7, SEQ + 1])
        cols = {}
        for n, w in (("gx", KD), ("lng", 2), ("cb", 2), ("ba", 2), ("bx", 2), ("lam", 2), ("fqg", 1), ("fkg", 1), ("fng", 4),
                     ("mu", 7), ("w0", 2), ("a0", 2), ("kk", 2), ("ka", 2), ("rk", 2), ("rlg", 2), ("rlb", 2), ("fb", 1)):
            cols[n] = sb(n, [P, w])
        taps = sb("taps", [P, 4, 2])
        wa, wx = sb("wa", [P, 2, P]), sb("wx", [P, 2, P])
        low = sb("low", [P, 3, RW])
        loaded = {n: nc.alloc_semaphore("s_loaded_" + n) for n in "small w0 w1 w2 w3 w4 w5 wkv out".split()}
        pieces = [(XA0, FQ0), (FQ0, FK0), (FK0, FV0), (FV0, FL0), (FL0, PC0 + 448), (PC0 + 448, IN_W)]
        memF = ExitStack()
        xa, ga = sb("xa", [P, 2, SEQ + 3], memF), sb("ga", [P, 2, SEQ], memF)
        fq, fk, fv, fl = sb("fq", [P, 4, SEQ], memF), sb("fk", [P, 4, SEQ], memF), sb("fv", [P, NT, SEQ], memF), sb("fl", [8, SEQ], memF)
        small = 0
        with ExitStack() as memW:
            W = sb("W", [P, KD, IN_W], memW)
            win = D["w_in_2"][0].rearrange("(p k) n -> p k n", k=KD)
            with stage(nc, "s_load", "zeroed") as (block, s):
                @block.sync
                def _(sp):
                    nonlocal small
                    sp.wait_ge(s["zeroed"], 2)
                    tiles = lambda n: D[n][0].rearrange("(i p) -> p i", p=P)
                    smalls = [(cols["gx"][:, :], D["norm1_g_2"][0].rearrange("(p k) -> p k", k=KD))]
                    smalls += [(cols[c][:, :], tiles(n)) for c, n in (
                        ("lng", "lru_norm_g_2"), ("cb", "conv_b_2"), ("ba", "lru_ba_2"), ("bx", "lru_bx_2"), ("lam", "lru_lambda_2"),
                        ("fng", "fox_norm_g_2"), ("mu", "rwkv_mu_2"), ("w0", "rwkv_w0_2"), ("a0", "rwkv_a0_2"), ("kk", "rwkv_kk_2"),
                        ("ka", "rwkv_ka_2"), ("rlg", "rwkv_ln_g_2"), ("rlb", "rwkv_ln_b_2"))]
                    smalls += [(cols["rk"][:, :], D["rwkv_rk_2"][0].rearrange("(i a) d -> (a d) i", a=2)),
                               (cols["fb"][0:8, :], column(D["fox_fb_2"][0]))]
                    for a in (0, HD):
                        smalls += [(cols["fqg"][a:a + HD, :], column(D["fox_qnorm_g_2"][0])),
                                   (cols["fkg"][a:a + HD, :], column(D["fox_knorm_g_2"][0]))]
                        for i in range(2):
                            smalls += [(wa[a:a + HD, i, a:a + HD], D["lru_wa_2"][0, 2 * i + a // HD]),
                                       (wx[a:a + HD, i, a:a + HD], D["lru_wx_2"][0, 2 * i + a // HD])]
                    smalls += [(taps[:, i], D["conv_w_2"][0, i].rearrange("(j p) -> p j", p=P)) for i in range(4)]
                    smalls += [(low[0:32, 0], D["rwkv_w2_2"][0]), (low[32:64, 1], D["rwkv_a2_2"][0]), (low[64:128, 2], D["rwkv_g2_2"][0])]
                    for dst, src in smalls:
                        sp.dma_start(dst, src, allow_slow_non_contiguous=True).then_inc(loaded["small"], 16)
                    small = 16 * len(smalls)
                    for i, (a, b) in enumerate(pieces):
                        sp.dma_start(W[:, :, a:b], win[:, :, a:b]).then_inc(loaded[f"w{i}"], 16)

                @block.vector
                def _(dve):
                    nc.vector.memset(wa[:, :, :], 0.0).then_inc(s["zeroed"], 1)
                    nc.vector.memset(wx[:, :, :], 0.0).then_inc(s["zeroed"], 1)
                    nc.vector.memset(xa[:, :, 0:3], 0.0)
                    nc.vector.memset(pm[:, :, 0:1], 0.0)
                    dve.wait_ge(loaded["small"], small)
                    nc.vector.tensor_scalar(cols["fqg"][:, :], cols["fqg"][:, :], float(HD) ** -0.5, None, ALU.mult)

            norm_transpose(nc, C, x, cols["gx"], xnT, yT[:, :, :].rearrange("p (t a) b -> p t (a b)", a=2), "s_norm")

            jobs, need = [], []

            def features(a, M, dst, w):
                jobs.append(([(W[:, k, a:a + M], xnT[:, k]) for k in range(KD)], slice(0, M), slice(0, SEQ), copy_to(nc, dst)))
                need.append(w)

            for i in range(2):
                features(XA0 + i * P, P, xa[:, i, 3:], [0])
                features(GA0 + i * P, P, ga[:, i], [0])
            for i in range(4):
                features(FQ0 + i * P, P, fq[:, i], [1])
            for i in range(4):
                features(FK0 + i * P, P, fk[:, i], [2])
            for t in range(NT):
                jobs.append(([(xnT[:, k, t * P:(t + 1) * P], W[:, k, FV0:FV0 + FW]) for k in range(KD)], slice(0, P), slice(0, FW),
                             copy_to(nc, fv[:, t])))
                need.append([3])
            features(FL0, 8, fl[:, :], [4])
            for i in range(7):
                features(PC0 + i * P, P, pm[:, i, 1:], [4, 5])
            products(nc, C, "s_in", jobs, lambda n: [(loaded[f"w{i}"], 16) for i in need[n]])

        with ExitStack() as m:
            xc, r, i_, la, h = (sb(n, [P, 2, SEQ], m) for n in ("xc", "r", "i", "la", "h"))
            lc = sb("lc", [P, 6, 2], m)
            both = [P, 2 * SEQ]
            flat = lambda ap: ap.rearrange("p a b -> p (a b)")
            with stage(nc, "s_conv", "steps") as (block, s):
                @block.vector
                def _(dve):
                    step = Steps(dve, s["steps"])
                    for i in range(2):
                        step(nc.vector.tensor_scalar(xc[:, i], xa[:, i, 0:SEQ], taps[:, 0, i:i + 1], cols["cb"][:, i:i + 1], ALU.mult, ALU.add))
                        for j in range(1, 4):
                            step(nc.vector.scalar_tensor_tensor(out=xc[:, i], in0=xa[:, i, j:j + SEQ], scalar=taps[:, j, i:i + 1],
                                                                in1=xc[:, i], op0=ALU.mult, op1=ALU.add))
            products(nc, C, "s_lru_gates", [([(w[:, i], xc[:, i])], slice(0, P), slice(0, SEQ), copy_to(nc, dst[:, i]))
                                            for w, dst in ((wa, r), (wx, i_)) for i in range(2)])
            with stage(nc, "s_lru", "steps act") as (block, s):
                @block.scalar
                def _(act):
                    step = Steps(act, s["act"])
                    for i in range(2):
                        nc.scalar.activation(r[:, i], r[:, i], ACT.Sigmoid, bias=cols["ba"][:, i:i + 1])
                        nc.scalar.activation(i_[:, i], i_[:, i], ACT.Sigmoid, bias=cols["bx"][:, i:i + 1])
                    act.wait_ge(s["steps"], 2)
                    step(nc.scalar.activation(lc[:, 2], lc[:, 1], ACT.Exp))
                    step(nc.scalar.activation(lc[:, 3], lc[:, 2], ACT.Ln, bias=C.one[:, 0:1]))
                    act.wait_ge(s["steps"], 6)
                    step(nc.scalar.activation(flat(h[:, :, :]), flat(la[:, :, :]), ACT.Tanh))
                    step(nc.scalar.activation(flat(la[:, :, :]), flat(la[:, :, :]), ACT.Exp))
                    act.wait_ge(s["steps"], 10)
                    step(nc.scalar.activation(flat(h[:, :, :]), flat(h[:, :, :]), ACT.Sqrt))
                    step(nc.scalar.activation(flat(ga[:, :, :]), flat(ga[:, :, :]), ACT.Gelu_apprx_tanh))

                @block.vector
                def _(dve):
                    step = Steps(dve, s["steps"])
                    lam = cols["lam"][:, :]
                    step(nc.vector.tensor_scalar(lc[:, 0], lam, -1.0, 0.0, ALU.mult, ALU.max))
                    step(nc.vector.scalar_tensor_tensor(out=lc[:, 1], in0=lc[:, 0], scalar=-2.0, in1=lam, op0=ALU.mult, op1=ALU.subtract))
                    dve.wait_ge(s["act"], 2)
                    step(nc.vector.tensor_tensor(lc[:, 4], lc[:, 0], lc[:, 3], ALU.add))
                    step(nc.vector.tensor_scalar(lc[:, 5], lc[:, 4], -8.0, None, ALU.mult))
                    for i in range(2):
                        step(nc.vector.tensor_scalar(la[:, i], r[:, i], lc[:, 5, i:i + 1], None, ALU.mult))
                    dve.wait_ge(s["act"], 4)
                    step(nc.vector.tensor_tensor(flat(r[:, :, :]), flat(la[:, :, :]), flat(la[:, :, :]), ALU.mult))
                    step(nc.vector.tensor_scalar(flat(r[:, :, :]), flat(r[:, :, :]), -1.0, -1.0, ALU.mult, ALU.add))
                    step(nc.vector.tensor_tensor(flat(h[:, :, :]), flat(h[:, :, :]), flat(r[:, :, :]), ALU.mult))
                    step(nc.vector.tensor_tensor(flat(i_[:, :, :]), flat(i_[:, :, :]), flat(xc[:, :, :]), ALU.mult))
                    dve.wait_ge(s["act"], 5)
                    step(nc.vector.tensor_tensor(flat(i_[:, :, :]), flat(i_[:, :, :]), flat(h[:, :, :]), ALU.mult))
                    for i in range(2):
                        step(nc.vector.tensor_tensor_scan(xc[:, i], la[:, i], i_[:, i], 0.0, ALU.mult, ALU.add))
                    dve.wait_ge(s["act"], 6)
                    for i in range(2):
                        step(nc.vector.tensor_tensor(yT[:, i], xc[:, i], ga[:, i], ALU.mult))
            norm_features(nc, C, "s_lru_norm", [dict(src=[yT[:, i] for i in range(2)], gain=[cols["lng"][:, i:i + 1] for i in range(2)],
                                                     dst=[yT[:, i] for i in range(2)], ones=C.ones[:, :], n=LW)])

        with ExitStack() as m:
            decay, lf, pick = sb("decay", [P, SEQ], m), sb("lf", [8, 4, SEQ], m), sb("pick", [P, 8, P], m)
            with stage(nc, "s_decay", "steps act") as (block, s):
                @block.vector
                def _(dve):
                    step = Steps(dve, s["steps"])
                    step(nc.vector.memset(decay[:, :], 0.0))
                    step(nc.vector.memset(lf[:, 3], 1.0))
                    step(nc.vector.tensor_scalar(fl[:, :], fl[:, :], cols["fb"][0:8, 0:1], None, ALU.add))
                    step(nc.vector.tensor_scalar(lf[:, 0], fl[:, :], -1.0, 0.0, ALU.mult, ALU.max))
                    step(nc.vector.scalar_tensor_tensor(out=lf[:, 1], in0=lf[:, 0], scalar=-2.0, in1=fl[:, :], op0=ALU.mult, op1=ALU.subtract))
                    nc.vector.tensor_copy(pick[:, :, :], bcast(C.ident[:, 0:8].unsqueeze(2), [P, 8, P]))
                    dve.wait_ge(s["act"], 2)
                    step(nc.vector.tensor_tensor(lf[:, 0], lf[:, 0], lf[:, 2], ALU.add))
                    step(nc.vector.tensor_tensor_scan(decay[0:8, :], lf[:, 3], lf[:, 0], 0.0, ALU.mult, ALU.add))

                @block.scalar
                def _(act):
                    act.wait_ge(s["steps"], 5)
                    nc.scalar.activation(lf[:, 1], lf[:, 1], ACT.Exp).then_inc(s["act"], 1)
                    act.wait_ge(s["act"], 1)
                    nc.scalar.activation(lf[:, 2], lf[:, 1], ACT.Ln, bias=C.one[0:8, 0:1]).then_inc(s["act"], 1)
            norm_features(nc, C, "s_fox_qk", [dict(src=[t[:, i]], gain=[cols[g][:, 0:1]], dst=[t[:, i]], ones=C.ones64[:, :], n=HD)
                                              for i in range(4) for t, g in ((fq, "fqg"), (fk, "fkg"))])
            qz = xnT
            with stage(nc, "s_fox_qz", "x") as (block, s):
                pairs = qz[:, :, :].rearrange("p (m a) t -> p m a t", a=2)

                @block.gpsimd
                def _(pool):
                    nc.gpsimd.memset(pairs[HD:P, :, 0], 0.0)

                @block.scalar
                def _(act):
                    nc.scalar.activation(pairs[0:HD, :, 0], fq[0:HD], ACT.Copy)

                @block.vector
                def _(dve):
                    nc.vector.memset(pairs[0:HD, :, 1], 0.0)
                    nc.vector.tensor_copy(pairs[HD:P, :, 1], fq[HD:P])
            jobs = []
            for h in range(8):
                half = slice(h % 2 * HD, h % 2 * HD + HD)
                jobs.append(dict(q=qz[:, h], k=fk[:, h // 2], v=lambda kb, h=h: fv[:, kb, h * HD:(h + 1) * HD],
                                 bias=C.causal[:, :], extra=(pick[:, h], decay[:, :]), gate=None, first=None, start=True, stop=True,
                                 rows=half, bank=h // 2 % 2, out=yT[:, 2 + h // 2]))
            attention(nc, C, "s_fox", jobs)
            norm_features(nc, C, "s_fox_norm", [dict(src=[yT[:, 2 + i] for i in range(4)], gain=[cols["fng"][:, i:i + 1] for i in range(4)],
                                                     dst=[yT[:, 2 + i] for i in range(4)], ones=C.ones[:, :], n=FW)])
        memF.close()
        rwkv(nc, C, D, yT, xnT, pm, cols, low, loaded["wkv"])

        if "yT_out" in D:
            with stage(nc, "dbg2", "l") as (block, s):
                @block.sync
                def _(sp):
                    sp.dma_start(D["yT_out"].rearrange("(k p) t -> p k t", p=P), yT[:, :, :]).then_inc(s["l"], 16)
                    sp.wait_ge(s["l"], 16)
        wout = sb("wout", [P, 8, DM])
        with stage(nc, "s_out_load", "x") as (block, s):
            @block.sync
            def _(sp):
                sp.dma_start(wout[:, :, :], D["w_out_2"][0].rearrange("(k p) n -> p k n", p=P)).then_inc(loaded["out"], 16)
        add_projection(nc, C, "s_out", yT, wout, x, (loaded["out"], 16))
        nc.clear_and_free_semaphores(list(loaded.values()))
        nc.all_engine_barrier(sem_only=True)


def paired(nc, C, name, jobs):
    with stage(nc, name, "made taken steps") as (block, s):
        PS = C.PS

        @block.tensor
        def _(pe):
            for n, (after, items, take) in enumerate(jobs):
                need = max(after, n - 3)
                if need > 0:
                    pe.wait_ge(s["taken"], need)
                for bank, cols, rows, lhsT, rhs, start, stop in items:
                    out = PS[rows, 2 * (n % 4) + bank, cols]
                    if start == "turn":
                        ins = nc.tensor.transpose(out, lhsT, rhs)
                    else:
                        ins = nc.tensor.matmul(out, lhsT, rhs, start=start, stop=stop)
                ins.then_inc(s["made"], 1)

        @block.vector
        def _(dve):
            steps = Steps(dve, s["steps"])
            for n, (after, items, take) in enumerate(jobs):
                dve.wait_ge(s["made"], n + 1)
                take(PS[:, 2 * (n % 4):2 * (n % 4) + 2, :], steps).then_inc(s["taken"], 1)
                dve.wait_ge(s["taken"], n + 1)


def rwkv(nc, C, D, yT, xnT, pm, cols, low, loaded):
    PR, HH = 2, 4
    with ExitStack() as mem:
        def sb(name, shape, m=mem):
            return m.enter_context(nc.sbuf_tensor("rw_" + name, shape, F32))

        At, Bt, Kt, Rt, al, gl, bonus, rs, eLx, enL = (sb(n, [P, 2, SEQ]) for n in (
            "At", "Bt", "Kt", "Rt", "al", "gl", "bonus", "rs", "eLx", "enL"))
        eL = sb("eL", [P, 2, SEQ])
        masks, restart = sb("masks", [P, 6, P]), sb("restart", [P, SEQ])
        ocol = sb("ocol", [P, 2])
        flat = lambda ap: ap.rearrange("p a b -> p (a b)")
        p = pm[:, :, 1:]
        with stage(nc, "rw_mix", "steps act diff") as (block, s):
            @block.sync
            def _(sp):
                sp.dma_start(masks[:, :, :], D["wkv_masks"].rearrange("m p c -> p m c")).then_inc(loaded, 16)
                sp.dma_start(restart[:, :], D["chunk_restart"]).then_inc(loaded, 16)

            @block.vector
            def _(dve):
                step = Steps(dve, s["steps"])
                for i in (6, 0, 1, 2, 3, 4, 5):
                    step(nc.vector.tensor_tensor(rs[:, 0], pm[:, i, 0:SEQ], pm[:, i, 1:], ALU.subtract))
                    step(nc.vector.scalar_tensor_tensor(out=pm[:, i, 1:], in0=rs[:, 0], scalar=cols["mu"][:, i:i + 1], in1=pm[:, i, 1:],
                                                        op0=ALU.mult, op1=ALU.add))
                nc.vector.tensor_scalar(ocol[:, :], cols["ka"][:, :], -1.0, 1.0, ALU.mult, ALU.add)
                for i in range(2):
                    step(nc.vector.tensor_scalar(At[:, i], p[:, 2 + i], cols["kk"][:, i:i + 1], None, ALU.mult))
                step(nc.vector.tensor_tensor(flat(bonus[:, :, :]), flat(At[:, :, :]), flat(At[:, :, :]), ALU.mult))

            @block.scalar
            def _(act):
                act.wait_ge(s["steps"], 2)
                nc.scalar.activation(p[0:32, 6], p[0:32, 6], ACT.Tanh)
                nc.scalar.activation(p[64:P, 6], p[64:P, 6], ACT.Sigmoid)
        jobs = []
        for i in range(2):
            c = slice(i * P, (i + 1) * P)
            jobs += [([(low[0:32, 0, c], p[0:32, 6])], slice(0, P), slice(0, SEQ), copy_to(nc, enL[:, i])),
                     ([(low[32:64, 1, c], p[32:64, 6])], slice(0, P), slice(0, SEQ), copy_to(nc, al[:, i])),
                     ([(low[64:P, 2, c], p[64:P, 6])], slice(0, P), slice(0, SEQ), copy_to(nc, gl[:, i])),
                     ([(C.ones64[:, :], bonus[:, i])], slice(0, P), slice(0, SEQ), copy_to(nc, rs[:, i]))]
        products(nc, C, "rw_low", jobs)
        with stage(nc, "rw_decay", "steps act") as (block, s):
            @block.scalar
            def _(act):
                step = Steps(act, s["act"])
                for i in range(2):
                    step(nc.scalar.activation(enL[:, i], enL[:, i], ACT.Sigmoid, bias=cols["w0"][:, i:i + 1]))
                for i in range(2):
                    step(nc.scalar.activation(al[:, i], al[:, i], ACT.Sigmoid, bias=cols["a0"][:, i:i + 1]))
                step(nc.scalar.activation(flat(rs[:, :, :]), flat(rs[:, :, :]), ACT.Sqrt))
                act.wait_ge(s["steps"], 4)
                step(nc.scalar.activation(flat(eLx[:, :, :]), flat(eLx[:, :, :]), ACT.Exp))
                step(nc.scalar.activation(flat(enL[:, :, :]), flat(eL[:, :, :]), ACT.Exp, scale=-1.0))
                step(nc.scalar.activation(flat(eL[:, :, :]), flat(eL[:, :, :]), ACT.Exp))

            @block.vector
            def _(dve):
                step = Steps(dve, s["steps"])
                dve.wait_ge(loaded, 32)
                dve.wait_ge(s["act"], 2)
                step(nc.vector.tensor_scalar(flat(enL[:, :, :]), flat(enL[:, :, :]), -math.exp(-0.5), None, ALU.mult))
                for i in range(2):
                    step(nc.vector.tensor_tensor_scan(eL[:, i], restart[:, :], enL[:, i], 0.0, ALU.mult, ALU.add))
                step(nc.vector.tensor_tensor(flat(eLx[:, :, :]), flat(eL[:, :, :]), flat(enL[:, :, :]), ALU.subtract))
                dve.wait_ge(s["act"], 5)
                step(nc.vector.tensor_scalar(flat(rs[:, :, :]), flat(rs[:, :, :]), 1e-12, None, ALU.max))
                step(nc.vector.reciprocal(flat(rs[:, :, :]), flat(rs[:, :, :])))
                step(nc.vector.tensor_tensor(flat(At[:, :, :]), flat(At[:, :, :]), flat(rs[:, :, :]), ALU.mult))
                step(nc.vector.tensor_tensor(flat(Bt[:, :, :]), flat(At[:, :, :]), flat(al[:, :, :]), ALU.mult))
                for i in range(2):
                    step(nc.vector.tensor_scalar(al[:, i], al[:, i], cols["ka"][:, i:i + 1], ocol[:, i:i + 1], ALU.mult, ALU.add))
                    step(nc.vector.tensor_tensor(al[:, i], al[:, i], p[:, 2 + i], ALU.mult))
                    step(nc.vector.scalar_tensor_tensor(out=bonus[:, i], in0=al[:, i], scalar=cols["rk"][:, i:i + 1], in1=p[:, i],
                                                        op0=ALU.mult, op1=ALU.mult))
                dve.wait_ge(s["act"], 8)
                step(nc.vector.scalar_tensor_tensor(out=flat(At[:, :, :]), in0=flat(At[:, :, :]), scalar=-1.0, in1=flat(eLx[:, :, :]),
                                                    op0=ALU.mult, op1=ALU.mult))
                step(nc.vector.tensor_tensor(flat(Bt[:, :, :]), flat(Bt[:, :, :]), flat(enL[:, :, :]), ALU.mult))
                step(nc.vector.tensor_tensor(flat(Kt[:, :, :]), flat(al[:, :, :]), flat(enL[:, :, :]), ALU.mult))
                for i in range(2):
                    step(nc.vector.tensor_tensor(Rt[:, i], p[:, i], eL[:, i], ALU.mult))
        products(nc, C, "rw_bonus", [([(C.ones64[:, :], bonus[:, i])], slice(0, P), slice(0, SEQ),
                                      lambda ps, steps, i=i: nc.vector.tensor_tensor(bonus[:, i], ps, p[:, 4 + i], ALU.mult)) for i in range(2)])

        with ExitStack() as m:
            MA, UA, MB, UB, Y, M1, M2, NTr = (sb(n, [P, NT, HH, P], m) for n in (
                "MA", "UA", "MB", "UB", "Y", "M1", "M2", "NT"))
            QB, QK = MB, UB
            tok = sb("tok", [P, NT, 3, HH, HD], m)
            free = xnT[:, :, :].rearrange("p a b -> p (a b)")
            AN = free[:, 0:2048].rearrange("p (t h c) -> p t h c", t=NT, h=HH)
            AZ = AN
            GF = free[:, 2048:4096].rearrange("p (c a b d) -> p c a b d", c=8, a=2, b=PR)
            ApT = al
            SA = eLx[:, :, :].rearrange("p a (b h d) -> p (a b) h d", h=HH, d=HD)
            AT = enL[:, :, :].rearrange("p a (b h d) -> p (a b) h d", h=HH, d=HD)
            S = sb("S", [P, 9, PR, HD], m)
            SF = sb("SF", [P, PR, HD], m)
            full = slice(0, P)

            def half(hp):
                return slice(hp * HD, (hp + 1) * HD)

            def bank_view(ps, w):
                return ps[:, :, 0:2 * w].rearrange("p a (b c) -> p a b c", b=2)

            def rows4(T, t):
                return T[:, t].rearrange("p (a b) c -> p a b c", a=2)

            def masked(ps, steps, t, *outs):
                for T, mk in outs:
                    for hp in range(2):
                        ins = nc.vector.tensor_tensor(T[:, t, 2 * hp:2 * hp + 2], ps[:, hp, 0:256].rearrange("p (b c) -> p b c", b=2),
                                                      bcast(masks[:, mk].unsqueeze(1), [P, 2, P]), ALU.mult)
                return ins

            def put(T, t):
                return lambda ps, steps: nc.vector.tensor_copy(rows4(T, t), bank_view(ps, P))

            jobs = []

            def gram(t, left, right, take, after=0):
                c = slice(t * P, (t + 1) * P)
                items = [(hp, slice(pr * P, (pr + 1) * P), full, left[half(hp), pr, c], right[half(hp), pr, c], True, True)
                         for hp in range(2) for pr in range(PR)]
                jobs.append((after, items, take))

            def mul(after, t, left, right, take, w=P):
                items = [(hp, slice(pr * w, (pr + 1) * w), full, left(2 * hp + pr), right(2 * hp + pr), True, True)
                         for hp in range(2) for pr in range(PR)]
                jobs.append((after, items, take))

            for t in range(NT):
                gram(t, At, Bt, lambda ps, st, t=t: masked(ps, st, t, (MA, 0), (M1, 2), (M2, 3)))
            for t in range(NT):
                def take_u(ps, st, t=t):
                    st(masked(ps, st, t, (UA, 1)))
                    return nc.vector.tensor_tensor(Y[:, t], UA[:, t], bcast(C.ident[:, :].unsqueeze(1), [P, HH, P]), ALU.add)
                gram(t, Bt, At, take_u)
            for t in range(NT):
                gram(t, Kt, At, lambda ps, st, t=t: masked(ps, st, t, (NTr, 4)))
            for t in range(NT):
                c = slice(t * P, (t + 1) * P)
                for qi, T in enumerate((At, Bt, Kt, None)):
                    src = lambda pr: (T[:, pr, c] if T is not None else p[:, 4 + pr, c])
                    items = [(0, slice(pr * P, (pr + 1) * P), full, src(pr), C.ident[:, :], "turn", True) for pr in range(PR)]

                    def take_tok(ps, st, t=t, qi=qi):
                        v = ps[:, 0, 0:256].rearrange("p (b a d) -> p a b d", b=2, a=2)
                        if qi == 0:
                            nc.vector.tensor_copy(rows4(AT, t), v)
                            return nc.vector.tensor_copy(rows4(AN, t)[:, :, :, 0:HD], v)
                        return nc.vector.tensor_copy(tok[:, t, qi - 1].rearrange("p (a b) d -> p a b d", a=2), v)
                    jobs.append((0, items, take_tok))

            def accumulate(t):
                return lambda ps, st: nc.vector.tensor_tensor(rows4(Y, t), rows4(Y, t), bank_view(ps, P), ALU.add)

            def level(make):
                done = len(jobs)
                for t in range(NT):
                    make(done, t)

            for (Mo, Uo), (Mn, Un), last in (((MA, UA), (MB, UB), False), ((MB, UB), (MA, UA), False), ((MA, UA), (MB, UB), True)):
                level(lambda d, t: mul(d, t, lambda h: Uo[:, t, h], lambda h: Mo[:, t, h], put(Mn, t)))
                if not last:
                    level(lambda d, t: mul(d - NT, t, lambda h: Mo[:, t, h], lambda h: Uo[:, t, h], put(Un, t)))
                level(lambda d, t: mul(d, t, lambda h: Mn[:, t, h], lambda h: Y[:, t, h], accumulate(t)))
            done = len(jobs)
            for t in range(NT):
                gram(t, Bt, Rt, lambda ps, st, t=t: masked(ps, st, t, (QB, 5)), done)
                gram(t, Kt, Rt, lambda ps, st, t=t: masked(ps, st, t, (QK, 5)), done)
            for Moff in (M1, M2):
                level(lambda d, t: jobs.append((d, [(h // 2, slice(h % 2 * P, (h % 2 + 1) * P), full, Y[:, t, h], C.ident[:, :], "turn", True)
                                                    for h in range(HH)], put(MA, t))))
                level(lambda d, t: mul(d - NT, t, lambda h: Moff[:, t, h], lambda h: Y[:, t, h], put(UA, t)))
                level(lambda d, t: mul(d, t, lambda h: MA[:, t, h], lambda h: UA[:, t, h], accumulate(t)))
            level(lambda d, t: mul(d, t, lambda h: NTr[:, t, h], lambda h: tok[:, t, 2, h],
                                   lambda ps, st: nc.vector.tensor_copy(rows4(AN, t)[:, :, :, HD:P], bank_view(ps, HD)), HD))
            level(lambda d, t: mul(d, t, lambda h: Y[:, t, h], lambda h: AN[:, t, h], put(AZ, t)))

            def apt(d, t):
                items = [(pr, slice(0, P), half(hp), AT[:, t, 2 * hp + pr], Y[:, t, 2 * hp + pr], True, True)
                         for pr in range(PR) for hp in range(2)]
                jobs.append((d - NT, items, lambda ps, st: nc.vector.tensor_copy(ApT[:, :, t * P:(t + 1) * P], ps[:, :, 0:P])))
            level(apt)
            done = len(jobs)
            for c in range(8):
                t, cr = c // 2, half(c % 2)
                items = []
                for hp in range(2):
                    for pr in range(PR):
                        h = 2 * hp + pr
                        items.append((c % 2, slice(pr * HD, (pr + 1) * HD), half(hp), AZ[cr, t, h, 0:HD], tok[cr, t, 0, h], True, True))
                        o = slice((2 + pr) * HD, (3 + pr) * HD)
                        items.append((c % 2, o, half(hp), tok[cr, t, 0, h], AZ[cr, t, h, HD:P], True, False))
                        items.append((c % 2, o, half(hp), tok[cr, t, 1, h], tok[cr, t, 2, h], False, True))
                jobs.append((done, items, lambda ps, st, c=c: nc.vector.tensor_copy(
                    GF[:, c].rearrange("p a b d -> p (a b d)"), ps[:, c % 2, 0:256])))
            paired(nc, C, "rw_chunks", jobs)

            with stage(nc, "rw_states", "made steps") as (block, s):
                PS = C.PS

                @block.tensor
                def _(pe):
                    for c in range(8):
                        pe.wait_ge(s["steps"], 1 + 3 * c)
                        for hp in range(2):
                            for pr in range(PR):
                                ins = nc.tensor.matmul(PS[half(hp), 2 * (c % 2) + hp, pr * HD:(pr + 1) * HD], GF[half(hp), c, 0, pr],
                                                       S[half(hp), c, pr], start=True, stop=True)
                        ins.then_inc(s["made"], 1)

                @block.vector
                def _(dve):
                    step = Steps(dve, s["steps"])
                    step(nc.vector.memset(S[:, 0], 0.0))
                    for c in range(8):
                        step(nc.vector.tensor_tensor(SF[:, :, :], S[:, c], GF[:, c, 1], ALU.add))
                        dve.wait_ge(s["made"], c + 1)
                        for hp in range(2):
                            ins = nc.vector.tensor_tensor(SF[half(hp)], SF[half(hp)], PS[half(hp), 2 * (c % 2) + hp, 0:P]
                                                          .rearrange("p (b d) -> p b d", b=2), ALU.add)
                        step(ins)
                        end = (c + 1) * CHUNK - 1
                        step(nc.vector.tensor_tensor(S[:, c + 1], SF[:, :, :], bcast(eL[:, :, end:end + 1], [P, PR, HD]), ALU.mult))

            jobs = []
            for t in range(NT):
                items = []
                for hp in range(2):
                    for pr in range(PR):
                        for c in (2 * t, 2 * t + 1):
                            items.append((hp, slice(pr * HD, (pr + 1) * HD), half(c % 2), ApT[half(hp), pr, c * CHUNK:(c + 1) * CHUNK],
                                          S[half(hp), c, pr], True, True))
                jobs.append((0, items, lambda ps, st, t=t: nc.vector.tensor_tensor(
                    rows4(SA, t), bank_view(ps, HD), rows4(AZ, t)[:, :, :, HD:P], ALU.add)))
            done = len(jobs)
            for t in range(NT):
                items = []
                for pr in range(PR):
                    for hp in range(2):
                        h = 2 * hp + pr
                        cs = slice(0, P)
                        items.append((pr, cs, half(hp), SA[:, t, h], QB[:, t, h], True, False))
                        items.append((pr, cs, half(hp), tok[:, t, 2, h], QK[:, t, h], False, False))
                        for c in (2 * t, 2 * t + 1):
                            items.append((pr, slice(c % 2 * CHUNK, (c % 2 + 1) * CHUNK), half(hp), S[half(hp), c, pr],
                                          Rt[half(hp), pr, c * CHUNK:(c + 1) * CHUNK], False, c % 2 == 1))
                jobs.append((done, items, lambda ps, st, t=t: nc.vector.tensor_copy(At[:, :, t * P:(t + 1) * P], ps[:, :, 0:P])))
            paired(nc, C, "rw_outputs", jobs)

        o = At
        products(nc, C, "rw_mean", [([(C.ones64[:, :], o[:, i])], slice(0, P), slice(0, SEQ), lambda ps, steps, i=i:
                                     nc.vector.scalar_tensor_tensor(out=Bt[:, i], in0=ps, scalar=-1.0 / HD, in1=o[:, i], op0=ALU.mult,
                                                                    op1=ALU.add)) for i in range(2)])
        norm_features(nc, C, "rw_gn", [dict(src=[Bt[:, i]], gain=[cols["rlg"][:, i:i + 1]], dst=[Bt[:, i]], ones=C.ones64[:, :], n=HD)
                                       for i in range(2)], eps=64e-5)
        with stage(nc, "rw_end", "steps") as (block, s):
            @block.vector
            def _(dve):
                step = Steps(dve, s["steps"])
                for i in range(2):
                    step(nc.vector.scalar_tensor_tensor(out=Bt[:, i], in0=Bt[:, i], scalar=cols["rlb"][:, i:i + 1], in1=bonus[:, i],
                                                        op0=ALU.add, op1=ALU.add))
                    step(nc.vector.tensor_tensor(yT[:, 6 + i], Bt[:, i], gl[:, i], ALU.mult))


CONSTANTS = {"bucket_table": bucket_table, "rope_table": lambda: rope_tables()[0], "rope_turn": lambda: rope_tables()[1],
             "ones_row": lambda: np.ones((1, NH), np.float32), "wkv_masks": wkv_masks, "chunk_restart": chunk_restart}


def two_blocks(nc, D, out):
    stored = nc.alloc_semaphore("out_stored")
    with ExitStack() as mem:
        x = mem.enter_context(nc.sbuf_tensor("x", [P, NT, DM], F32))
        xnT = mem.enter_context(nc.sbuf_tensor("xnT", [P, KD, SEQ], F32))
        C = make_consts(nc, mem)
        mixer_even(nc, C, D, x, xnT)
        ffn(nc, C, D, x, xnT)
        mixer_odd(nc, C, D, x, xnT)
        moe_top2(nc, C, D, x, xnT)
        mixer_second(nc, C, D, x, xnT)
        moe_groups(nc, C, D, x, xnT)
        with nc.Block(name="store", no_gpsimd_drain=True) as block:
            @block.sync
            def _(sp):
                sp.dma_start(out[0].rearrange("(t p) d -> p t d", p=P), x[:, :, :]).then_inc(stored, 16)
                sp.wait_ge(stored, 16)


def kernel(**inputs):
    import concourse.bacc as bacc
    from concourse.bass_utils import run_bass_kernel_spmd

    nc = bacc.Bacc("TRN2", target_bir_lowering=False, num_devices=1)
    arrays, D = {}, {}
    for name, a in list(inputs.items()) + [(n, f()) for n, f in CONSTANTS.items()]:
        arrays[f"in_{name}"] = np.ascontiguousarray(a)
        D[name] = nc.dram_tensor(f"in_{name}", arrays[f"in_{name}"].shape, F32, kind="ExternalInput").ap()
    out = nc.dram_tensor("out_x", (1, SEQ, DM), F32, kind="ExternalOutput").ap()
    two_blocks(nc, D, out)
    result = run_bass_kernel_spmd(nc, [arrays], core_ids=[0])
    return result.results[0]["out_x"]
```

```python
import math
from contextlib import ExitStack, contextmanager

import numpy as np

import concourse.bass as bass
from concourse import mybir

F32 = mybir.dt.float32
F32R = mybir.dt.float32r
ALU = mybir.AluOpType
ACT = mybir.ActivationFunctionType
AX = mybir.AxisListType

P = 128
SEQ, DM = 512, 1024
NT = SEQ // P
KD = DM // P
EPS = 1e-6
NEG = -1e30


@contextmanager
def stage(nc, name, sems):
    handles = {s: nc.alloc_semaphore(f"{name}_{s}") for s in sems.split()}
    with nc.Block(name=name, no_gpsimd_drain=True) as block:
        yield block, handles
    nc.clear_and_free_semaphores(list(handles.values()))
    nc.all_engine_barrier(sem_only=True)


class Steps:

    def __init__(self, eng, sem):
        self.eng, self.sem, self.n = eng, sem, 0

    def __call__(self, ins):
        self.n += 1
        ins.then_inc(self.sem, 1)
        self.eng.wait_ge(self.sem, self.n)


def bcast(ap, shape):
    return ap.to_broadcast(shape)


def norm_transpose(nc, C, x, gain, xnT, xs, name, loads=None, gain_loaded=None):
    with ExitStack() as mem, stage(nc, name, "squared_a squared_v mean root rstd scaled turned") as (block, s):
        ss = mem.enter_context(nc.sbuf_tensor(name + "_ss", [P, 4, NT], F32))
        PS = C.PS

        if loads is not None:
            @block.sync
            def _(sp):
                loads(sp)

        @block.scalar
        def _(act):
            for t in (0, 1):
                nc.scalar.activation(xs[:, t], x[:, t], ACT.Square, accum_out=ss[:, 0, t:t + 1]).then_inc(s["squared_a"], 1)
            act.wait_ge(s["mean"], 1)
            nc.scalar.activation(ss[:, 2], ss[:, 1], ACT.Sqrt).then_inc(s["root"], 1)
            act.wait_ge(s["rstd"], 1)
            for t in range(NT):
                nc.scalar.activation(xs[:, t], x[:, t], ACT.Copy, scale=ss[:, 3, t:t + 1]).then_inc(s["scaled"], 1)

        @block.vector
        def _(dve):
            for t in (2, 3):
                nc.vector.tensor_tensor_reduce(out=xs[:, t], in0=x[:, t], in1=x[:, t], scale=1.0, scalar=0.0, op0=ALU.mult,
                                               op1=ALU.add, accum_out=ss[:, 0, t:t + 1]).then_inc(s["squared_v"], 1)
            dve.wait_ge(s["squared_a"], 2)
            dve.wait_ge(s["squared_v"], 2)
            nc.vector.tensor_scalar(ss[:, 1], ss[:, 0], 1.0 / DM, EPS, ALU.mult, ALU.add).then_inc(s["mean"], 1)
            dve.wait_ge(s["root"], 1)
            nc.vector.reciprocal(ss[:, 3], ss[:, 2]).then_inc(s["rstd"], 1)
            if gain_loaded is not None:
                dve.wait_ge(*gain_loaded)
            for t in range(NT):
                dve.wait_ge(s["turned"], t + 1)
                for h in range(2):
                    g = bcast(gain[:, 4 * h:4 * h + 4].unsqueeze(2), [P, 4, P])
                    nc.vector.tensor_tensor(xnT[:, 4 * h:4 * h + 4, t * P:(t + 1) * P],
                                            PS[:, 2 * t + h].rearrange("p (k c) -> p k c", k=4), g, ALU.mult)

        @block.tensor
        def _(pe):
            for t in range(NT):
                pe.wait_ge(s["scaled"], t + 1)
                for k in range(KD):
                    ins = nc.tensor.transpose(PS[:, 2 * t + k // 4, (k % 4) * P:(k % 4 + 1) * P],
                                              xs[:, t].rearrange("p (m k) -> p k m", k=KD)[:, k], C.ident[:, :])
                ins.then_inc(s["turned"], 1)


def products(nc, C, name, jobs, ready=None, chained=False, loads=None):
    with stage(nc, name, "made taken steps") as (block, s):
        PS = C.PS

        if loads is not None:
            @block.sync
            def _(sp):
                loads(sp)

        @block.tensor
        def _(pe):
            for n, (pairs, rows, cols, take) in enumerate(jobs):
                if ready is not None:
                    for sem, value in ready(n):
                        pe.wait_ge(sem, value)
                if n >= 8:
                    pe.wait_ge(s["taken"], n - 7)
                for i, (lhsT, rhs) in enumerate(pairs):
                    ins = nc.tensor.matmul(PS[rows, n % 8, cols], lhsT, rhs, start=i == 0, stop=i == len(pairs) - 1)
                ins.then_inc(s["made"], 1)

        @block.vector
        def _(dve):
            steps = Steps(dve, s["steps"])
            for n, (pairs, rows, cols, take) in enumerate(jobs):
                dve.wait_ge(s["made"], n + 1)
                take(PS[rows, n % 8, cols], steps).then_inc(s["taken"], 1)
                if chained:
                    dve.wait_ge(s["taken"], n + 1)


def copy_to(nc, dst):
    return lambda ps, steps: nc.vector.tensor_copy(dst, ps)


def norm_features(nc, C, name, groups, eps=EPS):
    B = 4
    G = len(groups)
    batches = [range(a, min(a + B, G)) for a in range(0, G, B)]
    with ExitStack() as mem, stage(nc, name, "squared summed logged rstd steps normed") as (block, s):
        sq = mem.enter_context(nc.sbuf_tensor(name + "_sq", [P, 4, SEQ], F32))
        rs = mem.enter_context(nc.sbuf_tensor(name + "_rs", [P, 2 * B, SEQ], F32))
        tt = mem.enter_context(nc.sbuf_tensor(name + "_tt", [P, 2, SEQ], F32))
        ec = mem.enter_context(nc.sbuf_tensor(name + "_eps", [P, 1], F32))
        PS = C.PS
        first = [0]
        for g in groups:
            first.append(first[-1] + len(g["src"]))

        def part(ap):
            a = ap.start_partition() if callable(ap.start_partition) else ap.start_partition
            return slice(a, a + ap.shape[0]), ap.shape[1]

        @block.gpsimd
        def _(pool):
            nc.gpsimd.memset(ec[:, :], eps).then_inc(s["squared"], 1)
            for g, grp in enumerate(groups):
                for i, src in enumerate(grp["src"]):
                    m = first[g] + i
                    rows, n = part(src)
                    pool.wait_ge(s["squared"], m + 1)
                    if m >= 4:
                        pool.wait_ge(s["summed"], m - 3)
                    nc.gpsimd.tensor_tensor(sq[rows, m % 4, 0:n], src, src, ALU.mult).then_inc(s["squared"], 1)

        @block.scalar
        def _(act):
            act.wait_ge(s["squared"], 1)
            for batch in batches:
                for g in batch:
                    rows, n = part(groups[g]["src"][0])
                    act.wait_ge(s["summed"], first[g + 1])
                    if g >= 2 * B:
                        act.wait_ge(s["normed"], first[g - 2 * B + 1])
                    nc.scalar.activation(rs[rows, g % (2 * B), 0:n], PS[rows, g % 8, 0:n], ACT.Ln,
                                         bias=ec[rows, 0:1], scale=1.0 / groups[g]["n"]).then_inc(s["logged"], 1)
                for g in batch:
                    rows, n = part(groups[g]["src"][0])
                    act.wait_ge(s["logged"], g + 1)
                    nc.scalar.activation(rs[rows, g % (2 * B), 0:n], rs[rows, g % (2 * B), 0:n], ACT.Exp,
                                         scale=-0.5).then_inc(s["rstd"], 1)

        @block.tensor
        def _(pe):
            for g, grp in enumerate(groups):
                if g >= 8:
                    pe.wait_ge(s["normed"], first[g - 7])
                for i, src in enumerate(grp["src"]):
                    m = first[g] + i
                    rows, n = part(src)
                    pe.wait_ge(s["squared"], m + 2)
                    nc.tensor.matmul(PS[rows, g % 8, 0:n], grp["ones"], sq[rows, m % 4, 0:n],
                                     start=i == 0, stop=i == len(grp["src"]) - 1).then_inc(s["summed"], 1)

        @block.vector
        def _(dve):
            step = Steps(dve, s["steps"])

            def newton(gs, k):
                for g in gs:
                    rows, n = part(groups[g]["src"][0])
                    y, t, N = rs[rows, g % (2 * B), 0:n], tt[rows, g % 2, 0:n], groups[g]["n"]
                    if k == 0:
                        dve.wait_ge(s["rstd"], g + 1)
                        ins = nc.vector.scalar_tensor_tensor(out=t, in0=PS[rows, g % 8, 0:n], scalar=N * eps, in1=y, op0=ALU.add, op1=ALU.mult)
                    elif k == 1:
                        ins = nc.vector.scalar_tensor_tensor(out=t, in0=t, scalar=-0.5 / N, in1=y, op0=ALU.mult, op1=ALU.mult)
                    else:
                        ins = nc.vector.scalar_tensor_tensor(out=y, in0=t, scalar=1.5, in1=y, op0=ALU.add, op1=ALU.mult)
                    ins.then_inc(s["steps"], 1)
                    step.n += 1
                dve.wait_ge(s["steps"], step.n)

            for a in range(0, G, 2):
                gs = range(a, min(a + 2, G))
                for k in range(3):
                    newton(gs, k)
                for g in gs:
                    rows, n = part(groups[g]["src"][0])
                    for src, gain, dst in zip(groups[g]["src"], groups[g]["gain"], groups[g]["dst"]):
                        nc.vector.scalar_tensor_tensor(out=dst, in0=src, scalar=gain, in1=rs[rows, g % (2 * B), 0:n],
                                                       op0=ALU.mult, op1=ALU.mult).then_inc(s["normed"], 1)
                dve.wait_ge(s["normed"], first[gs[-1] + 1])


def attention(nc, C, name, jobs):
    U = NT * len(jobs)
    LAG = 3
    pairs = len(jobs) // 2
    with ExitStack() as mem, stage(
            nc, name, "scored biased maxed exped inv coef scaled turned placed valued stored") as (block, s):
        pr = mem.enter_context(nc.sbuf_tensor(name + "_p", [P, 3, SEQ], F32))
        pn = mem.enter_context(nc.sbuf_tensor(name + "_pn", [P, 3, SEQ], F32))
        pT = mem.enter_context(nc.sbuf_tensor(name + "_pT", [P, 4, NT, SEQ], F32))
        st = mem.enter_context(nc.sbuf_tensor(name + "_st", [P, 4, 8], F32))
        PS = C.PS
        stores = [0]
        for m in range(pairs):
            stores.append(stores[-1] + (1 if jobs[2 * m]["stop"] else 0))

        @block.tensor
        def _(pe):
            def scores(u):
                job, i = jobs[u // NT], u % NT
                if u >= 3:
                    pe.wait_ge(s["exped"], u - 2)
                q, k = job["q"], job["k"]
                ins = nc.tensor.matmul(PS[:, u % 3, 0:(i + 1) * P], q[:, i * P:(i + 1) * P], k[:, 0:(i + 1) * P],
                                       start=True, stop=job["extra"] is None)
                if job["extra"] is not None:
                    ins = nc.tensor.matmul(PS[:, u % 3, 0:(i + 1) * P], job["extra"][0], job["extra"][1][:, 0:(i + 1) * P],
                                           start=False, stop=True)
                ins.then_inc(s["scored"], 1)

            def turn(u):
                i = u % NT
                pe.wait_ge(s["scaled"], u + 1)
                if u >= 2:
                    pe.wait_ge(s["placed"], u - 1)
                for kb in range(i + 1):
                    ins = nc.tensor.transpose(PS[:, 3 + u % 2, kb * P:(kb + 1) * P], pn[:, u % 3, kb * P:(kb + 1) * P],
                                              C.ident[:, :])
                ins.then_inc(s["turned"], 1)

            def values(m):
                both = jobs[2 * m], jobs[2 * m + 1]
                pe.wait_ge(s["placed"], NT * (2 * m + 2))
                bank, start, stop = 5 + both[0]["bank"], both[0]["start"], both[0]["stop"]
                if start and stores[m] >= 2:
                    pe.wait_ge(s["stored"], stores[m] - 1)
                if both[0]["first"] is not None:
                    for job in both:
                        nc.tensor.matmul(PS[job["rows"], bank, :], job["first"][0], job["first"][1], start=True, stop=False)
                for kb in range(NT):
                    for n, job in enumerate(both):
                        ins = nc.tensor.matmul(PS[job["rows"], bank, kb * P:SEQ], job["v"](kb), pT[:, (2 * m + n) % 4, kb, kb * P:SEQ],
                                               start=kb == 0 and start and job["first"] is None, stop=kb == NT - 1 and stop)
                        if kb == NT - 1:
                            ins.then_inc(s["valued"], 1)

            for u in range(U + LAG + 1):
                if u < U:
                    scores(u)
                if 0 <= u - LAG < U:
                    turn(u - LAG)
                v = u - LAG - 1
                if v >= 0 and v % (2 * NT) == 2 * NT - 1:
                    values(v // (2 * NT))

        @block.scalar
        def _(act):
            def exps(u):
                i = u % NT
                act.wait_ge(s["maxed"], u + 1)
                if u >= 3:
                    act.wait_ge(s["scaled"], u - 2)
                nc.scalar.activation(pr[:, u % 3, 0:(i + 1) * P], PS[:, u % 3, 0:(i + 1) * P], ACT.Exp,
                                     bias=st[:, 0, u % 8:u % 8 + 1], accum_out=st[:, 1, u % 8:u % 8 + 1]).then_inc(s["exped"], 1)

            def scale(u):
                i = u % NT
                act.wait_ge(s["coef"], u + 1)
                if u >= 3:
                    act.wait_ge(s["turned"], u - 2)
                nc.scalar.activation(pn[:, u % 3, 0:(i + 1) * P], pr[:, u % 3, 0:(i + 1) * P], ACT.Copy,
                                     scale=st[:, 3, u % 8:u % 8 + 1]).then_inc(s["scaled"], 1)

            def place(u):
                if u % 4 not in (1, 2):
                    return
                j, i = u // NT, u % NT
                act.wait_ge(s["turned"], u + 1)
                if u >= 1:
                    act.wait_ge(s["placed"], u)
                if j >= 4:
                    act.wait_ge(s["valued"], (j // 2 - 1) * 2)
                nc.scalar.activation(pT[:, j % 4, 0:i + 1, i * P:(i + 1) * P],
                                     PS[:, 3 + u % 2, 0:(i + 1) * P].rearrange("p (k c) -> p k c", c=P), ACT.Copy).then_inc(s["placed"], 1)

            for u in range(U + LAG + 1):
                if u < U:
                    exps(u)
                if 0 <= u - 1 < U:
                    scale(u - 1)
                if 0 <= u - LAG < U:
                    place(u - LAG)

        @block.vector
        def _(dve):
            def biased(u):
                job, i = jobs[u // NT], u % NT
                wb = job["bias"].shape[1]
                w = min(wb, (i + 1) * P)
                dve.wait_ge(s["scored"], u + 1)
                cols = slice((i + 1) * P - w, (i + 1) * P)
                nc.vector.tensor_tensor(PS[:, u % 3, cols], PS[:, u % 3, cols], job["bias"][:, wb - w:wb],
                                        ALU.add).then_inc(s["biased"], 1)

            def maxed(u):
                i = u % NT
                dve.wait_ge(s["biased"], u + 1)
                nc.vector.tensor_reduce(st[:, 0, u % 8:u % 8 + 1], PS[:, u % 3, 0:(i + 1) * P], AX.X, ALU.max,
                                        negate=True).then_inc(s["maxed"], 1)

            def coef(u):
                job, i = jobs[u // NT], u % NT
                dve.wait_ge(s["exped"], u + 1)
                nc.vector.reciprocal(st[:, 2, u % 8:u % 8 + 1], st[:, 1, u % 8:u % 8 + 1]).then_inc(s["inv"], 1)
                dve.wait_ge(s["inv"], u + 1)
                gate = C.one[:, 0:1] if job["gate"] is None else job["gate"](i)
                nc.vector.tensor_tensor(st[:, 3, u % 8:u % 8 + 1], st[:, 2, u % 8:u % 8 + 1], gate,
                                        ALU.mult).then_inc(s["coef"], 1)

            def place(u):
                if u % 4 in (1, 2):
                    return
                j, i = u // NT, u % NT
                dve.wait_ge(s["turned"], u + 1)
                if u >= 1:
                    dve.wait_ge(s["placed"], u)
                if j >= 4:
                    dve.wait_ge(s["valued"], (j // 2 - 1) * 2)
                nc.vector.tensor_copy(pT[:, j % 4, 0:i + 1, i * P:(i + 1) * P],
                                      PS[:, 3 + u % 2, 0:(i + 1) * P].rearrange("p (k c) -> p k c", c=P)).then_inc(s["placed"], 1)

            def store(m):
                if jobs[2 * m]["stop"]:
                    dve.wait_ge(s["valued"], 2 * m + 2)
                    nc.vector.tensor_copy(jobs[2 * m]["out"], PS[:, 5 + jobs[2 * m]["bank"], :]).then_inc(s["stored"], 1)

            done = 0
            for u in range(U + LAG + 3):
                if u < U:
                    biased(u)
                if 0 <= u - 1 < U:
                    coef(u - 1)
                if u < U:
                    maxed(u)
                if 0 <= u - LAG < U:
                    place(u - LAG)
                v = u - LAG - 2
                if v >= 0 and v % (2 * NT) == 2 * NT - 1:
                    store(v // (2 * NT))
                    done += 1
            assert done == pairs


def split_product(nc, out, left, right, start, stop):
    (lh, ll), (rh, rl) = left, right
    nc.tensor.matmul(out, lh, rl, start=start, stop=False)
    nc.tensor.matmul(out, ll, rh, start=False, stop=False)
    return nc.tensor.matmul(out, lh, rh, start=False, stop=stop)


def low_alias(nc, name, shape):
    size = 4 * math.prod(shape[1:])
    return nc.alloc_sbuf_tensor_at(name, shape, F32R, offset=nc.sbuf_base - size)


def f32(ap):
    return ap.bitcast(F32)


def add_projection(nc, C, name, yT, yL, w, wL, x, source):
    with ExitStack() as mem, stage(nc, name, "y_high w_high y_split w_split made " + " ".join(f"w{k}" for k in range(KD))) as (block, s):
        yH = mem.enter_context(nc.sbuf_tensor(name + "_yH", [P, KD, SEQ], F32R))
        wH = mem.enter_context(nc.sbuf_tensor(name + "_wH", [P, KD, DM], F32R))
        PS = C.PS
        outs = [(t, h) for t in range(NT) for h in range(2)]

        @block.sync
        def _(sp):
            for k in range(KD):
                sp.dma_start(w[:, k], source[:, k]).then_inc(s[f"w{k}"], 16)

        @block.scalar
        def _(act):
            for k in range(KD):
                nc.scalar.activation(yH[:, k], yT[:, k], ACT.Copy).then_inc(s["y_high"], 1)
                act.wait_ge(s[f"w{k}"], 16)
                nc.scalar.activation(wH[:, k], w[:, k], ACT.Copy).then_inc(s["w_high"], 1)

        @block.tensor
        def _(pe):
            for k in range(KD):
                pe.wait_ge(s["y_split"], k + 1)
                pe.wait_ge(s["w_split"], k + 1)
                for n, (t, h) in enumerate(outs):
                    tok, cols = slice(t * P, (t + 1) * P), slice(h * 512, (h + 1) * 512)
                    ins = split_product(nc, PS[:, n, :], (yH[:, k, tok], yL[:, k, tok]), (wH[:, k, cols], wL[:, k, cols]),
                                        k == 0, k == KD - 1)
                    if k == KD - 1:
                        ins.then_inc(s["made"], 1)

        @block.vector
        def _(dve):
            for k in range(KD):
                dve.wait_ge(s["y_high"], k + 1)
                nc.vector.tensor_tensor(yL[:, k], yT[:, k], f32(yH[:, k]), ALU.subtract).then_inc(s["y_split"], 1)
                dve.wait_ge(s["w_high"], k + 1)
                nc.vector.tensor_tensor(wL[:, k], w[:, k], f32(wH[:, k]), ALU.subtract).then_inc(s["w_split"], 1)
            for n, (t, h) in enumerate(outs):
                dve.wait_ge(s["made"], n + 1)
                dst = x[:, t, h * 512:(h + 1) * 512]
                nc.vector.tensor_tensor(dst, PS[:, n, :], dst, ALU.add)


def split_features(nc, C, name, xnT, xL, xH, jobs, plain=(), chained=False, loads=None, wH=None):
    RH = 2
    NP = len(plain)
    with ExitStack() as mem, stage(nc, name, "made taken steps x_high x_split high split") as (block, s):
        if wH is None:
            wH = mem.enter_context(nc.sbuf_tensor(name + "_wH", [P, RH, KD, P], F32R))
        PS = C.PS

        if loads is not None:
            @block.sync
            def _(sp):
                loads(sp)

        @block.tensor
        def _(pe):
            for n, (pairs, rows, cols, take, ready) in enumerate(plain):
                for need in ready:
                    pe.wait_ge(*need)
                if n >= 8:
                    pe.wait_ge(s["taken"], n - 7)
                for i, (lhsT, rhs) in enumerate(pairs):
                    ins = nc.tensor.matmul(PS[rows, n % 8, cols], lhsT, rhs, start=i == 0, stop=i == len(pairs) - 1)
                ins.then_inc(s["made"], 1)
            for j, (w, wL, take, ready) in enumerate(jobs):
                n = NP + j
                pe.wait_ge(s["split"], j + 1)
                if n >= 8:
                    pe.wait_ge(s["taken"], n - 7)
                for k in range(KD):
                    if j == 0:
                        pe.wait_ge(s["x_split"], k + 1)
                    ins = split_product(nc, PS[:, n % 8, :], (wH[:, j % RH, k], wL[:, k]), (xH[:, k], xL[:, k]), k == 0, k == KD - 1)
                ins.then_inc(s["made"], 1)

        @block.scalar
        def _(act):
            def high(j):
                for need in jobs[j][3]:
                    act.wait_ge(*need)
                if j >= RH:
                    act.wait_ge(s["made"], NP + j - RH + 1)
                nc.scalar.activation(wH[:, j % RH], jobs[j][0], ACT.Copy).then_inc(s["high"], 1)

            for k in range(2):
                nc.scalar.activation(xH[:, k], xnT[:, k], ACT.Copy).then_inc(s["x_high"], 1)
            high(0)
            for k in range(2, KD):
                nc.scalar.activation(xH[:, k], xnT[:, k], ACT.Copy).then_inc(s["x_high"], 1)
            for j in range(1, len(jobs)):
                high(j)

        @block.vector
        def _(dve):
            steps = Steps(dve, s["steps"])

            def low(j):
                dve.wait_ge(s["high"], j + 1)
                nc.vector.tensor_tensor(jobs[j][1], jobs[j][0], f32(wH[:, j % RH]), ALU.subtract).then_inc(s["split"], 1)

            def x_low(k):
                dve.wait_ge(s["x_high"], k + 1)
                nc.vector.tensor_tensor(xL[:, k], xnT[:, k], f32(xH[:, k]), ALU.subtract).then_inc(s["x_split"], 1)

            for n, (pairs, rows, cols, take, ready) in enumerate(plain):
                dve.wait_ge(s["made"], n + 1)
                take(PS[rows, n % 8, cols], steps).then_inc(s["taken"], 1)
            for k in range(2):
                x_low(k)
            low(0)
            for k in range(2, KD):
                x_low(k)
            low(1)
            for j, (w, wL, take, ready) in enumerate(jobs):
                n = NP + j
                dve.wait_ge(s["made"], n + 1)
                if j + 2 < len(jobs):
                    low(j + 2)
                take(PS[:, n % 8, :], steps).then_inc(s["taken"], 1)
                if chained:
                    dve.wait_ge(s["taken"], n + 1)


def gated_parts(nc, C, name, xnT, x, parts, F, wg, wu, wd):
    NF = F // P
    ND = 2 * NF
    UR, DR = 4, NF
    last_user = {c % UR: c for c in range(NF)}
    uses = [len(range(r, NF, UR)) for r in range(UR)]
    sems = ("xh xl up_high up_split up_free down_high down_split down_free made u_made silu hidden h_high h_split y_made y_taken "
            + " ".join(f"up{r}" for r in range(UR)) + " " + " ".join(f"down{r}" for r in range(DR)))
    with ExitStack() as mem, stage(nc, name, sems) as (block, s):
        def sb(n, shape, dt=F32R):
            return mem.enter_context(nc.sbuf_tensor(name + n, shape, dt))

        def whole_and_low(n, shape):
            return sb(n, shape, F32), low_alias(nc, name + n + "_low", shape)

        up, upL = whole_and_low("_up", [P, UR, 2, KD, P])
        down, downL = whole_and_low("_down", [P, DR, 512])
        hT, hL = whole_and_low("_hT", [P, NF, SEQ])
        upH, downH, hH, xH = sb("_upH", [P, UR, 2, KD, P]), sb("_downH", [P, DR, 512]), sb("_hH", [P, NF, SEQ]), sb("_xH", [P, KD, SEQ])
        sg = sb("_sg", [P, 2, SEQ], F32)
        xL = C.xL
        PS = C.PS

        @block.sync
        def _(sp):
            def load_down(e, d):
                sp.wait_ge(s["down_free"], e * ND + d + 1)
                sp.dma_start(down[:, d % DR], wd(e)[:, d % NF, d // NF * 512:(d // NF + 1) * 512]).then_inc(s[f"down{d % DR}"], 16)

            with sp.Fori(0, parts) as e:
                for c in range(NF):
                    r = c % UR
                    before = c - UR + NF if c >= UR else last_user[r]
                    sp.wait_ge(s["up_free"], e * NF + before + 1)
                    sp.dma_start(up[:, r, 0], wg(e)[:, :, c * P:(c + 1) * P]).then_inc(s[f"up{r}"], 16)
                    sp.dma_start(up[:, r, 1], wu(e)[:, :, c * P:(c + 1) * P]).then_inc(s[f"up{r}"], 16)
                    if c >= 2:
                        load_down(e, c - 2)
                for d in range(NF - 2, ND):
                    load_down(e, d)

        @block.tensor
        def _(pe):
            pe.sem_inc(s["up_free"], NF)
            pe.sem_inc(s["down_free"], DR)
            with pe.Fori(0, parts) as e:
                for c in range(NF):
                    r = c % UR
                    pe.wait_ge(s["up_split"], e * NF + c + 1)
                    pe.wait_ge(s["hidden"], e * NF + c + 1)
                    for m in range(2):
                        for k in range(KD):
                            if c == 0 and m == 0:
                                pe.wait_ge(s["xl"], k + 1)
                            ins = split_product(nc, PS[:, 2 * m + c % 2, :], (upH[:, r, m, k], upL[:, r, m, k]),
                                                (xH[:, k], xL[:, k]), k == 0, k == KD - 1)
                        ins.then_inc(s["made"] if m == 0 else s["up_free"], 1)
                for d in range(ND):
                    c = d % NF
                    pe.wait_ge(s["down_split"], e * ND + d + 1)
                    if d < NF:
                        pe.wait_ge(s["h_split"], e * NF + c + 1)
                    for t in range(NT):
                        if c == 0:
                            pe.wait_ge(s["y_taken"], e * 8 + d // NF * NT + t + 1)
                        tok = slice(t * P, (t + 1) * P)
                        ins = split_product(nc, PS[:, 4 + t, :], (hH[:, c, tok], hL[:, c, tok]),
                                            (downH[:, d % DR], downL[:, d % DR]), c == 0, c == NF - 1)
                        if c == NF - 1:
                            ins.then_inc(s["y_made"], 1)
                    if c == NF - 1:
                        pe.wait_ge(s["y_made"], e * 8 + d // NF * NT + NT)
                        pe.sem_inc(s["down_free"], 1)
                    else:
                        ins.then_inc(s["down_free"], 1)

        @block.scalar
        def _(act):
            for k in range(KD):
                nc.scalar.activation(xH[:, k], xnT[:, k], ACT.Copy).then_inc(s["xh"], 1)
            with act.Fori(0, parts) as e:
                def up_high(c):
                    r = c % UR
                    act.wait_ge(s[f"up{r}"], (e * uses[r] + c // UR + 1) * 32)
                    nc.scalar.activation(upH[:, r], up[:, r], ACT.Copy).then_inc(s["up_high"], 1)

                def down_high(d):
                    act.wait_ge(s[f"down{d % DR}"], (e * 2 + d // DR + 1) * 16)
                    nc.scalar.activation(downH[:, d % DR], down[:, d % DR], ACT.Copy).then_inc(s["down_high"], 1)

                def h_high(c):
                    act.wait_ge(s["hidden"], e * NF + c + 3)
                    nc.scalar.activation(hH[:, c], hT[:, c], ACT.Copy).then_inc(s["h_high"], 1)

                up_high(0)
                up_high(1)
                for c in range(NF):
                    if c + 2 < NF:
                        up_high(c + 2)
                    act.wait_ge(s["made"], e * NF + c + 1)
                    act.wait_ge(s["hidden"], e * NF + c + 1)
                    nc.scalar.activation(sg[:, c % 2], PS[:, c % 2, :], ACT.Silu).then_inc(s["silu"], 1)
                    if c >= 1:
                        h_high(c - 1)
                    if c >= 2:
                        down_high(c - 2)
                h_high(NF - 1)
                for d in range(NF - 2, ND):
                    down_high(d)

        @block.vector
        def _(dve):
            dve.sem_inc(s["hidden"], 2)
            dve.sem_inc(s["y_taken"], 4)
            for k in range(KD):
                dve.wait_ge(s["xh"], k + 1)
                nc.vector.tensor_tensor(xL[:, k], xnT[:, k], f32(xH[:, k]), ALU.subtract).then_inc(s["xl"], 1)
            with dve.Fori(0, parts) as e:
                def low(tile, whole, high, need, done):
                    dve.wait_ge(*need)
                    nc.vector.tensor_tensor(tile, whole, f32(high), ALU.subtract).then_inc(done, 1)

                def up_low(c):
                    low(upL[:, c % UR], up[:, c % UR], upH[:, c % UR], (s["up_high"], e * NF + c + 1), s["up_split"])

                def down_low(d):
                    low(downL[:, d % DR], down[:, d % DR], downH[:, d % DR], (s["down_high"], e * ND + d + 1), s["down_split"])

                def h_low(c):
                    low(hL[:, c], hT[:, c], hH[:, c], (s["h_high"], e * NF + c + 1), s["h_split"])

                up_low(0)
                up_low(1)
                for c in range(NF):
                    if c + 2 < NF:
                        up_low(c + 2)
                    dve.wait_ge(s["silu"], e * NF + c + 1)
                    dve.wait_ge(s["up_free"], NF + e * NF + c + 1)
                    nc.vector.tensor_tensor(hT[:, c], sg[:, c % 2], PS[:, 2 + c % 2, :], ALU.mult).then_inc(s["hidden"], 1)
                    if c >= 1:
                        h_low(c - 1)
                    if c >= 3:
                        down_low(c - 3)
                h_low(NF - 1)
                for d in range(NF - 3, ND + 3):
                    if d < ND:
                        down_low(d)
                    h = (d - NF - 2) // NF
                    if d in (NF + 2, ND + 2):
                        for t in range(NT):
                            dve.wait_ge(s["y_made"], e * 8 + h * NT + t + 1)
                            dst = x[:, t, h * 512:(h + 1) * 512]
                            nc.vector.tensor_tensor(dst, PS[:, 4 + t, :], dst, ALU.add).then_inc(s["y_taken"], 1)


I32 = mybir.dt.int32
FAR = 4096.0


def plan_passes(nc, C, name, mem, mask, NE):
    Q = 8 * NT * 2 // 4 if NE == 4 else 2 * NE
    def sb(n, shape, m=mem, dt=F32):
        return m.enter_context(nc.sbuf_tensor(name + n, shape, dt))

    rank, table, slots = sb("_rank", [P, NT, 4 * NE]), sb("_table", [P, 2 * Q + 1], dt=I32), sb("_slots", [P, P])
    with ExitStack() as m2, stage(nc, name, "zeroed counted steps") as (block, s):
        before = sb("_before", [P, P], m2)
        cnt, t, le, qi = sb("_cnt", [P, NE], m2), sb("_t", [P, 4, NE], m2), sb("_le", [P, Q, NE], m2), sb("_qi", [P, Q], m2)
        tf = sb("_tf", [P, 3, Q], m2)
        PS = C.PS

        @block.gpsimd
        def _(pool):
            step = Steps(pool, s["zeroed"])
            step(nc.gpsimd.memset(before[:, :], 1.0))
            step(nc.gpsimd.affine_select(out=before[:, :], in_=before[:, :], compare_op=ALU.is_gt, fill=0.0, base=0,
                                         pattern=[[1, P]], channel_multiplier=-1))
            step(nc.gpsimd.iota(slots[:, :], pattern=[[1, P]], base=0, channel_multiplier=0, allow_small_or_imprecise_dtypes=True))
            step(nc.gpsimd.iota(qi[:, :], pattern=[[1, Q]], base=0, channel_multiplier=0, allow_small_or_imprecise_dtypes=True))

        @block.tensor
        def _(pe):
            pe.wait_ge(s["zeroed"], 4)
            for i in range(NT + 1):
                for j in range(i):
                    nc.tensor.matmul(PS[:, i, 0:NE], C.ones[:, :], mask[:, j], start=j == 0, stop=i == NT and j == NT - 1) \
                        .then_inc(s["counted"], 1)
                if i < NT:
                    nc.tensor.matmul(PS[:, i, 0:NE], before[:, :], mask[:, i], start=i == 0, stop=True).then_inc(s["counted"], 1)

        @block.vector
        def _(dve):
            step = Steps(dve, s["steps"])
            dve.wait_ge(s["zeroed"], 4)
            dve.wait_ge(s["counted"], 2 * NT + NT * (NT - 1) // 2)
            for i in range(NT):
                r0 = rank[:, i, 0:NE]
                step(nc.vector.tensor_scalar(r0, mask[:, i], -FAR, FAR, ALU.mult, ALU.add))
                step(nc.vector.tensor_tensor(r0, r0, PS[:, i, 0:NE], ALU.add))
                for b in range(1, 4):
                    step(nc.vector.tensor_scalar(rank[:, i, b * NE:(b + 1) * NE], r0, -128.0 * b, None, ALU.add))
            step(nc.vector.tensor_copy(cnt[:, :], PS[:, NT, 0:NE]))
            step(nc.vector.tensor_scalar(t[:, 0], cnt[:, :], 0.0, None, ALU.is_gt))
            for b in range(1, 4):
                step(nc.vector.scalar_tensor_tensor(out=t[:, 0], in0=cnt[:, :], scalar=128.0 * b, in1=t[:, 0], op0=ALU.is_gt, op1=ALU.add))
            step(nc.vector.memset(t[:, 2], 1.0))
            step(nc.vector.tensor_tensor_scan(t[:, 1], t[:, 2], t[:, 0], 0.0, ALU.mult, ALU.add))
            full = [P, Q, NE]
            step(nc.vector.tensor_tensor(le[:, :, :], bcast(t[:, 1].unsqueeze(1), full), bcast(qi[:, :].unsqueeze(2), full), ALU.is_le))
            step(nc.vector.tensor_reduce(tf[:, 0], le[:, :, :], AX.X, ALU.add))
            step(nc.vector.tensor_tensor(le[:, :, :], le[:, :, :], bcast(t[:, 0].unsqueeze(1), full), ALU.mult))
            step(nc.vector.tensor_reduce(tf[:, 1], le[:, :, :], AX.X, ALU.add))
            step(nc.vector.tensor_scalar(tf[:, 0], tf[:, 0], NE - 1.0, None, ALU.min))
            step(nc.vector.tensor_tensor(tf[:, 1], qi[:, :], tf[:, 1], ALU.subtract))
            step(nc.vector.tensor_scalar(tf[:, 1], tf[:, 1], 3.0, None, ALU.min))
            step(nc.vector.scalar_tensor_tensor(out=tf[:, 2], in0=tf[:, 1], scalar=float(NE), in1=tf[:, 0], op0=ALU.mult, op1=ALU.add))
            nc.vector.tensor_copy(table[:, 0:Q], tf[:, 0])
            nc.vector.tensor_copy(table[:, Q:2 * Q], tf[:, 2])
            nc.vector.tensor_copy(table[:, 2 * Q:2 * Q + 1], t[:, 1, NE - 1:NE])
    return rank, table, slots, Q


def routed_passes(nc, C, name, x, xs, xnT, gain, plan, NE, F, wg, wu, wd, weights, NW, CUT=1):
    rank, table, slots, Q = plan
    NF = F // P
    chunks = [(f, min(512, F - f)) for f in range(0, F, 512)]
    NC = len(chunks)
    part = F // NW
    pieces = [[(max(f, j * part), min(f + n, (j + 1) * part), j) for j in range(NW) if max(f, j * part) < min(f + n, (j + 1) * part)]
              for f, n in chunks]
    HK = KD // 2
    items = [(m, c, half) for c in range(NC) for m in ("gate", "up") for half in range(2)]
    items += [("down", i, min(2, NF - i)) for i in range(0, NF, 2)]
    NI, R, AHEAD = len(items), 6, 2
    after = lambda offset: {min(4 * c + offset, NI - 1): c for c in range(NC)}
    turn_after, silu_after, hT_high_after, hid_after, hT_low_after = (after(o) for o in (5, 5, 8, 5, 8))
    assert NI % R == 0
    ybank = (2, 3, 1)
    sems = ("issued sel gathered placed xg_high xg pt_made pt high split free silu hid turned hT_high hT_done o_high o_taken y_made y_taken "
            + " ".join(f"loaded{r}" for r in range(R)))
    with ExitStack() as mem, stage(nc, name, sems) as (block, s):
        def sb(n, shape, dt=F32R):
            return mem.enter_context(nc.sbuf_tensor(name + n, shape, dt))

        w, wL = sb("_w", [P, R, HK * 512], F32), low_alias(nc, name + "_w_low", [P, R, HK * 512])
        wH = sb("_wH", [P, R, HK * 512])
        hTH, hTL, OH, OL, xgH = sb("_hTH", [P, NF, P]), sb("_hTL", [P, NF, P]), sb("_OH", [P, DM]), sb("_OL", [P, DM]), sb("_xgH", [P, KD, P])
        sel, cw, selT = sb("_sel", [P, NT, P], F32), sb("_cw", [P, NW], F32), sb("_selT", [P, SEQ])
        xg, xgL = sb("_xg", [P, KD, P], F32), low_alias(nc, name + "_xg_low", [P, KD, P])
        free = xnT[:, :, :].rearrange("p a b -> p (a b)")
        sg, h = (free[:, a:a + 1024].rearrange("p (c f) -> p c f", c=2) for a in (0, 1024))
        PS = C.PS

        def size(i):
            kind, c, n = items[i]
            return n * DM if kind == "down" else HK * chunks[c][1]

        def view(tile, i):
            kind, c, n = items[i]
            return tile[:, i % R, 0:size(i)].rearrange("p (k f) -> p k f", k=n if kind == "down" else HK)

        def passes(eng):
            return eng.value_load(table[0:1, 2 * Q:2 * Q + 1], min_val=1, max_val=Q - 1)

        def expert(eng, q):
            return eng.value_load(table[0:1, bass.ds(q, 1)], min_val=0, max_val=NE - 1)

        @block.sync
        def _(sp):
            def load(q, e, i):
                kind, c, n = items[i]
                if kind == "down":
                    src = wd(e)[:, c:c + n]
                else:
                    src = (wg if kind == "gate" else wu)(e, c)[:, n * HK:(n + 1) * HK]
                sp.wait_ge(s["free"], q * NI + i + 1)
                sp.sem_inc(s["issued"], 1)
                dst = view(w, i)
                for j in range(CUT):
                    if CUT == 1:
                        to, come = dst, src
                    elif kind == "down":
                        to, come = dst[:, j:j + 1], src[:, j:j + 1]
                    else:
                        to, come = dst[:, :, j * 512 // CUT:(j + 1) * 512 // CUT], src[:, :, j]
                    sp.dma_start(to, come).then_inc(s[f"loaded{i % R}"], 16)

            n = passes(sp)
            e = expert(sp, 0)
            for i in range(AHEAD):
                load(0, e, i)
            with sp.Fori(0, n) as q:
                e = expert(sp, q)
                for i in range(AHEAD, NI):
                    load(q, e, i)
                e = expert(sp, q + 1)
                for i in range(AHEAD):
                    load(q + 1, e, i)

        @block.tensor
        def _(pe):
            def gather(q):
                pe.wait_ge(s["sel"], q + 1)
                e = expert(pe, q) if NW == 1 else 0
                for t in range(NT):
                    nc.tensor.matmul(PS[:, 1, 0:NW], sel[:, t], weights(t, e), start=t == 0, stop=t == NT - 1)
                for k in range(KD):
                    for t in range(NT):
                        ins = nc.tensor.matmul(PS[:, 4 + k // 4, k % 4 * P:(k % 4 + 1) * P],
                                               xs[:, t].rearrange("p (m k) -> p k m", k=KD)[:, k], sel[:, t],
                                               start=t == 0, stop=t == NT - 1)
                ins.then_inc(s["gathered"], 1)

            def turn_sel():
                for t in range(NT):
                    ins = nc.tensor.transpose(PS[:, 6, t * P:(t + 1) * P], sel[:, t], C.ident[:, :])
                ins.then_inc(s["pt_made"], 1)

            pe.sem_inc(s["free"], R)
            n = passes(pe)
            gather(0)
            turn_sel()
            with pe.Fori(0, n) as q:
                def turn(c):
                    f, width = chunks[c]
                    pe.wait_ge(s["hid"], q * NC + c + 1)
                    if c >= 2:
                        pe.wait_ge(s["hT_done"], q * NC + c - 1)
                    for i in range(width // P):
                        ins = nc.tensor.transpose(PS[:, 4 + c % 2, i * P:(i + 1) * P], h[:, c % 2, i * P:(i + 1) * P], C.ident[:, :])
                    ins.then_inc(s["turned"], 1)

                pe.wait_ge(s["xg"], q + 1)
                for i, (kind, c, half) in enumerate(items[:4 * NC]):
                    if i == 2:
                        pe.wait_ge(s["y_taken"], q * 8 + 8)
                    m, width = ("gate", "up").index(kind), chunks[c][1]
                    if c >= 2 and i % 4 == 0:
                        pe.wait_ge(s["hid"], q * NC + c - 1)
                    pe.wait_ge(s["split"], q * NI + i + 1)
                    for kk in range(HK):
                        k = half * HK + kk
                        ins = split_product(nc, PS[:, 2 * m + c % 2, 0:width], (xgH[:, k], xgL[:, k]),
                                            (view(wH, i)[:, kk], view(wL, i)[:, kk]), k == 0, k == KD - 1)
                    ins.then_inc(s["free"], 1)
                    if i in turn_after:
                        turn(turn_after[i])
                pe.wait_ge(s["pt"], q + 1)
                for i, (kind, c, n) in enumerate(items[4 * NC:], 4 * NC):
                    pe.wait_ge(s["split"], q * NI + i + 1)
                    for r in range(n):
                        row = c + r
                        pe.wait_ge(s["hT_done"], q * NC + row * P // 512 + 1)
                        for half in range(2):
                            cols = slice(half * 512, (half + 1) * 512)
                            ins = split_product(nc, PS[:, 6 + half, :], (hTH[:, row], hTL[:, row]),
                                                (view(wH, i)[:, r, cols], view(wL, i)[:, r, cols]), row == 0, row == NF - 1)
                    ins.then_inc(s["free"], 1)
                    if i in turn_after:
                        turn(turn_after[i])
                gather(q + 1)
                pe.wait_ge(s["o_taken"], q * 2 + 2)
                for i in range(8):
                    t, half = i // 2, i % 2
                    if i == 2:
                        pe.wait_ge(s["placed"], q + 2)
                    if i >= 3:
                        pe.wait_ge(s["y_taken"], q * 8 + i + 6)
                    for part, O in enumerate((OL, OH)):
                        ins = nc.tensor.matmul(PS[:, ybank[i % 3], :], selT[:, t * P:(t + 1) * P], O[:, half * 512:(half + 1) * 512],
                                               start=part == 0, stop=part == 1)
                    ins.then_inc(s["y_made"], 1)
                turn_sel()

        @block.scalar
        def _(act):
            def high(q, i):
                act.wait_ge(s[f"loaded{i % R}"], (q * (NI // R) + i // R + 1) * 16 * CUT)
                n = size(i)
                nc.scalar.activation(wH[:, i % R, 0:n], w[:, i % R, 0:n], ACT.Copy).then_inc(s["high"], 1)

            def xg_high(q):
                act.wait_ge(s["placed"], q + 1)
                nc.scalar.activation(xgH[:, :, :], xg[:, :, :], ACT.Copy).then_inc(s["xg_high"], 1)

            n = passes(act)
            for i in range(AHEAD):
                high(0, i)
            xg_high(0)
            with act.Fori(0, n) as q:
                act.wait_ge(s["pt_made"], q + 1)
                nc.scalar.activation(selT[:, :], PS[:, 6, :], ACT.Copy).then_inc(s["pt"], 1)

                def place(c):
                    f, width = chunks[c]
                    act.wait_ge(s["turned"], q * NC + c + 1)
                    nc.scalar.activation(hTH[:, f // P:(f + width) // P].rearrange("p a b -> p (a b)"), PS[:, 4 + c % 2, 0:width],
                                         ACT.Copy).then_inc(s["hT_high"], 1)

                for i in range(AHEAD, NI):
                    high(q, i)
                    if i in silu_after:
                        c = silu_after[i]
                        width = chunks[c][1]
                        act.wait_ge(s["free"], q * NI + 4 * c + 2 + R)
                        if c >= 2:
                            act.wait_ge(s["hid"], q * NC + c - 1)
                        nc.scalar.activation(sg[:, c % 2, 0:width], PS[:, c % 2, 0:width], ACT.Silu).then_inc(s["silu"], 1)
                    if i in hT_high_after:
                        place(hT_high_after[i])
                act.wait_ge(s["free"], q * NI + NI + R)
                for half in range(2):
                    nc.scalar.activation(OH[:, half * 512:(half + 1) * 512], PS[:, 6 + half, :], ACT.Copy).then_inc(s["o_high"], 1)
                for i in range(AHEAD):
                    high(q + 1, i)
                xg_high(q + 1)

        @block.vector
        def _(dve):
            def low(q, i):
                dve.wait_ge(s["high"], q * NI + i + 1)
                n = size(i)
                nc.vector.tensor_tensor(wL[:, i % R, 0:n], w[:, i % R, 0:n], f32(wH[:, i % R, 0:n]), ALU.subtract) \
                    .then_inc(s["split"], 1)

            def select(q):
                at = dve.value_load(table[0:1, bass.ds(q + Q, 1)], min_val=0, max_val=4 * NE - 1)
                for t in range(NT):
                    ins = nc.vector.tensor_scalar(sel[:, t], slots[:, :], rank[:, t, bass.ds(at, 1)], None, ALU.is_equal)
                ins.then_inc(s["sel"], 1)

            def place(q):
                dve.wait_ge(s["gathered"], q + 1)
                nc.vector.tensor_copy(cw[:, :], PS[:, 1, 0:NW])
                for i in range(2):
                    ins = nc.vector.tensor_tensor(xg[:, 4 * i:4 * i + 4], PS[:, 4 + i, :].rearrange("p (k c) -> p k c", k=4),
                                                  bcast(gain[:, 4 * i:4 * i + 4].unsqueeze(2), [P, 4, P]), ALU.mult)
                ins.then_inc(s["placed"], 1)

            def xg_low(q):
                dve.wait_ge(s["xg_high"], q + 1)
                nc.vector.tensor_tensor(xgL[:, :, :], xg[:, :, :], f32(xgH[:, :, :]), ALU.subtract).then_inc(s["xg"], 1)

            dve.sem_inc(s["y_taken"], 8)
            n = passes(dve)
            select(0)
            for i in range(AHEAD):
                low(0, i)
            place(0)
            xg_low(0)
            with dve.Fori(0, n) as q:
                def hT_low(c):
                    f, width = chunks[c]
                    dve.wait_ge(s["hT_high"], q * NC + c + 1)
                    tiles = slice(f // P, (f + width) // P)
                    nc.vector.tensor_tensor(hTL[:, tiles].rearrange("p a b -> p (a b)"), PS[:, 4 + c % 2, 0:width],
                                            f32(hTH[:, tiles]).rearrange("p a b -> p (a b)"), ALU.subtract).then_inc(s["hT_done"], 1)

                dve.wait_ge(s["placed"], q + 1)
                for i in range(AHEAD, NI):
                    low(q, i)
                    if i in hid_after:
                        c = hid_after[i]
                        dve.wait_ge(s["silu"], q * NC + c + 1)
                        dve.wait_ge(s["free"], q * NI + 4 * c + 4 + R)
                        if c >= 2:
                            dve.wait_ge(s["turned"], q * NC + c - 1)
                        for a, b, j in pieces[c]:
                            f = slice(a - chunks[c][0], b - chunks[c][0])
                            ins = nc.vector.scalar_tensor_tensor(out=h[:, c % 2, f], in0=sg[:, c % 2, f], scalar=cw[:, j:j + 1],
                                                                 in1=PS[:, 2 + c % 2, f], op0=ALU.mult, op1=ALU.mult)
                        ins.then_inc(s["hid"], 1)
                    if i in hT_low_after:
                        hT_low(hT_low_after[i])
                dve.wait_ge(s["pt_made"], q + 1)
                select(q + 1)
                for half in range(2):
                    cols = slice(half * 512, (half + 1) * 512)
                    dve.wait_ge(s["o_high"], q * 2 + half + 1)
                    nc.vector.tensor_tensor(OL[:, cols], PS[:, 6 + half, :], f32(OH[:, cols]), ALU.subtract).then_inc(s["o_taken"], 1)
                for i in range(AHEAD):
                    low(q + 1, i)
                place(q + 1)
                for i in range(8):
                    t, half = i // 2, i % 2
                    dve.wait_ge(s["y_made"], q * 8 + i + 1)
                    dst = x[:, t, half * 512:(half + 1) * 512]
                    nc.vector.tensor_tensor(dst, PS[:, ybank[i % 3], :], dst, ALU.add).then_inc(s["y_taken"], 1)
                    if i == 1:
                        xg_low(q + 1)


class Consts:
    pass


def make_consts(nc, mem):
    C = Consts()
    C.PS = mem.enter_context(nc.psum_tensor("PS", [P, 8, 512], F32))
    C.ident = mem.enter_context(nc.sbuf_tensor("ident", [P, P], F32))
    C.ones = mem.enter_context(nc.sbuf_tensor("ones", [P, P], F32))
    C.ones64 = mem.enter_context(nc.sbuf_tensor("ones64", [P, P], F32))
    C.causal = mem.enter_context(nc.sbuf_tensor("causal", [P, P], F32))
    C.one = mem.enter_context(nc.sbuf_tensor("one", [P, 1], F32))
    with stage(nc, "consts", "zeroed") as (block, s):
        @block.gpsimd
        def _(pool):
            step = Steps(pool, s["zeroed"])
            for tile, value in ((C.ones, 1.0), (C.one, 1.0), (C.ident, 0.0), (C.causal, 0.0), (C.ones64, 0.0)):
                step(nc.gpsimd.memset(tile[:, :], value))
            for a in (0, 64):
                step(nc.gpsimd.memset(C.ones64[a:a + 64, a:a + 64], 1.0))
            step(nc.gpsimd.affine_select(out=C.ident[:, :], in_=C.ident[:, :], compare_op=ALU.not_equal, fill=1.0,
                                         base=0, pattern=[[-1, P]], channel_multiplier=1))
            step(nc.gpsimd.affine_select(out=C.causal[:, :], in_=C.causal[:, :], compare_op=ALU.is_ge, fill=NEG,
                                         base=0, pattern=[[-1, P]], channel_multiplier=1))
    return C


def column(ap):
    return ap.rearrange("(p o) -> p o", o=1)


Q0, KC0, VC0, KS0, VS0, KW0, VW0, GT0, CQ0, CKV0, KR0, EV_W = (
    0, 512, 640, 768, 896, 1024, 1152, 1280, 1304, 1560, 1688, 1720)
NH, HD = 8, 64
CMP_L, CMP_S = 32, 16
NCMP = (SEQ - CMP_L) // CMP_S + 1
MQK, ROT = 96, 32
BUCKETS = 32
REV_ZERO, FWD_ZERO = 2 * P - 1, 527


def bucket_table():
    n = np.arange(SEQ)
    large = 16 + (np.log(np.maximum(n, 16).astype(np.float32) / np.float32(16)) / np.float32(math.log(8.0))
                  * np.float32(16)).astype(np.int32)
    bucket = np.where(n < 16, n, np.minimum(large, BUCKETS - 1))
    d = np.concatenate([REV_ZERO - np.arange(SEQ), np.arange(2 * SEQ) - FWD_ZERO])
    seen = (d >= 0) & (d < SEQ)
    table = np.zeros((BUCKETS + 1, d.size), np.float32)
    table[bucket[d[seen]], np.nonzero(seen)[0]] += 1.0
    table[BUCKETS - 1, seen] -= 1.0
    table[BUCKETS, d < 0] = NEG
    return table


def rope_tables():
    half = ROT // 2
    inv = (np.float32(10000.0) ** (-np.arange(half, dtype=np.float32) / np.float32(half))).astype(np.float32)
    ang = np.arange(SEQ, dtype=np.float32)[None, :] * inv[:, None]
    turn = np.zeros((ROT, ROT), np.float32)
    for m in range(half):
        turn[m + half, m] = -1.0
        turn[m, m + half] = 1.0
    return np.stack([np.tile(np.cos(ang), (2, 1)), np.tile(np.sin(ang), (2, 1))]).astype(np.float32), turn


def mixer_even(nc, C, D, x, xnT):
    with ExitStack() as mem:
        def sb(name, shape, m=mem):
            return m.enter_context(nc.sbuf_tensor("ev_" + name, shape, F32))

        yT = sb("yT", [P, 8, SEQ])
        yL = low_alias(nc, "ev_yT_low", [P, 8, SEQ])
        q = sb("q", [P, 4, SEQ])
        ks, kw = sb("ks", [P, SEQ]), sb("kw", [P, SEQ])
        vsw = sb("vsw", [P, NT, 2, P])
        gate = sb("gate", [P, NT, 3 * NH])
        cq6 = sb("latent", [P, 4, SEQ])
        cq, ckv, kr = cq6[:, 0:2], cq6[:, 2], cq6[:, 3]
        uq, ukv = sb("uq", [P, 2, NH * MQK]), sb("ukv", [P, NH * P])
        vblk = sb("vblk", [P, 2, 4, HD])
        pcT = sb("pcT", [P, 2, SEQ])
        T = sb("T", [P, NH, 2 * P])
        ring = low_alias(nc, "ev_ring", [P, 2, KD, P])
        TcT = sb("TcT", [P, 2, SEQ])
        relb = sb("relb", [BUCKETS + 1, NH])
        gx, gq, gk, gcq, gckv, gmq, gmk = (sb(n, [P, w]) for n, w in (
            ("gx", KD), ("gq", 1), ("gk", 3), ("gcq", 2), ("gckv", 1), ("gmq", 1), ("gmk", 1)))
        loaded = {n: nc.alloc_semaphore("ev_loaded_" + n) for n in "gx small x tables scratch bias w0 w1 w2 w3 w4 cmp mla rope".split()}
        pieces = [(Q0, KC0), (KC0, KS0), (KS0, KW0), (KW0, CQ0), (CQ0, EV_W)]
        with ExitStack() as memB:
            kc, vc = sb("kc", [P, SEQ], memB), sb("vc", [P, SEQ], memB)
            X = sb("X", [P, 2, 16, 2, 32], memB)
            w1, w2, pos = sb("w1", [P, 2, 16, 256], memB), sb("w2", [P, 2, 2, P], memB), sb("pos", [P, 2, 16], memB)
            hid, kcT = sb("hid", [P, 2, 2, 64], memB), sb("kcT", [P, 64], memB)
            pair, hid4 = sb("pair", [P, 2, P], memB), sb("hid4", [P, 2, 2, 4, 32], memB)
            E = q[:, :, :].rearrange("p a b -> p (a b)")[0:BUCKETS + 1, 0:3 * SEQ]
            with ExitStack() as memW:
                W = sb("W", [P, KD, EV_W], memW)
                WL = low_alias(nc, "ev_W_low", [P, KD, EV_W])
                win = D["ev_w_in"][0].rearrange("(p k) n -> p k n", k=KD)
                small = 0

                def load_weights(sp):
                    sp.dma_start(E, D["bucket_table"]).then_inc(loaded["tables"], 16)
                    sp.dma_start(relb[0:BUCKETS, :], D["rel_bias"]).then_inc(loaded["tables"], 16)
                    sp.dma_start(relb[BUCKETS:BUCKETS + 1, :], D["ones_row"]).then_inc(loaded["tables"], 16)
                    for i in (2, 3, 4):
                        a, b = pieces[i]
                        sp.dma_start(W[:, :, a:b], win[:, :, a:b]).then_inc(loaded[f"w{i}"], 16)
                    for i in range(2):
                        dst = W[:, :, 0:KC0].rearrange("p k (j s d) -> p k j s d", s=2, d=HD)[:, :, :, i]
                        for k in range(KD):
                            sp.dma_start(dst[:, k], win[:, k, i * 256:(i + 1) * 256].rearrange("p (j d) -> p j d", d=HD)) \
                                .then_inc(loaded["w0"], 16)
                    a, b = pieces[1]
                    sp.dma_start(W[:, :, a:b], win[:, :, a:b]).then_inc(loaded["w1"], 16)

                def load_rest(sp):
                    nonlocal small
                    smalls = [(gcq[:, :], D["mla_cq_norm"][0].rearrange("(k p) -> p k", p=P)),
                              (gckv[:, :], column(D["mla_ckv_norm"][0])),
                              (gmq[0:MQK, :], column(D["mla_q_norm"][0])),
                              (gmk[0:MQK, :], column(D["mla_k_norm"][0]))]
                    for a in (0, HD):
                        smalls += [(gq[a:a + HD, :], column(D["nsa_q_norm"][0])),
                                   (gk[a:a + HD, :], D["nsa_k_norm"][0].rearrange("i p -> p i"))]
                    for v in range(2):
                        smalls += [(pos[:, v], D["nsa_cmp_pos"][0, v].rearrange("(j a) d -> (a d) j", a=2))]
                    for dst, src in smalls:
                        sp.dma_start(dst, src, allow_slow_non_contiguous=True).then_inc(loaded["small"], 16)
                    small = 16 * len(smalls)
                    for v in range(2):
                        sp.dma_start(w1[:, v], D["nsa_cmp_w1"][0, v].rearrange("(j p) n -> p j n", p=P)).then_inc(loaded["cmp"], 16)
                        for a in (0, HD):
                            sp.dma_start(w2[:, v, :, a:a + HD], D["nsa_cmp_w2"][0, v].rearrange("(a p) n -> p a n", p=P)).then_inc(loaded["cmp"], 16)
                    sp.dma_start(uq[:, :, :], D["mla_w_uq"][0].rearrange("(k p) n -> p k n", p=P)).then_inc(loaded["mla"], 16)
                    sp.dma_start(ukv[:, :], D["mla_w_ukv"][0]).then_inc(loaded["mla"], 16)

                with stage(nc, "ev_load", "zeroed") as (block, s):
                    @block.sync
                    def _(sp):
                        sp.dma_start(gx[:, :], D["ev_mix_norm"][0].rearrange("(p k) -> p k", k=KD)).then_inc(loaded["gx"], 16)
                        sp.dma_start(x[:, :, :], D["x"][0].rearrange("(t p) d -> p t d", p=P)).then_inc(loaded["x"], 16)
                        sp.wait_ge(loaded["x"], 16)

                    @block.gpsimd
                    def _(pool):
                        step = Steps(pool, s["zeroed"])
                        step(nc.gpsimd.memset(X[:, :, :, :, :], 0.0))
                        step(nc.gpsimd.memset(vblk[:, :, :, :], 0.0))

                with stage(nc, "ev_wait", "x") as (block, s):
                    @block.vector
                    def _(dve):
                        dve.wait_ge(loaded["gx"], 16)
                        dve.wait_ge(loaded["x"], 16)

                norm_transpose(nc, C, x, gx, xnT, yT[:, :, :].rearrange("p (t a) b -> p t (a b)", a=2), "ev_norm", load_weights)

                scratch = nc.dram_tensor("bias_by_distance", [NH, 3 * SEQ], F32, kind="Internal").ap()
                with stage(nc, "ev_bias", "made copied") as (block, s):
                    PS = C.PS
                    by_head = cq6[0:NH, 0:3]

                    @block.tensor
                    def _(pe):
                        pe.wait_ge(loaded["tables"], 48)
                        for i in range(3):
                            nc.tensor.matmul(PS[0:NH, i, :], relb[:, :], E[:, i * SEQ:(i + 1) * SEQ], start=True, stop=True) \
                                .then_inc(s["made"], 1)

                    @block.vector
                    def _(dve):
                        dve.wait_ge(s["made"], 3)
                        for i in range(3):
                            ins = nc.vector.tensor_copy(by_head[:, i], PS[0:NH, i, :])
                        ins.then_inc(s["copied"], 1)

                    @block.sync
                    def _(sp):
                        sp.wait_ge(s["copied"], 1)
                        sp.dma_start(scratch, by_head.rearrange("p a b -> p (a b)")).then_inc(loaded["scratch"], 16)
                        sp.wait_ge(loaded["scratch"], 16)
                        for h in range(NH):
                            src = bass.AP(scratch.tensor, h * 3 * SEQ + SEQ + FWD_ZERO - (CMP_L - 1) - 31 * CMP_S, [[CMP_S, 32], [1, SEQ]])
                            sp.dma_start(TcT[h % 4 * 32:h % 4 * 32 + 32, h // 4], src).then_inc(loaded["bias"], 16)

                def features(a, dst, piece):
                    jobs.append((W[:, :, a:a + P], WL[:, :, a:a + P], copy_to(nc, dst),
                                 [(loaded[f"w{piece}"], 16 if piece else 32 * KD)]))

                def take_vw(t):
                    def f(ps, steps):
                        nc.vector.tensor_copy(vsw[:, t, 1], ps[:, 0:P])
                        return nc.vector.tensor_copy(gate[:, t], ps[:, P:P + 3 * NH])
                    return f

                jobs, plain = [], []
                for t in range(NT):
                    tok = slice(t * P, (t + 1) * P)
                    plain.append(([(xnT[:, k, tok], W[:, k, VS0:VS0 + P]) for k in range(KD)], slice(0, P), slice(0, P),
                                  copy_to(nc, vsw[:, t, 0]), [(loaded["w2"], 16)]))
                    plain.append(([(xnT[:, k, tok], W[:, k, VW0:VW0 + P + 3 * NH]) for k in range(KD)], slice(0, P),
                                  slice(0, P + 3 * NH), take_vw(t), [(loaded["w3"], 16)]))
                plain.append(([(W[:, k, KR0:KR0 + ROT], xnT[:, k]) for k in range(KD)], slice(64, 96), slice(0, SEQ),
                              copy_to(nc, kr[64:96, :]), [(loaded["w4"], 16)]))
                for a, dst, piece in ((KS0, ks[:, :], 2), (KW0, kw[:, :], 3), (CQ0, cq[:, 0], 4), (CQ0 + P, cq[:, 1], 4), (CKV0, ckv, 4)):
                    features(a, dst, piece)
                for j in range(4):
                    features(j * P, q[:, j], 0)
                for a, dst in ((KC0, kc), (VC0, vc)):
                    features(a, dst[:, :], 1)
                split_features(nc, C, "ev_in", xnT, C.xL, yL, jobs, plain, loads=load_rest, wH=ring)

            with stage(nc, "ev_gains", "scaled") as (block, s):
                @block.vector
                def _(dve):
                    dve.wait_ge(loaded["small"], small)
                    nc.vector.tensor_scalar(gq[:, :], gq[:, :], float(HD) ** -0.5, None, ALU.mult)
                    nc.vector.tensor_scalar(gmq[0:MQK, :], gmq[0:MQK, :], float(MQK) ** -0.5, None, ALU.mult)
                    for g in range(2):
                        nc.vector.tensor_copy(pair[:, g].rearrange("p (a d) -> p a d", a=2),
                                              bcast(C.ident[:, g * HD:(g + 1) * HD].unsqueeze(1), [P, 2, HD]))

            groups = [dict(src=[q[:, j]], gain=[gq[:, 0:1]], dst=[q[:, j]], ones=C.ones64[:, :], n=HD) for j in range(4)]
            groups += [dict(src=[k[:, :]], gain=[gk[:, i:i + 1]], dst=[k[:, :]], ones=C.ones64[:, :], n=HD)
                       for k, i in ((ks, 1), (kw, 2))]
            groups += [dict(src=[cq[:, 0], cq[:, 1]], gain=[gcq[:, 0:1], gcq[:, 1:2]], dst=[cq[:, 0], cq[:, 1]],
                            ones=C.ones[:, :], n=2 * P),
                       dict(src=[ckv], gain=[gckv[:, 0:1]], dst=[ckv], ones=C.ones[:, :], n=P)]
            norm_features(nc, C, "ev_norms", groups)

            flip, flip32 = yT[:, 0, 0:P], yT[:, 0, P:2 * P]
            Tr = xnT[:, 0:4].rearrange("p k (a c) -> p (k a) c", c=2 * P)
            def take_X(v, g):
                def f(ps, steps):
                    for a in range(2):
                        h = slice(a * HD, (a + 1) * HD)
                        src = ps[h].rearrange("p (c j a) -> p j c a", j=8, a=2)
                        for jh in range(2):
                            js = slice(8 * jh, 8 * jh + 8)
                            ins = nc.vector.tensor_tensor(X[h, v, js, g, 0:NCMP], src[:, :, jh:jh + NCMP, a],
                                                          bcast(pos[h, v, js].unsqueeze(2), [HD, 8, NCMP]), ALU.add)
                    return ins
                return f

            products(nc, C, "ev_X", [([(pair[:, g], (kc, vc)[v][:, :])], slice(0, P),
                                      slice(0, SEQ), take_X(v, g)) for v in range(2) for g in range(2)],
                     loads=lambda sp: sp.dma_start(
                         Tr, bass.AP(scratch.tensor, REV_ZERO - (2 * P - 1), [[1, P], [3 * SEQ, NH], [1, 2 * P]])
                     ).then_inc(loaded["bias"], 16))
            products(nc, C, "ev_hid", [([(w1[:, v, j, a * P:(a + 1) * P], X[:, v, j].rearrange("p g c -> p (g c)")) for j in range(16)],
                                        slice(0, P), slice(0, 64), copy_to(nc, hid[:, v, a])) for v in range(2) for a in range(2)],
                     lambda n: [(loaded["cmp"], 96)] if n == 0 else [])
            with stage(nc, "ev_gelu", "gelu sigmoid steps") as (block, s):
                @block.scalar
                def _(act):
                    nc.scalar.activation(hid[:, :, :, :], hid[:, :, :, :], ACT.Gelu_apprx_tanh).then_inc(s["gelu"], 1)
                    nc.scalar.activation(gate[:, :, :], gate[:, :, :], ACT.Sigmoid).then_inc(s["sigmoid"], 1)

                @block.vector
                def _(dve):
                    dve.wait_ge(s["gelu"], 1)
                    for a in range(2):
                        for g in range(2):
                            nc.vector.tensor_copy(hid4[:, a, g], bcast(hid[:, 1, a, g * 32:g * 32 + 32].unsqueeze(1), [P, 4, 32]))

                @block.gpsimd
                def _(pool):
                    step = Steps(pool, s["steps"])
                    for tile in (flip, flip32):
                        step(nc.gpsimd.memset(tile, 0.0))
                    step(nc.gpsimd.affine_select(out=flip, in_=flip, compare_op=ALU.not_equal, fill=1.0,
                                                 base=-(P - 1), pattern=[[1, P]], channel_multiplier=1))
                    step(nc.gpsimd.affine_select(out=flip32, in_=flip32, compare_op=ALU.not_equal, fill=1.0,
                                                 base=-31, pattern=[[-32, 4], [1, 32]], channel_multiplier=1))
                    pool.wait_ge(s["sigmoid"], 1)
                    g0 = gate[:, 0].rearrange("p (h b) -> p h b", b=3)[:, :, 0]
                    nc.gpsimd.affine_select(out=g0, in_=g0, compare_op=ALU.is_ge, fill=0.0, base=-(CMP_L - 1),
                                            pattern=[[0, NH]], channel_multiplier=1)

            def take_vblk(g):
                def f(ps, steps):
                    for h in range(4):
                        ins = nc.vector.tensor_copy(vblk[32 * h:32 * h + 32, g, h], ps[32 * h:32 * h + 32])
                    return ins
                return f

            jobs = [([(w2[:, 0, a], hid[:, 0, a]) for a in range(2)], slice(0, P), slice(0, 64), copy_to(nc, kcT[:, :]))]
            jobs += [([(hid4[:, a, g].rearrange("p r c -> p (r c)"), w2[:, 1, a, 0:HD]) for a in range(2)], slice(0, P), slice(0, HD),
                      take_vblk(g)) for g in range(2)]
            jobs += [([(flip, Tr[:, i:i + 2].rearrange("p a b -> p (a b)"))], slice(0, P), slice(0, SEQ),
                      copy_to(nc, T[:, i:i + 2].rearrange("p a b -> p (a b)"))) for i in range(0, NH, 2)]
            products(nc, C, "ev_cmp", jobs, lambda n: [(loaded["bias"], 16 * (NH + 1))] if n == 0 else [])
            norm_features(nc, C, "ev_kc", [dict(src=[kcT[:, :]], gain=[gk[:, 0:1]], dst=[kcT[:, :]], ones=C.ones64[:, :], n=HD)])

            with ExitStack() as m2, stage(nc, "ev_pc", "scored steps exped turned") as (block, s):
                sc = sb("sc", [P, NT, NH, 32], m2)
                mx = sb("mx", [P, 3, NT, NH], m2)
                PS = C.PS

                @block.tensor
                def _(pe):
                    pe.wait_ge(loaded["bias"], 16 * (NH + 1))
                    for t in range(NT):
                        for h in range(NH):
                            g = h // 4
                            if h % 4 == 0:
                                nc.tensor.matmul(PS[:, 4 * g + t, 0:P], TcT[:, g, t * P:(t + 1) * P], flip32, start=True, stop=False)
                            half = slice(g * HD, (g + 1) * HD)
                            ins = nc.tensor.matmul(PS[:, 4 * g + t, h % 4 * 32:(h % 4 + 1) * 32], q[half, h % 4, t * P:(t + 1) * P],
                                                   kcT[half, g * 32:(g + 1) * 32], start=False, stop=h % 4 == 3)
                            if h % 4 == 3:
                                ins.then_inc(s["scored"], 1)
                    pe.wait_ge(s["steps"], 2 * NT + 7)
                    for t in range(NT):
                        for g in range(2):
                            rows = sc[:, t, 4 * g:4 * g + 4].rearrange("p h c -> p (h c)")
                            nc.tensor.transpose(PS[:, g, t * P:(t + 1) * P], rows, C.ident[:, :]).then_inc(s["turned"], 1)

                @block.scalar
                def _(act):
                    act.wait_ge(s["steps"], 2 * NT + 3)
                    nc.scalar.activation(sc[:, :, :, :], sc[:, :, :, :], ACT.Exp).then_inc(s["exped"], 1)

                @block.vector
                def _(dve):
                    step = Steps(dve, s["steps"])
                    for t in range(NT):
                        for g in range(2):
                            hs = slice(4 * g, 4 * g + 4)
                            dve.wait_ge(s["scored"], 2 * t + g + 1)
                            step(nc.vector.tensor_copy(sc[:, t, hs].rearrange("p h c -> p (h c)"), PS[:, 4 * g + t, 0:P]))
                    rows = sc[:, :, :, :].rearrange("p t h c -> p (t h) c")
                    m = [mx[:, i].rearrange("p t h -> p (t h)") for i in range(3)]
                    step(nc.vector.tensor_reduce(m[0], rows, AX.X, ALU.max))
                    step(nc.vector.tensor_tensor(rows, rows, bcast(m[0].unsqueeze(2), [P, NT * NH, 32]), ALU.subtract))
                    dve.sem_inc(s["steps"], 1)
                    step.n += 1
                    dve.wait_ge(s["exped"], 1)
                    step(nc.vector.tensor_reduce(m[1], rows, AX.X, ALU.add))
                    step(nc.vector.reciprocal(m[2], m[1]))
                    g0 = gate[:, :, :].rearrange("p t (h b) -> p (t h) b", b=3)[:, :, 0]
                    step(nc.vector.tensor_tensor(m[2], m[2], g0, ALU.mult))
                    step(nc.vector.tensor_tensor(rows, rows, bcast(m[2].unsqueeze(2), [P, NT * NH, 32]), ALU.mult))
                    dve.wait_ge(s["turned"], 2 * NT)
                    nc.vector.tensor_copy(pcT[:, :, :], PS[:, 0:2, :])

        cosT, sinT, turn = sb("cos", [P, SEQ]), sb("sin", [P, SEQ]), sb("turn", [P, ROT])
        qz = xnT
        with stage(nc, "ev_out_load", "x") as (block, s):
            @block.gpsimd
            def _(pool):
                nc.gpsimd.memset(qz[HD:P, 0:4], 0.0)

            @block.scalar
            def _(act):
                nc.scalar.activation(qz[0:HD, 0:4], q[0:HD], ACT.Copy)

            @block.vector
            def _(dve):
                nc.vector.memset(qz[0:HD, 4:8], 0.0)
                nc.vector.tensor_copy(qz[HD:P, 4:8], q[HD:P])

            @block.sync
            def _(sp):
                for dst, src in ((cosT[64:96, :], D["rope_table"][0]), (sinT[64:96, :], D["rope_table"][1]),
                                 (turn[64:96, :], D["rope_turn"])):
                    sp.dma_start(dst, src).then_inc(loaded["rope"], 16)

        jobs = []
        for m in range(NH // 2):
            for br, k in enumerate((ks, kw)):
                for h in (2 * m, 2 * m + 1):
                    g, half = h // 4, slice(h // 4 * HD, (h // 4 + 1) * HD)
                    jobs.append(dict(q=qz[:, h], k=k[:, :], v=lambda kb, br=br, half=half: vsw[:, kb, br, half],
                                     bias=T[:, h], extra=None, gate=lambda i, h=h, br=br: gate[:, i, 3 * h + 1 + br:3 * h + 2 + br],
                                     first=(vblk[:, g, h % 4], pcT[:, g]) if br == 0 else None, start=br == 0, stop=br == 1,
                                     rows=slice(h % 2 * HD, (h % 2 + 1) * HD), bank=m % 2, out=yT[:, m]))
        attention(nc, C, "ev_nsa", jobs)

        with ExitStack() as m3:
            km, vm = sb("km", [MQK, NH, SEQ], m3), sb("vm", [P, NT, 512], m3)
            qm = xnT[0:MQK]

            def take_k(h):
                def f(ps, steps):
                    nc.vector.tensor_copy(km[64:96, h], kr[64:96, :])
                    return nc.vector.tensor_copy(km[0:64, h], ps)
                return f

            jobs = []
            for h in range(NH):
                jobs.append(([(uq[:, k, MQK * h:MQK * (h + 1)], cq[:, k]) for k in range(2)], slice(0, MQK), slice(0, SEQ),
                             copy_to(nc, qm[:, h])))
                jobs.append(([(ukv[:, P * h:P * h + HD], ckv)], slice(0, HD), slice(0, SEQ), take_k(h)))
            vcols = ukv[:, :].rearrange("p (h d) -> p h d", d=P)[:, :, HD:P]
            for t in range(NT):
                jobs.append(([(ckv[:, t * P:(t + 1) * P], vcols)], slice(0, P), slice(0, SEQ), copy_to(nc, vm[:, t])))
            products(nc, C, "ev_mla_in", jobs, lambda n: [(loaded["mla"], 32)] if n == 0 else [])
            norm_features(nc, C, "ev_mla_norm", [
                dict(src=[t[0:MQK, h]], gain=[g[0:MQK, 0:1]], dst=[t[0:MQK, h]], ones=C.ones[0:MQK, 0:MQK], n=MQK)
                for h in range(NH) for t, g in ((qm, gmq), (km, gmk))])

            with stage(nc, "ev_rope", "turned steps") as (block, s):
                r = slice(64, 96)
                tiles = [t[r, h] for h in range(NH) for t in (qm, km)]
                PS = C.PS

                @block.tensor
                def _(pe):
                    pe.wait_ge(loaded["rope"], 48)
                    for n, tile in enumerate(tiles):
                        if n >= 8:
                            pe.wait_ge(s["steps"], 3 * (n - 7))
                        nc.tensor.matmul(PS[r, n % 8, :], turn[r, :], tile, start=True, stop=True).then_inc(s["turned"], 1)

                @block.vector
                def _(dve):
                    step = Steps(dve, s["steps"])
                    dve.wait_ge(loaded["rope"], 48)
                    for n, tile in enumerate(tiles):
                        dve.wait_ge(s["turned"], n + 1)
                        step(nc.vector.tensor_tensor(tile, tile, cosT[r, :], ALU.mult))
                        step(nc.vector.tensor_tensor(PS[r, n % 8, :], PS[r, n % 8, :], sinT[r, :], ALU.mult))
                        step(nc.vector.tensor_tensor(tile, tile, PS[r, n % 8, :], ALU.add))

            jobs = []
            for h in range(NH):
                jobs.append(dict(q=qm[:, h], k=km[:, h], v=lambda kb, h=h: vm[:, kb, h * HD:(h + 1) * HD],
                                 bias=C.causal[:, :], extra=None, gate=None, first=None, start=True, stop=True,
                                 rows=slice(h % 2 * HD, (h % 2 + 1) * HD), bank=h // 2 % 2, out=yT[:, 4 + h // 2]))
            attention(nc, C, "ev_mla", jobs)
        wout = sb("wout", [P, 8, DM])
        woutL = low_alias(nc, "ev_wout_low", [P, 8, DM])
        add_projection(nc, C, "ev_out", yT, yL, wout, woutL, x, D["ev_w_out"][0].rearrange("(k p) n -> p k n", p=P))
        nc.clear_and_free_semaphores(list(loaded.values()))
        nc.all_engine_barrier(sem_only=True)


def mixer_odd(nc, C, D, x, xnT):
    TAPS = 3
    with ExitStack() as mem:
        def sb(name, shape, m=mem):
            return m.enter_context(nc.sbuf_tensor("od_" + name, shape, F32))

        yT = sb("yT", [P, 8, SEQ])
        yL = low_alias(nc, "od_yT_low", [P, 8, SEQ])
        gx, taps = sb("gx", [P, KD]), sb("taps", [P, TAPS, 8])
        memW = mem.enter_context(ExitStack())
        cg, cu, conv = sb("cg", [P, SEQ], memW), sb("cu", [P, 2, SEQ + TAPS - 1], memW), sb("conv", [P, 2, SEQ], memW)
        W = sb("W", [P, KD, 3 * DM], memW)
        WL = low_alias(nc, "od_W_low", [P, KD, 3 * DM])
        xH = memW.enter_context(nc.sbuf_tensor("od_xH", [P, KD, SEQ], F32R))
        loaded = {n: nc.alloc_semaphore("od_loaded_" + n) for n in "gx small w0 w1 w2 w3".split()}
        win = D["od_w_in"][0].rearrange("(p k) (s n) -> p k s n", k=KD, s=3)
        def load_piece(sp, i):
            for part in range(3):
                sp.dma_start(W[:, :, part * DM + i * 256:part * DM + i * 256 + 256],
                             win[:, :, part, i * 256:i * 256 + 256]).then_inc(loaded[f"w{i}"], 16)

        def load_first(sp):
            load_piece(sp, 0)
            for tap in range(TAPS):
                sp.dma_start(taps[:, tap], D["conv_w"][0, tap].rearrange("(j p) -> p j", p=P),
                             allow_slow_non_contiguous=True).then_inc(loaded["small"], 16)

        def load_rest(sp):
            for i in range(1, 4):
                load_piece(sp, i)

        with stage(nc, "od_load", "zeroed") as (block, s):
            @block.sync
            def _(sp):
                sp.dma_start(gx[:, :], D["od_mix_norm"][0].rearrange("(p k) -> p k", k=KD)).then_inc(loaded["gx"], 16)

            @block.vector
            def _(dve):
                nc.vector.memset(cu[:, :, 0:TAPS - 1], 0.0)

        norm_transpose(nc, C, x, gx, xnT, yT[:, :, :].rearrange("p (t a) b -> p t (a b)", a=2), "od_norm",
                       load_first, (loaded["gx"], 16))

        def take_cu(j):
            def f(ps, steps):
                if j == 0:
                    steps.eng.wait_ge(loaded["small"], 16 * TAPS)
                steps(nc.vector.tensor_tensor(cu[:, j % 2, TAPS - 1:], cg[:, :], ps, ALU.mult))
                steps(nc.vector.tensor_scalar(conv[:, j % 2], cu[:, j % 2, 0:SEQ], taps[:, 0, j:j + 1], None, ALU.mult))
                for i in range(1, TAPS - 1):
                    steps(nc.vector.scalar_tensor_tensor(out=conv[:, j % 2], in0=cu[:, j % 2, i:i + SEQ], scalar=taps[:, i, j:j + 1],
                                                         in1=conv[:, j % 2], op0=ALU.mult, op1=ALU.add))
                i = TAPS - 1
                return nc.vector.scalar_tensor_tensor(out=conv[:, j % 2], in0=cu[:, j % 2, i:i + SEQ], scalar=taps[:, i, j:j + 1],
                                                      in1=conv[:, j % 2], op0=ALU.mult, op1=ALU.add)
            return f

        jobs = []
        for j in range(8):
            for part, take in ((1, copy_to(nc, cg[:, :])), (2, take_cu(j)),
                               (0, lambda ps, steps, j=j: nc.vector.tensor_tensor(yT[:, j], ps, conv[:, j % 2], ALU.mult))):
                a = part * DM + j * P
                jobs.append((W[:, :, a:a + P], WL[:, :, a:a + P], take, [(loaded[f"w{j // 2}"], 48)]))
        split_features(nc, C, "od_in", xnT, C.xL, xH, jobs, chained=True, loads=load_rest)
        memW.close()
        wout = sb("wout", [P, 8, DM])
        woutL = low_alias(nc, "od_wout_low", [P, 8, DM])
        add_projection(nc, C, "od_out", yT, yL, wout, woutL, x, D["od_w_out"][0].rearrange("(k p) n -> p k n", p=P))
        nc.clear_and_free_semaphores(list(loaded.values()))
        nc.all_engine_barrier(sem_only=True)


def first_max(nc, step, scores, index, low, top, at, hit, shape):
    step(nc.vector.tensor_reduce(top, scores, AX.X, ALU.max))
    step(nc.vector.tensor_tensor(hit, scores, bcast(top.unsqueeze(2), shape), ALU.is_equal))
    step(nc.vector.scalar_tensor_tensor(out=hit, in0=hit, scalar=-16.0, in1=index, op0=ALU.mult, op1=ALU.add))
    step(nc.vector.tensor_reduce(at, hit, AX.X, ALU.min))
    step(nc.vector.tensor_tensor(hit, low, bcast(at.unsqueeze(2), shape), ALU.is_equal))


def make_index(nc, name, mem, n):
    index, low = (mem.enter_context(nc.sbuf_tensor(name + s, [P, NT, n], F32)) for s in ("_index", "_low"))
    with stage(nc, name, "made") as (block, s):
        @block.gpsimd
        def _(pool):
            nc.gpsimd.iota(index[:, :, :], pattern=[[0, NT], [1, n]], base=0, channel_multiplier=0,
                           allow_small_or_imprecise_dtypes=True).then_inc(s["made"], 1)
            pool.wait_ge(s["made"], 1)
            nc.gpsimd.tensor_scalar(low[:, :, :], index[:, :, :], 16.0, None, ALU.subtract)
    return index, low


def two_of(nc, C, name, mem, scores, n, factor=None):
    def sb(s, shape):
        return mem.enter_context(nc.sbuf_tensor(name + s, shape, F32))

    index, low = make_index(nc, name + "_index", mem, n)
    one, two, rest, w = (sb(a, [P, NT, n]) for a in ("_one", "_two", "_rest", "_w"))
    t = sb("_t", [P, 6, NT])
    shape = [P, NT, n]
    with stage(nc, name, "steps exped") as (block, s):
        @block.vector
        def _(dve):
            step = Steps(dve, s["steps"])
            first_max(nc, step, scores, index[:, :, :], low[:, :, :], t[:, 0], t[:, 1], one[:, :, :], shape)
            step(nc.vector.scalar_tensor_tensor(out=rest[:, :, :], in0=one[:, :, :], scalar=NEG, in1=scores, op0=ALU.mult, op1=ALU.add))
            first_max(nc, step, rest[:, :, :], index[:, :, :], low[:, :, :], t[:, 2], t[:, 1], two[:, :, :], shape)
            step(nc.vector.tensor_tensor(t[:, 3], t[:, 2], t[:, 0], ALU.subtract))
            dve.wait_ge(s["exped"], 1)
            step(nc.vector.tensor_scalar(t[:, 1], t[:, 4], 1.0, None, ALU.add))
            step(nc.vector.reciprocal(t[:, 0], t[:, 1]))
            step(nc.vector.tensor_tensor(t[:, 2], t[:, 4], t[:, 0], ALU.mult))
            step(nc.vector.tensor_tensor(one[:, :, :], one[:, :, :], bcast(t[:, 0].unsqueeze(2), shape), ALU.mult))
            step(nc.vector.tensor_tensor(two[:, :, :], two[:, :, :], bcast(t[:, 2].unsqueeze(2), shape), ALU.mult))
            step(nc.vector.tensor_tensor(w[:, :, :], one[:, :, :], two[:, :, :], ALU.add))

        @block.scalar
        def _(act):
            act.wait_ge(s["steps"], 12)
            nc.scalar.activation(t[:, 4], t[:, 3], ACT.Exp).then_inc(s["exped"], 1)
    return w


def logits(nc, C, name, xnT, w, bias, out, n):
    jobs = [([(xnT[:, k, t * P:(t + 1) * P], w[:, k]) for k in range(KD)], slice(0, P), slice(0, n),
             lambda ps, steps, t=t: nc.vector.tensor_tensor(out[:, t], ps, bias, ALU.add)) for t in range(NT)]
    products(nc, C, name, jobs)


def moe_top2(nc, C, D, x, xnT):
    NE, F = D["moe_w_gate"].shape[1], D["moe_w_gate"].shape[3]
    with ExitStack() as mem:
        def sb(name, shape):
            return mem.enter_context(nc.sbuf_tensor("moe_" + name, shape, F32))

        gx, wr, br, score = sb("gx", [P, KD]), sb("wr", [P, KD, NE]), sb("br", [P, NE]), sb("score", [P, NT, NE])
        with stage(nc, "moe_load", "loaded") as (block, s):
            @block.sync
            def _(sp):
                sp.dma_start(gx[:, :], D["od_ffn_norm"][0].rearrange("(p k) -> p k", k=KD)).then_inc(s["loaded"], 16)
                sp.dma_start(wr[:, :, :], D["moe_w_router"][0].rearrange("(p k) n -> p k n", k=KD)).then_inc(s["loaded"], 16)
                sp.dma_start(br[:, :], D["moe_b_router"].partition_broadcast(P).rearrange("p a n -> p (a n)")).then_inc(s["loaded"], 16)
                sp.wait_ge(s["loaded"], 48)
        xs = sb("xs", [P, NT, DM])
        norm_transpose(nc, C, x, gx, xnT, xs, "moe_norm")
        logits(nc, C, "moe_logits", xnT, wr, br[:, :], score, NE)
        w = two_of(nc, C, "moe_route", mem, score[:, :, :], NE)
        gv, uv = (D[n][0].rearrange("e (p k) f -> e p k f", k=KD) for n in ("moe_w_gate", "moe_w_up"))
        dv = D["moe_w_down"][0].rearrange("e (c p) d -> e p c d", p=P)
        mask = sb("mask", [P, NT, NE])
        with stage(nc, "moe_mask", "x") as (block, s):
            @block.vector
            def _(dve):
                nc.vector.tensor_scalar(mask[:, :, :], w[:, :, :], 0.0, None, ALU.is_gt)
        plan = plan_passes(nc, C, "moe_plan", mem, mask, NE)
        cut = lambda v: lambda e, c: v[e][:, :, c * 512:min((c + 1) * 512, F)]
        routed_passes(nc, C, "moe_pass", x, xs, xnT, gx, plan, NE, F, cut(gv), cut(uv), lambda e: dv[e],
                      lambda t, e: w[:, t, bass.ds(e, 1)], 1)


def ffn(nc, C, D, x, xnT):
    with ExitStack() as mem:
        gx = mem.enter_context(nc.sbuf_tensor("ffn_gx", [P, KD], F32))
        with stage(nc, "ffn_load", "loaded") as (block, s):
            @block.sync
            def _(sp):
                sp.dma_start(gx[:, :], D["ev_ffn_norm"][0].rearrange("(p k) -> p k", k=KD)).then_inc(s["loaded"], 16)
                sp.wait_ge(s["loaded"], 16)
        with ExitStack() as m2:
            xs = m2.enter_context(nc.sbuf_tensor("ffn_xs", [P, NT, DM], F32))
            norm_transpose(nc, C, x, gx, xnT, xs, "ffn_norm")
        parts = 2
        F = D["ffn_w_gate"].shape[2] // parts
        gv, uv = (D[n][0].rearrange("(p k) (e f) -> e p k f", k=KD, f=F) for n in ("ffn_w_gate", "ffn_w_up"))
        dv = D["ffn_w_down"][0].rearrange("(e c p) d -> e p c d", e=parts, p=P)
        gated_parts(nc, C, "ffn", xnT, x, parts, F, lambda e: gv[e], lambda e: uv[e], lambda e: dv[e])


def moe_groups(nc, C, D, x, xnT):
    NE, F = D["exp_w_gate_2"].shape[1], D["exp_w_gate_2"].shape[3]
    NG = D["router_gw_2"].shape[2]
    PG = NE // NG
    with ExitStack() as mem:
        def sb(name, shape):
            return mem.enter_context(nc.sbuf_tensor("hm_" + name, shape, F32))

        gx, wr, br, score = sb("gx", [P, KD]), sb("wr", [P, KD, NG + NE]), sb("br", [P, NG + NE]), sb("score", [P, NT, NG + NE])
        with stage(nc, "hm_load", "loaded") as (block, s):
            @block.sync
            def _(sp):
                sp.dma_start(gx[:, :], D["norm2_g_2"][0].rearrange("(p k) -> p k", k=KD)).then_inc(s["loaded"], 16)
                for w, b, a, n in (("router_gw_2", "router_gb_2", 0, NG), ("router_ew_2", "router_eb_2", NG, NE)):
                    sp.dma_start(wr[:, :, a:a + n], D[w][0].rearrange("(p k) n -> p k n", k=KD)).then_inc(s["loaded"], 16)
                    sp.dma_start(br[:, a:a + n], D[b].partition_broadcast(P).rearrange("p a n -> p (a n)")).then_inc(s["loaded"], 16)
                sp.wait_ge(s["loaded"], 80)
        xs = sb("xs", [P, NT, DM])
        norm_transpose(nc, C, x, gx, xnT, xs, "hm_norm")
        logits(nc, C, "hm_logits", xnT, wr, br[:, :], score, NG + NE)
        index, low = make_index(nc, "hm_index", mem, NG)
        group, ex, sel, t = sb("group", [P, NT, NG]), sb("ex", [P, NT, NG]), sb("sel", [P, NT, PG]), sb("t", [P, 4, NT])
        chosen = sb("chosen", [P, NT, NG, PG])
        shape = [P, NT, NG]
        with stage(nc, "hm_group", "steps exped") as (block, s):
            @block.vector
            def _(dve):
                step = Steps(dve, s["steps"])
                first_max(nc, step, score[:, :, 0:NG], index[:, :, :], low[:, :, :], t[:, 0], t[:, 1], group[:, :, :], shape)
                step(nc.vector.tensor_tensor(ex[:, :, :], score[:, :, 0:NG], bcast(t[:, 0].unsqueeze(2), shape), ALU.subtract))
                el = score[:, :, NG:NG + NE].rearrange("p t (g e) -> p t g e", g=NG)
                for i in range(NT):
                    nc.vector.tensor_tensor(chosen[:, i], el[:, i], bcast(group[:, i].unsqueeze(2), [P, NG, PG]), ALU.mult)
                step(nc.vector.tensor_copy(t[:, 1], t[:, 0]))
                step(nc.vector.tensor_reduce(sel[:, :, :], chosen[:, :, :, :].rearrange("p t g e -> p t e g"), AX.X, ALU.add))
                dve.wait_ge(s["exped"], 1)
                step(nc.vector.tensor_reduce(t[:, 2], ex[:, :, :], AX.X, ALU.add))
                step(nc.vector.reciprocal(t[:, 3], t[:, 2]))

            @block.scalar
            def _(act):
                act.wait_ge(s["steps"], 6)
                nc.scalar.activation(ex[:, :, :], ex[:, :, :], ACT.Exp).then_inc(s["exped"], 1)
        w = two_of(nc, C, "hm_route", mem, sel[:, :, :], PG)
        with stage(nc, "hm_weights", "steps") as (block, s):
            @block.vector
            def _(dve):
                step = Steps(dve, s["steps"])
                step(nc.vector.tensor_tensor(w[:, :, :], w[:, :, :], bcast(t[:, 3].unsqueeze(2), [P, NT, PG]), ALU.mult))
        plan = plan_passes(nc, C, "hm_plan", mem, group, NG)
        gv, uv = (D[n][0].rearrange("(g h e) (p k) f -> g h p k e f", g=NG, h=2, k=KD) for n in ("exp_w_gate_2", "exp_w_up_2"))
        dv = D["exp_w_down_2"][0].rearrange("(g e) (c p) d -> g p (e c) d", g=NG, p=P)
        routed_passes(nc, C, "hm_pass", x, xs, xnT, gx, plan, NG, PG * F, lambda e, c: gv[e, c], lambda e, c: uv[e, c], lambda e: dv[e],
                      lambda t, e: w[:, t], PG, CUT=2)


LW, FW, RW = 256, 512, 256
XA0, GA0, FQ0, FK0, FV0, FL0, PC0, IN_W = 0, 256, 512, 1024, 1536, 2048, 2056, 2952
CHUNK = 64
SUB = 16


def wkv_masks():
    r, c = np.arange(P)[:, None], np.arange(P)[None, :]
    same = lambda n: (r // n) == (c // n)
    return np.stack([same(SUB) & (r > c), same(SUB) & (r < c), same(2 * SUB) & ~same(SUB) & (r > c),
                     same(CHUNK) & ~same(2 * SUB) & (r > c), same(CHUNK) & (r < c), same(CHUNK) & (r <= c)]).astype(np.float32)


def chunk_restart():
    return np.broadcast_to((np.arange(SEQ) % CHUNK != 0).astype(np.float32), (P, SEQ)).copy()


def mixer_second(nc, C, D, x, xnT):
    with ExitStack() as mem:
        def sb(name, shape, m=mem):
            return m.enter_context(nc.sbuf_tensor("s_" + name, shape, F32))

        yT = sb("yT", [P, 8, SEQ])
        yL = low_alias(nc, "s_yT_low", [P, 8, SEQ])
        pm = sb("pm", [P, 7, SEQ + 1])
        cols = {}
        for n, w in (("gx", KD), ("lng", 2), ("cb", 2), ("ba", 2), ("bx", 2), ("lam", 2), ("fqg", 1), ("fkg", 1), ("fng", 4),
                     ("mu", 7), ("w0", 2), ("a0", 2), ("kk", 2), ("ka", 2), ("rk", 2), ("rlg", 2), ("rlb", 2), ("fb", 1)):
            cols[n] = sb(n, [P, w])
        taps = sb("taps", [P, 4, 2])
        wa, wx = sb("wa", [P, 2, P]), sb("wx", [P, 2, P])
        low = sb("low", [P, 3, RW])
        loaded = {n: nc.alloc_semaphore("s_loaded_" + n) for n in "gx small w0 w1 w2 w3 w4 w5 wkv".split()}
        pieces = [(XA0, FQ0), (FQ0, FK0), (FK0, FV0), (FV0, FL0), (FL0, PC0 + 448), (PC0 + 448, IN_W)]
        memF = ExitStack()
        xa, ga = sb("xa", [P, 2, SEQ + 3], memF), sb("ga", [P, 2, SEQ], memF)
        fq, fk, fv, fl = sb("fq", [P, 4, SEQ], memF), sb("fk", [P, 4, SEQ], memF), sb("fv", [P, NT, SEQ], memF), sb("fl", [8, SEQ], memF)
        small = 0
        with ExitStack() as memW:
            W = sb("W", [P, KD, IN_W], memW)
            WL = low_alias(nc, "s_W_low", [P, KD, IN_W])
            win = D["w_in_2"][0].rearrange("(p k) n -> p k n", k=KD)
            def load_pieces(sp, which):
                for i in which:
                    a, b = pieces[i]
                    sp.dma_start(W[:, :, a:b], win[:, :, a:b]).then_inc(loaded[f"w{i}"], 16)

            def load_rest(sp):
                nonlocal small
                load_pieces(sp, (1, 2, 5))
                tiles = lambda n: D[n][0].rearrange("(i p) -> p i", p=P)
                smalls = [(cols[c][:, :], tiles(n)) for c, n in (
                    ("lng", "lru_norm_g_2"), ("cb", "conv_b_2"), ("ba", "lru_ba_2"), ("bx", "lru_bx_2"), ("lam", "lru_lambda_2"),
                    ("fng", "fox_norm_g_2"), ("mu", "rwkv_mu_2"), ("w0", "rwkv_w0_2"), ("a0", "rwkv_a0_2"), ("kk", "rwkv_kk_2"),
                    ("ka", "rwkv_ka_2"), ("rlg", "rwkv_ln_g_2"), ("rlb", "rwkv_ln_b_2"))]
                smalls += [(cols["rk"][:, :], D["rwkv_rk_2"][0].rearrange("(i a) d -> (a d) i", a=2)),
                           (cols["fb"][0:8, :], column(D["fox_fb_2"][0]))]
                for a in (0, HD):
                    smalls += [(cols["fqg"][a:a + HD, :], column(D["fox_qnorm_g_2"][0])),
                               (cols["fkg"][a:a + HD, :], column(D["fox_knorm_g_2"][0]))]
                    for i in range(2):
                        smalls += [(wa[a:a + HD, i, a:a + HD], D["lru_wa_2"][0, 2 * i + a // HD]),
                                   (wx[a:a + HD, i, a:a + HD], D["lru_wx_2"][0, 2 * i + a // HD])]
                smalls += [(taps[:, i], D["conv_w_2"][0, i].rearrange("(j p) -> p j", p=P)) for i in range(4)]
                smalls += [(low[0:32, 0], D["rwkv_w2_2"][0]), (low[32:64, 1], D["rwkv_a2_2"][0]), (low[64:128, 2], D["rwkv_g2_2"][0])]
                for dst, src in smalls:
                    sp.dma_start(dst, src, allow_slow_non_contiguous=True).then_inc(loaded["small"], 16)
                small = 16 * len(smalls)

            with stage(nc, "s_load", "x") as (block, s):
                @block.sync
                def _(sp):
                    sp.dma_start(cols["gx"][:, :], D["norm1_g_2"][0].rearrange("(p k) -> p k", k=KD)).then_inc(loaded["gx"], 16)

                @block.vector
                def _(dve):
                    nc.vector.memset(wa[:, :, :], 0.0)
                    nc.vector.memset(wx[:, :, :], 0.0)
                    nc.vector.memset(xa[:, :, 0:3], 0.0)
                    nc.vector.memset(pm[:, :, 0:1], 0.0)

            norm_transpose(nc, C, x, cols["gx"], xnT, yT[:, :, :].rearrange("p (t a) b -> p t (a b)", a=2), "s_norm",
                           lambda sp: load_pieces(sp, (3, 4, 0)), (loaded["gx"], 16))

            plain, jobs = [], []

            def features(a, dst, pieces):
                jobs.append((W[:, :, a:a + P], WL[:, :, a:a + P], copy_to(nc, dst), [(loaded[f"w{i}"], 16) for i in pieces]))

            for t in range(NT):
                plain.append(([(xnT[:, k, t * P:(t + 1) * P], W[:, k, FV0:FV0 + FW]) for k in range(KD)], slice(0, P), slice(0, FW),
                              copy_to(nc, fv[:, t]), [(loaded["w3"], 16)]))
            plain.append(([(W[:, k, FL0:FL0 + 8], xnT[:, k]) for k in range(KD)], slice(0, 8), slice(0, SEQ),
                          copy_to(nc, fl[:, :]), [(loaded["w4"], 16)]))
            for i in range(2):
                features(XA0 + i * P, xa[:, i, 3:], [0])
                features(GA0 + i * P, ga[:, i], [0])
            for i in range(4):
                features(FQ0 + i * P, fq[:, i], [1])
            for i in range(4):
                features(FK0 + i * P, fk[:, i], [2])
            for i in range(7):
                features(PC0 + i * P, pm[:, i, 1:], [4, 5])
            split_features(nc, C, "s_in", xnT, C.xL, yL, jobs, plain, loads=load_rest)

        with ExitStack() as m:
            xc, r, i_, la, h = (sb(n, [P, 2, SEQ], m) for n in ("xc", "r", "i", "la", "h"))
            lc = sb("lc", [P, 6, 2], m)
            both = [P, 2 * SEQ]
            flat = lambda ap: ap.rearrange("p a b -> p (a b)")
            with stage(nc, "s_conv", "steps") as (block, s):
                @block.vector
                def _(dve):
                    step = Steps(dve, s["steps"])
                    dve.wait_ge(loaded["small"], small)
                    nc.vector.tensor_scalar(cols["fqg"][:, :], cols["fqg"][:, :], float(HD) ** -0.5, None, ALU.mult)
                    for i in range(2):
                        step(nc.vector.tensor_scalar(xc[:, i], xa[:, i, 0:SEQ], taps[:, 0, i:i + 1], cols["cb"][:, i:i + 1], ALU.mult, ALU.add))
                        for j in range(1, 4):
                            step(nc.vector.scalar_tensor_tensor(out=xc[:, i], in0=xa[:, i, j:j + SEQ], scalar=taps[:, j, i:i + 1],
                                                                in1=xc[:, i], op0=ALU.mult, op1=ALU.add))
            products(nc, C, "s_lru_gates", [([(w[:, i], xc[:, i])], slice(0, P), slice(0, SEQ), copy_to(nc, dst[:, i]))
                                            for w, dst in ((wa, r), (wx, i_)) for i in range(2)])
            with stage(nc, "s_lru", "steps act") as (block, s):
                @block.scalar
                def _(act):
                    step = Steps(act, s["act"])
                    for i in range(2):
                        nc.scalar.activation(r[:, i], r[:, i], ACT.Sigmoid, bias=cols["ba"][:, i:i + 1])
                        nc.scalar.activation(i_[:, i], i_[:, i], ACT.Sigmoid, bias=cols["bx"][:, i:i + 1])
                    act.wait_ge(s["steps"], 2)
                    step(nc.scalar.activation(lc[:, 2], lc[:, 1], ACT.Exp))
                    step(nc.scalar.activation(lc[:, 3], lc[:, 2], ACT.Ln, bias=C.one[:, 0:1]))
                    act.wait_ge(s["steps"], 6)
                    step(nc.scalar.activation(flat(h[:, :, :]), flat(la[:, :, :]), ACT.Tanh))
                    step(nc.scalar.activation(flat(la[:, :, :]), flat(la[:, :, :]), ACT.Exp))
                    act.wait_ge(s["steps"], 10)
                    step(nc.scalar.activation(flat(h[:, :, :]), flat(h[:, :, :]), ACT.Sqrt))
                    step(nc.scalar.activation(flat(ga[:, :, :]), flat(ga[:, :, :]), ACT.Gelu_apprx_tanh))

                @block.vector
                def _(dve):
                    step = Steps(dve, s["steps"])
                    lam = cols["lam"][:, :]
                    step(nc.vector.tensor_scalar(lc[:, 0], lam, -1.0, 0.0, ALU.mult, ALU.max))
                    step(nc.vector.scalar_tensor_tensor(out=lc[:, 1], in0=lc[:, 0], scalar=-2.0, in1=lam, op0=ALU.mult, op1=ALU.subtract))
                    dve.wait_ge(s["act"], 2)
                    step(nc.vector.tensor_tensor(lc[:, 4], lc[:, 0], lc[:, 3], ALU.add))
                    step(nc.vector.tensor_scalar(lc[:, 5], lc[:, 4], -8.0, None, ALU.mult))
                    for i in range(2):
                        step(nc.vector.tensor_scalar(la[:, i], r[:, i], lc[:, 5, i:i + 1], None, ALU.mult))
                    dve.wait_ge(s["act"], 4)
                    step(nc.vector.tensor_tensor(flat(r[:, :, :]), flat(la[:, :, :]), flat(la[:, :, :]), ALU.mult))
                    step(nc.vector.tensor_scalar(flat(r[:, :, :]), flat(r[:, :, :]), -1.0, -1.0, ALU.mult, ALU.add))
                    step(nc.vector.tensor_tensor(flat(h[:, :, :]), flat(h[:, :, :]), flat(r[:, :, :]), ALU.mult))
                    step(nc.vector.tensor_tensor(flat(i_[:, :, :]), flat(i_[:, :, :]), flat(xc[:, :, :]), ALU.mult))
                    dve.wait_ge(s["act"], 5)
                    step(nc.vector.tensor_tensor(flat(i_[:, :, :]), flat(i_[:, :, :]), flat(h[:, :, :]), ALU.mult))
                    for i in range(2):
                        step(nc.vector.tensor_tensor_scan(xc[:, i], la[:, i], i_[:, i], 0.0, ALU.mult, ALU.add))
                    dve.wait_ge(s["act"], 6)
                    for i in range(2):
                        step(nc.vector.tensor_tensor(yT[:, i], xc[:, i], ga[:, i], ALU.mult))
            norm_features(nc, C, "s_lru_norm", [dict(src=[yT[:, i] for i in range(2)], gain=[cols["lng"][:, i:i + 1] for i in range(2)],
                                                     dst=[yT[:, i] for i in range(2)], ones=C.ones[:, :], n=LW)])

        with ExitStack() as m:
            decay, lf, pick = sb("decay", [P, SEQ], m), sb("lf", [8, 4, SEQ], m), sb("pick", [P, 8, P], m)
            with stage(nc, "s_decay", "steps act") as (block, s):
                @block.vector
                def _(dve):
                    step = Steps(dve, s["steps"])
                    step(nc.vector.memset(decay[:, :], 0.0))
                    step(nc.vector.memset(lf[:, 3], 1.0))
                    step(nc.vector.tensor_scalar(fl[:, :], fl[:, :], cols["fb"][0:8, 0:1], None, ALU.add))
                    step(nc.vector.tensor_scalar(lf[:, 0], fl[:, :], -1.0, 0.0, ALU.mult, ALU.max))
                    step(nc.vector.scalar_tensor_tensor(out=lf[:, 1], in0=lf[:, 0], scalar=-2.0, in1=fl[:, :], op0=ALU.mult, op1=ALU.subtract))
                    nc.vector.tensor_copy(pick[:, :, :], bcast(C.ident[:, 0:8].unsqueeze(2), [P, 8, P]))
                    dve.wait_ge(s["act"], 2)
                    step(nc.vector.tensor_tensor(lf[:, 0], lf[:, 0], lf[:, 2], ALU.add))
                    step(nc.vector.tensor_tensor_scan(decay[0:8, :], lf[:, 3], lf[:, 0], 0.0, ALU.mult, ALU.add))

                @block.scalar
                def _(act):
                    act.wait_ge(s["steps"], 5)
                    nc.scalar.activation(lf[:, 1], lf[:, 1], ACT.Exp).then_inc(s["act"], 1)
                    act.wait_ge(s["act"], 1)
                    nc.scalar.activation(lf[:, 2], lf[:, 1], ACT.Ln, bias=C.one[0:8, 0:1]).then_inc(s["act"], 1)
            norm_features(nc, C, "s_fox_qk", [dict(src=[t[:, i]], gain=[cols[g][:, 0:1]], dst=[t[:, i]], ones=C.ones64[:, :], n=HD)
                                              for i in range(4) for t, g in ((fq, "fqg"), (fk, "fkg"))])
            qz = xnT
            with stage(nc, "s_fox_qz", "x") as (block, s):
                pairs = qz[:, :, :].rearrange("p (m a) t -> p m a t", a=2)

                @block.gpsimd
                def _(pool):
                    nc.gpsimd.memset(pairs[HD:P, :, 0], 0.0)

                @block.scalar
                def _(act):
                    nc.scalar.activation(pairs[0:HD, :, 0], fq[0:HD], ACT.Copy)

                @block.vector
                def _(dve):
                    nc.vector.memset(pairs[0:HD, :, 1], 0.0)
                    nc.vector.tensor_copy(pairs[HD:P, :, 1], fq[HD:P])
            jobs = []
            for h in range(8):
                half = slice(h % 2 * HD, h % 2 * HD + HD)
                jobs.append(dict(q=qz[:, h], k=fk[:, h // 2], v=lambda kb, h=h: fv[:, kb, h * HD:(h + 1) * HD],
                                 bias=C.causal[:, :], extra=(pick[:, h], decay[:, :]), gate=None, first=None, start=True, stop=True,
                                 rows=half, bank=h // 2 % 2, out=yT[:, 2 + h // 2]))
            attention(nc, C, "s_fox", jobs)
            norm_features(nc, C, "s_fox_norm", [dict(src=[yT[:, 2 + i] for i in range(4)], gain=[cols["fng"][:, i:i + 1] for i in range(4)],
                                                     dst=[yT[:, 2 + i] for i in range(4)], ones=C.ones[:, :], n=FW)])
        memF.close()
        rwkv(nc, C, D, yT, xnT, pm, cols, low, loaded["wkv"])

        wout = sb("wout", [P, 8, DM])
        woutL = low_alias(nc, "s_wout_low", [P, 8, DM])
        add_projection(nc, C, "s_out", yT, yL, wout, woutL, x, D["w_out_2"][0].rearrange("(k p) n -> p k n", p=P))
        nc.clear_and_free_semaphores(list(loaded.values()))
        nc.all_engine_barrier(sem_only=True)


def paired(nc, C, name, jobs):
    with stage(nc, name, "made taken steps") as (block, s):
        PS = C.PS

        @block.tensor
        def _(pe):
            for n, (after, items, take) in enumerate(jobs):
                need = max(after, n - 3)
                if need > 0:
                    pe.wait_ge(s["taken"], need)
                for bank, cols, rows, lhsT, rhs, start, stop in items:
                    out = PS[rows, 2 * (n % 4) + bank, cols]
                    if start == "turn":
                        ins = nc.tensor.transpose(out, lhsT, rhs)
                    else:
                        ins = nc.tensor.matmul(out, lhsT, rhs, start=start, stop=stop)
                ins.then_inc(s["made"], 1)

        @block.vector
        def _(dve):
            steps = Steps(dve, s["steps"])
            for n, (after, items, take) in enumerate(jobs):
                dve.wait_ge(s["made"], n + 1)
                take(PS[:, 2 * (n % 4):2 * (n % 4) + 2, :], steps).then_inc(s["taken"], 1)
                dve.wait_ge(s["taken"], n + 1)


def rwkv(nc, C, D, yT, xnT, pm, cols, low, loaded):
    PR, HH = 2, 4
    with ExitStack() as mem:
        def sb(name, shape, m=mem):
            return m.enter_context(nc.sbuf_tensor("rw_" + name, shape, F32))

        At, Bt, Kt, Rt, al, gl, bonus, rs, eLx, enL = (sb(n, [P, 2, SEQ]) for n in (
            "At", "Bt", "Kt", "Rt", "al", "gl", "bonus", "rs", "eLx", "enL"))
        eL = sb("eL", [P, 2, SEQ])
        masks, restart = sb("masks", [P, 6, P]), sb("restart", [P, SEQ])
        ocol = sb("ocol", [P, 2])
        flat = lambda ap: ap.rearrange("p a b -> p (a b)")
        p = pm[:, :, 1:]
        with stage(nc, "rw_mix", "steps act diff") as (block, s):
            @block.sync
            def _(sp):
                sp.dma_start(masks[:, :, :], D["wkv_masks"].rearrange("m p c -> p m c")).then_inc(loaded, 16)
                sp.dma_start(restart[:, :], D["chunk_restart"]).then_inc(loaded, 16)

            @block.vector
            def _(dve):
                step = Steps(dve, s["steps"])
                for i in (6, 0, 1, 2, 3, 4, 5):
                    step(nc.vector.tensor_tensor(rs[:, 0], pm[:, i, 0:SEQ], pm[:, i, 1:], ALU.subtract))
                    step(nc.vector.scalar_tensor_tensor(out=pm[:, i, 1:], in0=rs[:, 0], scalar=cols["mu"][:, i:i + 1], in1=pm[:, i, 1:],
                                                        op0=ALU.mult, op1=ALU.add))
                nc.vector.tensor_scalar(ocol[:, :], cols["ka"][:, :], -1.0, 1.0, ALU.mult, ALU.add)
                for i in range(2):
                    step(nc.vector.tensor_scalar(At[:, i], p[:, 2 + i], cols["kk"][:, i:i + 1], None, ALU.mult))
                step(nc.vector.tensor_tensor(flat(bonus[:, :, :]), flat(At[:, :, :]), flat(At[:, :, :]), ALU.mult))

            @block.scalar
            def _(act):
                act.wait_ge(s["steps"], 2)
                nc.scalar.activation(p[0:32, 6], p[0:32, 6], ACT.Tanh)
                nc.scalar.activation(p[64:P, 6], p[64:P, 6], ACT.Sigmoid)
        jobs = []
        for i in range(2):
            c = slice(i * P, (i + 1) * P)
            jobs += [([(low[0:32, 0, c], p[0:32, 6])], slice(0, P), slice(0, SEQ), copy_to(nc, enL[:, i])),
                     ([(low[32:64, 1, c], p[32:64, 6])], slice(0, P), slice(0, SEQ), copy_to(nc, al[:, i])),
                     ([(low[64:P, 2, c], p[64:P, 6])], slice(0, P), slice(0, SEQ), copy_to(nc, gl[:, i])),
                     ([(C.ones64[:, :], bonus[:, i])], slice(0, P), slice(0, SEQ), copy_to(nc, rs[:, i]))]
        products(nc, C, "rw_low", jobs)
        with stage(nc, "rw_decay", "steps act") as (block, s):
            @block.scalar
            def _(act):
                step = Steps(act, s["act"])
                for i in range(2):
                    step(nc.scalar.activation(enL[:, i], enL[:, i], ACT.Sigmoid, bias=cols["w0"][:, i:i + 1]))
                for i in range(2):
                    step(nc.scalar.activation(al[:, i], al[:, i], ACT.Sigmoid, bias=cols["a0"][:, i:i + 1]))
                step(nc.scalar.activation(flat(rs[:, :, :]), flat(rs[:, :, :]), ACT.Sqrt))
                act.wait_ge(s["steps"], 4)
                step(nc.scalar.activation(flat(eLx[:, :, :]), flat(eLx[:, :, :]), ACT.Exp))
                step(nc.scalar.activation(flat(enL[:, :, :]), flat(eL[:, :, :]), ACT.Exp, scale=-1.0))
                step(nc.scalar.activation(flat(eL[:, :, :]), flat(eL[:, :, :]), ACT.Exp))

            @block.vector
            def _(dve):
                step = Steps(dve, s["steps"])
                dve.wait_ge(loaded, 32)
                dve.wait_ge(s["act"], 2)
                step(nc.vector.tensor_scalar(flat(enL[:, :, :]), flat(enL[:, :, :]), -math.exp(-0.5), None, ALU.mult))
                for i in range(2):
                    step(nc.vector.tensor_tensor_scan(eL[:, i], restart[:, :], enL[:, i], 0.0, ALU.mult, ALU.add))
                step(nc.vector.tensor_tensor(flat(eLx[:, :, :]), flat(eL[:, :, :]), flat(enL[:, :, :]), ALU.subtract))
                dve.wait_ge(s["act"], 5)
                step(nc.vector.tensor_scalar(flat(rs[:, :, :]), flat(rs[:, :, :]), 1e-12, None, ALU.max))
                step(nc.vector.reciprocal(flat(rs[:, :, :]), flat(rs[:, :, :])))
                step(nc.vector.tensor_tensor(flat(At[:, :, :]), flat(At[:, :, :]), flat(rs[:, :, :]), ALU.mult))
                step(nc.vector.tensor_tensor(flat(Bt[:, :, :]), flat(At[:, :, :]), flat(al[:, :, :]), ALU.mult))
                for i in range(2):
                    step(nc.vector.tensor_scalar(al[:, i], al[:, i], cols["ka"][:, i:i + 1], ocol[:, i:i + 1], ALU.mult, ALU.add))
                    step(nc.vector.tensor_tensor(al[:, i], al[:, i], p[:, 2 + i], ALU.mult))
                    step(nc.vector.scalar_tensor_tensor(out=bonus[:, i], in0=al[:, i], scalar=cols["rk"][:, i:i + 1], in1=p[:, i],
                                                        op0=ALU.mult, op1=ALU.mult))
                dve.wait_ge(s["act"], 8)
                step(nc.vector.scalar_tensor_tensor(out=flat(At[:, :, :]), in0=flat(At[:, :, :]), scalar=-1.0, in1=flat(eLx[:, :, :]),
                                                    op0=ALU.mult, op1=ALU.mult))
                step(nc.vector.tensor_tensor(flat(Bt[:, :, :]), flat(Bt[:, :, :]), flat(enL[:, :, :]), ALU.mult))
                step(nc.vector.tensor_tensor(flat(Kt[:, :, :]), flat(al[:, :, :]), flat(enL[:, :, :]), ALU.mult))
                for i in range(2):
                    step(nc.vector.tensor_tensor(Rt[:, i], p[:, i], eL[:, i], ALU.mult))
        products(nc, C, "rw_bonus", [([(C.ones64[:, :], bonus[:, i])], slice(0, P), slice(0, SEQ),
                                      lambda ps, steps, i=i: nc.vector.tensor_tensor(bonus[:, i], ps, p[:, 4 + i], ALU.mult)) for i in range(2)])

        with ExitStack() as m:
            MA, UA, MB, UB, Y, M1, M2, NTr = (sb(n, [P, NT, HH, P], m) for n in (
                "MA", "UA", "MB", "UB", "Y", "M1", "M2", "NT"))
            QB, QK = MB, UB
            tok = sb("tok", [P, NT, 3, HH, HD], m)
            free = xnT[:, :, :].rearrange("p a b -> p (a b)")
            AN = free[:, 0:2048].rearrange("p (t h c) -> p t h c", t=NT, h=HH)
            AZ = AN
            GF = free[:, 2048:4096].rearrange("p (c a b d) -> p c a b d", c=8, a=2, b=PR)
            ApT = al
            SA = eLx[:, :, :].rearrange("p a (b h d) -> p (a b) h d", h=HH, d=HD)
            AT = enL[:, :, :].rearrange("p a (b h d) -> p (a b) h d", h=HH, d=HD)
            S = sb("S", [P, 9, PR, HD], m)
            SF = sb("SF", [P, PR, HD], m)
            full = slice(0, P)

            def half(hp):
                return slice(hp * HD, (hp + 1) * HD)

            def bank_view(ps, w):
                return ps[:, :, 0:2 * w].rearrange("p a (b c) -> p a b c", b=2)

            def rows4(T, t):
                return T[:, t].rearrange("p (a b) c -> p a b c", a=2)

            def masked(ps, steps, t, *outs):
                for T, mk in outs:
                    for hp in range(2):
                        ins = nc.vector.tensor_tensor(T[:, t, 2 * hp:2 * hp + 2], ps[:, hp, 0:256].rearrange("p (b c) -> p b c", b=2),
                                                      bcast(masks[:, mk].unsqueeze(1), [P, 2, P]), ALU.mult)
                return ins

            def put(T, t):
                return lambda ps, steps: nc.vector.tensor_copy(rows4(T, t), bank_view(ps, P))

            jobs = []

            def gram(t, left, right, take, after=0):
                c = slice(t * P, (t + 1) * P)
                items = [(hp, slice(pr * P, (pr + 1) * P), full, left[half(hp), pr, c], right[half(hp), pr, c], True, True)
                         for hp in range(2) for pr in range(PR)]
                jobs.append((after, items, take))

            def mul(after, t, left, right, take, w=P):
                items = [(hp, slice(pr * w, (pr + 1) * w), full, left(2 * hp + pr), right(2 * hp + pr), True, True)
                         for hp in range(2) for pr in range(PR)]
                jobs.append((after, items, take))

            for t in range(NT):
                gram(t, At, Bt, lambda ps, st, t=t: masked(ps, st, t, (MA, 0), (M1, 2), (M2, 3)))
            for t in range(NT):
                def take_u(ps, st, t=t):
                    st(masked(ps, st, t, (UA, 1)))
                    return nc.vector.tensor_tensor(Y[:, t], UA[:, t], bcast(C.ident[:, :].unsqueeze(1), [P, HH, P]), ALU.add)
                gram(t, Bt, At, take_u)
            for t in range(NT):
                gram(t, Kt, At, lambda ps, st, t=t: masked(ps, st, t, (NTr, 4)))
            for t in range(NT):
                c = slice(t * P, (t + 1) * P)
                for qi, T in enumerate((At, Bt, Kt, None)):
                    src = lambda pr: (T[:, pr, c] if T is not None else p[:, 4 + pr, c])
                    items = [(0, slice(pr * P, (pr + 1) * P), full, src(pr), C.ident[:, :], "turn", True) for pr in range(PR)]

                    def take_tok(ps, st, t=t, qi=qi):
                        v = ps[:, 0, 0:256].rearrange("p (b a d) -> p a b d", b=2, a=2)
                        if qi == 0:
                            nc.vector.tensor_copy(rows4(AT, t), v)
                            return nc.vector.tensor_copy(rows4(AN, t)[:, :, :, 0:HD], v)
                        return nc.vector.tensor_copy(tok[:, t, qi - 1].rearrange("p (a b) d -> p a b d", a=2), v)
                    jobs.append((0, items, take_tok))

            def accumulate(t):
                return lambda ps, st: nc.vector.tensor_tensor(rows4(Y, t), rows4(Y, t), bank_view(ps, P), ALU.add)

            def level(make):
                done = len(jobs)
                for t in range(NT):
                    make(done, t)

            for (Mo, Uo), (Mn, Un), last in (((MA, UA), (MB, UB), False), ((MB, UB), (MA, UA), False), ((MA, UA), (MB, UB), True)):
                level(lambda d, t: mul(d, t, lambda h: Uo[:, t, h], lambda h: Mo[:, t, h], put(Mn, t)))
                if not last:
                    level(lambda d, t: mul(d - NT, t, lambda h: Mo[:, t, h], lambda h: Uo[:, t, h], put(Un, t)))
                level(lambda d, t: mul(d, t, lambda h: Mn[:, t, h], lambda h: Y[:, t, h], accumulate(t)))
            done = len(jobs)
            for t in range(NT):
                gram(t, Bt, Rt, lambda ps, st, t=t: masked(ps, st, t, (QB, 5)), done)
                gram(t, Kt, Rt, lambda ps, st, t=t: masked(ps, st, t, (QK, 5)), done)
            for Moff in (M1, M2):
                level(lambda d, t: jobs.append((d, [(h // 2, slice(h % 2 * P, (h % 2 + 1) * P), full, Y[:, t, h], C.ident[:, :], "turn", True)
                                                    for h in range(HH)], put(MA, t))))
                level(lambda d, t: mul(d - NT, t, lambda h: Moff[:, t, h], lambda h: Y[:, t, h], put(UA, t)))
                level(lambda d, t: mul(d, t, lambda h: MA[:, t, h], lambda h: UA[:, t, h], accumulate(t)))
            level(lambda d, t: mul(d, t, lambda h: NTr[:, t, h], lambda h: tok[:, t, 2, h],
                                   lambda ps, st: nc.vector.tensor_copy(rows4(AN, t)[:, :, :, HD:P], bank_view(ps, HD)), HD))
            level(lambda d, t: mul(d, t, lambda h: Y[:, t, h], lambda h: AN[:, t, h], put(AZ, t)))

            def apt(d, t):
                items = [(pr, slice(0, P), half(hp), AT[:, t, 2 * hp + pr], Y[:, t, 2 * hp + pr], True, True)
                         for pr in range(PR) for hp in range(2)]
                jobs.append((d - NT, items, lambda ps, st: nc.vector.tensor_copy(ApT[:, :, t * P:(t + 1) * P], ps[:, :, 0:P])))
            level(apt)
            done = len(jobs)
            for c in range(8):
                t, cr = c // 2, half(c % 2)
                items = []
                for hp in range(2):
                    for pr in range(PR):
                        h = 2 * hp + pr
                        items.append((c % 2, slice(pr * HD, (pr + 1) * HD), half(hp), AZ[cr, t, h, 0:HD], tok[cr, t, 0, h], True, True))
                        o = slice((2 + pr) * HD, (3 + pr) * HD)
                        items.append((c % 2, o, half(hp), tok[cr, t, 0, h], AZ[cr, t, h, HD:P], True, False))
                        items.append((c % 2, o, half(hp), tok[cr, t, 1, h], tok[cr, t, 2, h], False, True))
                jobs.append((done, items, lambda ps, st, c=c: nc.vector.tensor_copy(
                    GF[:, c].rearrange("p a b d -> p (a b d)"), ps[:, c % 2, 0:256])))
            paired(nc, C, "rw_chunks", jobs)

            with stage(nc, "rw_states", "made steps") as (block, s):
                PS = C.PS

                @block.tensor
                def _(pe):
                    for c in range(8):
                        pe.wait_ge(s["steps"], 1 + 3 * c)
                        for hp in range(2):
                            for pr in range(PR):
                                ins = nc.tensor.matmul(PS[half(hp), 2 * (c % 2) + hp, pr * HD:(pr + 1) * HD], GF[half(hp), c, 0, pr],
                                                       S[half(hp), c, pr], start=True, stop=True)
                        ins.then_inc(s["made"], 1)

                @block.vector
                def _(dve):
                    step = Steps(dve, s["steps"])
                    step(nc.vector.memset(S[:, 0], 0.0))
                    for c in range(8):
                        step(nc.vector.tensor_tensor(SF[:, :, :], S[:, c], GF[:, c, 1], ALU.add))
                        dve.wait_ge(s["made"], c + 1)
                        for hp in range(2):
                            ins = nc.vector.tensor_tensor(SF[half(hp)], SF[half(hp)], PS[half(hp), 2 * (c % 2) + hp, 0:P]
                                                          .rearrange("p (b d) -> p b d", b=2), ALU.add)
                        step(ins)
                        end = (c + 1) * CHUNK - 1
                        step(nc.vector.tensor_tensor(S[:, c + 1], SF[:, :, :], bcast(eL[:, :, end:end + 1], [P, PR, HD]), ALU.mult))

            jobs = []
            for t in range(NT):
                items = []
                for hp in range(2):
                    for pr in range(PR):
                        for c in (2 * t, 2 * t + 1):
                            items.append((hp, slice(pr * HD, (pr + 1) * HD), half(c % 2), ApT[half(hp), pr, c * CHUNK:(c + 1) * CHUNK],
                                          S[half(hp), c, pr], True, True))
                jobs.append((0, items, lambda ps, st, t=t: nc.vector.tensor_tensor(
                    rows4(SA, t), bank_view(ps, HD), rows4(AZ, t)[:, :, :, HD:P], ALU.add)))
            done = len(jobs)
            for t in range(NT):
                items = []
                for pr in range(PR):
                    for hp in range(2):
                        h = 2 * hp + pr
                        cs = slice(0, P)
                        items.append((pr, cs, half(hp), SA[:, t, h], QB[:, t, h], True, False))
                        items.append((pr, cs, half(hp), tok[:, t, 2, h], QK[:, t, h], False, False))
                        for c in (2 * t, 2 * t + 1):
                            items.append((pr, slice(c % 2 * CHUNK, (c % 2 + 1) * CHUNK), half(hp), S[half(hp), c, pr],
                                          Rt[half(hp), pr, c * CHUNK:(c + 1) * CHUNK], False, c % 2 == 1))
                jobs.append((done, items, lambda ps, st, t=t: nc.vector.tensor_copy(At[:, :, t * P:(t + 1) * P], ps[:, :, 0:P])))
            paired(nc, C, "rw_outputs", jobs)

        o = At
        products(nc, C, "rw_mean", [([(C.ones64[:, :], o[:, i])], slice(0, P), slice(0, SEQ), lambda ps, steps, i=i:
                                     nc.vector.scalar_tensor_tensor(out=Bt[:, i], in0=ps, scalar=-1.0 / HD, in1=o[:, i], op0=ALU.mult,
                                                                    op1=ALU.add)) for i in range(2)])
        norm_features(nc, C, "rw_gn", [dict(src=[Bt[:, i]], gain=[cols["rlg"][:, i:i + 1]], dst=[Bt[:, i]], ones=C.ones64[:, :], n=HD)
                                       for i in range(2)], eps=64e-5)
        with stage(nc, "rw_end", "steps") as (block, s):
            @block.vector
            def _(dve):
                step = Steps(dve, s["steps"])
                for i in range(2):
                    step(nc.vector.scalar_tensor_tensor(out=Bt[:, i], in0=Bt[:, i], scalar=cols["rlb"][:, i:i + 1], in1=bonus[:, i],
                                                        op0=ALU.add, op1=ALU.add))
                    step(nc.vector.tensor_tensor(yT[:, 6 + i], Bt[:, i], gl[:, i], ALU.mult))


CONSTANTS = {"bucket_table": bucket_table, "rope_table": lambda: rope_tables()[0], "rope_turn": lambda: rope_tables()[1],
             "ones_row": lambda: np.ones((1, NH), np.float32), "wkv_masks": wkv_masks, "chunk_restart": chunk_restart}


def two_blocks(nc, D, out):
    stored = nc.alloc_semaphore("out_stored")
    with ExitStack() as mem:
        x = mem.enter_context(nc.sbuf_tensor("x", [P, NT, DM], F32))
        xnT = mem.enter_context(nc.sbuf_tensor("xnT", [P, KD, SEQ], F32))
        xL = low_alias(nc, "xnT_low", [P, KD, SEQ])
        C = make_consts(nc, mem)
        C.xL = xL
        mixer_even(nc, C, D, x, xnT)
        ffn(nc, C, D, x, xnT)
        mixer_odd(nc, C, D, x, xnT)
        moe_top2(nc, C, D, x, xnT)
        mixer_second(nc, C, D, x, xnT)
        moe_groups(nc, C, D, x, xnT)
        with nc.Block(name="store", no_gpsimd_drain=True) as block:
            @block.sync
            def _(sp):
                sp.dma_start(out[0].rearrange("(t p) d -> p t d", p=P), x[:, :, :]).then_inc(stored, 16)
                sp.wait_ge(stored, 16)


def kernel(**inputs):
    import concourse.bacc as bacc
    from concourse.bass_utils import run_bass_kernel_spmd

    nc = bacc.Bacc("TRN2", target_bir_lowering=False, num_devices=1)
    arrays, D = {}, {}
    for name, a in list(inputs.items()) + [(n, f()) for n, f in CONSTANTS.items()]:
        arrays[f"in_{name}"] = np.ascontiguousarray(a)
        D[name] = nc.dram_tensor(f"in_{name}", arrays[f"in_{name}"].shape, F32, kind="ExternalInput").ap()
    out = nc.dram_tensor("out_x", (1, SEQ, DM), F32, kind="ExternalOutput").ap()
    two_blocks(nc, D, out)
    result = run_bass_kernel_spmd(nc, [arrays], core_ids=[0])
    return result.results[0]["out_x"]
```
